# Optimizing a Trainium2 kernel written in Bass

```python
import math
import jax
import jax.numpy as jnp
from jax import lax
import numpy as np

D_MODEL = 1024
BATCH = 1
SEQ = 256
DEPTH = 2
DEC_BATCH = 8
DEC_SEQ = 8
PAST_LEN = 256
PAGE_SIZE = 128

N_EVEN = (DEPTH + 1) // 2
N_ODD = DEPTH // 2

H_A = 4
DK_A = 128
DV_A = 128
CONV_A = 4
CHUNK_A = 64
QKV_A = H_A * (2 * DK_A + DV_A)
D_B = 512
CONV_B = 3
IN_EVEN = QKV_A + H_A * DV_A + 2 * H_A + 3 * D_B
CAT_EVEN = H_A * DV_A + D_B
H_C = 16
HD_C = 64
BRANCHES = ((128, 1), (512, 4), (2048, 16))
WINDOW_MAX = 2048
BAND_BLK = 128
N_GROUPS = 4
E_PER_GROUP = 8
TOP_K_IN_GROUP = 2
D_EXPERT = 256
EPS = 1e-6

kernel_name = 'hybrid_deltanet_shortconv_dilatedattn_hmoe_step'

def rms_norm(x, gain):
    xf = x.astype(jnp.float32)
    y = xf * lax.rsqrt(jnp.mean(xf * xf, axis=-1, keepdims=True) + EPS)
    return (y * gain.astype(jnp.float32)).astype(x.dtype)

def l2norm(x):
    return x * lax.rsqrt(jnp.sum(x * x, axis=-1, keepdims=True) + EPS)

def causal_dwconv(x_ext, w):
    k_w = w.shape[0]
    length = x_ext.shape[1] - k_w + 1
    return sum(x_ext[:, j:j + length] * w[j] for j in range(k_w))

def gated_delta_chunked(q, k, v, g, beta, s0):
    n, length, h, _ = q.shape
    dv = v.shape[-1]
    c = CHUNK_A
    nc = -(-length // c)
    pad = nc * c - length

    def blocks(x):
        x = jnp.pad(x, [(0, 0), (0, pad)] + [(0, 0)] * (x.ndim - 2))
        x = x.reshape((n, nc, c) + x.shape[2:])
        return jnp.moveaxis(x, 3, 1)

    qb, kb, vb, gb, bb = (blocks(t) for t in (q, k, v, g, beta))
    gcum = jnp.cumsum(gb, axis=-1)
    pos = jnp.arange(c)
    lower_incl = pos[:, None] >= pos[None, :]
    strict = pos[:, None] > pos[None, :]
    gamma = jnp.exp(jnp.where(lower_incl, gcum[..., :, None] - gcum[..., None, :], -jnp.inf))
    kk = jnp.einsum('nhcid,nhcjd->nhcij', kb, kb)
    a_mat = jnp.where(strict, bb[..., :, None] * kk * gamma, 0.0)
    t_mat = a_mat + jnp.eye(c, dtype=a_mat.dtype)
    rhs = jnp.concatenate([vb * bb[..., None], kb * (bb * jnp.exp(gcum))[..., None]], axis=-1)
    sol = lax.linalg.triangular_solve(t_mat, rhs, left_side=True, lower=True, unit_diagonal=True)
    u_base, w_mat = sol[..., :dv], sol[..., dv:]
    qk = jnp.einsum('nhcid,nhcjd->nhcij', qb, kb) * gamma
    q_dec = qb * jnp.exp(gcum)[..., None]
    k_dec = kb * jnp.exp(gcum[..., -1:] - gcum)[..., None]
    decay = jnp.exp(gcum[..., -1])

    def step(s, xs):
        u_b, w_c, qk_c, qd_c, kd_c, dec_c = xs
        u = u_b - jnp.einsum('nhck,nhkv->nhcv', w_c, s)
        o = jnp.einsum('nhck,nhkv->nhcv', qd_c, s) + jnp.einsum('nhij,nhjv->nhiv', qk_c, u)
        s = s * dec_c[..., None, None] + jnp.einsum('nhck,nhcv->nhkv', kd_c, u)
        return s, o

    xs = tuple(jnp.moveaxis(t, 2, 0) for t in (u_base, w_mat, qk, q_dec, k_dec, decay))
    s_fin, o = lax.scan(step, s0, xs)
    o = jnp.transpose(o, (1, 0, 3, 2, 4)).reshape(n, nc * c, h, dv)[:, :length]
    return o, s_fin

def even_mixer(h, a_conv_hist, b_conv_hist, s0, w_in, conv_a_w, a_log, dt_bias, o_gain, conv_b_w, w_out):
    n, length, _ = h.shape
    f32 = jnp.float32
    sizes = (QKV_A, H_A * DV_A, H_A, H_A, D_B, D_B, D_B)
    offs = np.cumsum(sizes)[:-1].tolist()
    qkv_pre, z, a, b, b_gate, c_gate, x_in = jnp.split(h @ w_in, offs, axis=-1)
    qkv_ext = jnp.concatenate([a_conv_hist.astype(h.dtype), qkv_pre], axis=1)
    qkv = jax.nn.silu(causal_dwconv(qkv_ext, conv_a_w)).astype(f32)
    q, k, v = jnp.split(qkv, [H_A * DK_A, 2 * H_A * DK_A], axis=-1)
    q = l2norm(q.reshape(n, length, H_A, DK_A)) * DK_A ** -0.5
    k = l2norm(k.reshape(n, length, H_A, DK_A))
    v = v.reshape(n, length, H_A, DV_A)
    g = -jnp.exp(a_log.astype(f32)) * jax.nn.softplus(a.astype(f32) + dt_bias.astype(f32))
    beta = jax.nn.sigmoid(b.astype(f32))
    o, s_new = gated_delta_chunked(q, k, v, g, beta, s0.astype(f32))
    o = rms_norm(o, o_gain) * jax.nn.silu(z.astype(f32).reshape(n, length, H_A, DV_A))
    out_a = o.reshape(n, length, H_A * DV_A).astype(h.dtype)
    bx = c_gate * x_in
    bx_ext = jnp.concatenate([b_conv_hist.astype(h.dtype), bx], axis=1)
    out_b = b_gate * causal_dwconv(bx_ext, conv_b_w)
    y = jnp.concatenate([out_a, out_b], axis=-1) @ w_out
    return y.astype(h.dtype), s_new, qkv_ext[:, -(CONV_A - 1):], bx_ext[:, -(CONV_B - 1):]

def band_attention(q, k, v, span):
    n, length, h, d = q.shape
    blk = BAND_BLK
    nb = -(-length // blk)
    pad = nb * blk - length
    padw = ((0, 0), (0, pad), (0, 0), (0, 0))
    qb = jnp.pad(q, padw).reshape(n, nb, blk, h, d)
    kb = jnp.pad(k, padw).reshape(n, nb, blk, h, d)
    vb = jnp.pad(v, padw).reshape(n, nb, blk, h, d)

    def with_prev(xb):
        prev = jnp.pad(xb, ((0, 0), (1, 0), (0, 0), (0, 0), (0, 0)))[:, :-1]
        return jnp.concatenate([prev, xb], axis=2)

    kc, vc = with_prev(kb), with_prev(vb)
    s = jnp.einsum('nbqhd,nbkhd->nbhqk', qb, kc, preferred_element_type=jnp.float32) * d ** -0.5
    bidx = jnp.arange(nb)[:, None, None] * blk
    qpos = bidx + jnp.arange(blk)[None, :, None]
    kpos = bidx - blk + jnp.arange(2 * blk)[None, None, :]
    dist = qpos - kpos
    mask = (dist >= 0) & (dist <= span) & (kpos >= 0)
    s = jnp.where(mask[None, :, None], s, -jnp.inf)
    m = jnp.max(s, axis=-1, keepdims=True)
    p = jnp.exp(s - m)
    den = jnp.sum(p, axis=-1)
    o = jnp.einsum('nbhqk,nbkhd->nbqhd', p, vc.astype(jnp.float32))
    o = o / jnp.swapaxes(den, -1, -2)[..., None]
    lse = jnp.swapaxes(m[..., 0] + jnp.log(den), -1, -2)
    return o.reshape(n, nb * blk, h, d)[:, :length], lse.reshape(n, nb * blk, h)[:, :length]

def merge_branches(outs, lses):
    alpha = jax.nn.softmax(jnp.stack(lses, axis=-1), axis=-1)
    return jnp.einsum('nlhgd,nlhg->nlhd', jnp.stack(outs, axis=-2), alpha)

def dilated_attention_prompt(q, k, v):
    n, s_len, h, d = q.shape
    outs, lses = [], []
    for window, dil in BRANCHES:
        sub = s_len // dil

        def to_sub(x):
            return x.reshape(n, sub, dil, h, d).transpose(0, 2, 1, 3, 4).reshape(n * dil, sub, h, d)

        o, lse = band_attention(to_sub(q), to_sub(k), to_sub(v), window // dil)
        outs.append(o.reshape(n, dil, sub, h, d).transpose(0, 2, 1, 3, 4).reshape(n, s_len, h, d))
        lses.append(lse.reshape(n, dil, sub, h).transpose(0, 2, 1, 3).reshape(n, s_len, h))
    return merge_branches(outs, lses)

def dilated_attention_sample(q, k_new, v_new, k_buf, v_buf):
    n, t_len, h, d = q.shape
    w_buf = k_buf.shape[1]
    kk = jnp.concatenate([k_buf.astype(k_new.dtype), k_new], axis=1)
    vv = jnp.concatenate([v_buf.astype(v_new.dtype), v_new], axis=1)
    outs, lses = [], []
    for window, dil in BRANCHES:
        n_keys = window // dil + 1
        idx = w_buf + jnp.arange(t_len)[:, None] - dil * jnp.arange(n_keys)[None, :]
        valid = idx >= 0
        idx = jnp.maximum(idx, 0)
        kg = kk[:, idx]
        vg = vv[:, idx]
        s = jnp.einsum('nthd,ntjhd->nthj', q, kg, preferred_element_type=jnp.float32) * d ** -0.5
        s = jnp.where(valid[None, :, None, :], s, -jnp.inf)
        m = jnp.max(s, axis=-1, keepdims=True)
        p = jnp.exp(s - m)
        den = jnp.sum(p, axis=-1)
        o = jnp.einsum('nthj,ntjhd->nthd', p, vg.astype(jnp.float32)) / den[..., None]
        outs.append(o)
        lses.append(m[..., 0] + jnp.log(den))
    return merge_branches(outs, lses)

def hier_moe(h, w_rg, b_rg, w_re, b_re, w_gate, w_up, w_down):
    n, length, d = h.shape
    f32 = jnp.float32
    x = h.reshape(n * length, d)
    p_group = jax.nn.softmax((x @ w_rg + b_rg).astype(f32), axis=-1)
    p_top, g_top = lax.top_k(p_group, 1)
    g_onehot = jax.nn.one_hot(g_top[:, 0], N_GROUPS, dtype=f32)
    e_logits = (x @ w_re + b_re).astype(f32).reshape(-1, N_GROUPS, E_PER_GROUP)
    p_in = jax.nn.softmax(jnp.einsum('tge,tg->te', e_logits, g_onehot), axis=-1)
    w_top, e_top = lax.top_k(p_in, TOP_K_IN_GROUP)
    w_top = w_top / jnp.sum(w_top, axis=-1, keepdims=True)
    gate_in = jnp.einsum('tk,tke->te', w_top, jax.nn.one_hot(e_top, E_PER_GROUP, dtype=f32))
    gate = g_onehot[:, :, None] * (p_top * gate_in)[:, None, :]
    y = jnp.zeros((n * length, d), f32)
    for gi in range(N_GROUPS):
        hid = jax.nn.silu(jnp.einsum('td,edf->tef', x, w_gate[gi])) * jnp.einsum('td,edf->tef', x, w_up[gi])
        y = y + jnp.einsum('tef,efd->td', hid * gate[:, gi, :, None], w_down[gi])
    return y.astype(h.dtype).reshape(n, length, d)

def trunk(x, c, a_ssm, a_conv, b_conv, kv_k, kv_v, p, sample):
    n, length, _ = x.shape
    cond = jax.nn.silu(c)
    new_ssm, new_aconv, new_bconv, new_k, new_v = [], [], [], [], []
    for layer in range(DEPTH):
        mod = cond @ p['w_ada'][layer] + p['b_ada'][layer]
        sh1, sc1, g1, sh2, sc2, g2 = [m[:, None, :] for m in jnp.split(mod, 6, axis=-1)]
        h = rms_norm(x, p['norm1'][layer]) * (1 + sc1) + sh1
        if layer % 2 == 0:
            e = layer // 2
            y, s_new, ca, cb = even_mixer(h, a_conv[e], b_conv[e], a_ssm[e], p['w_in_even'][e],
                                          p['conv_a_w'][e], p['a_log'][e], p['dt_bias'][e],
                                          p['o_gain_a'][e], p['conv_b_w'][e], p['w_out_even'][e])
            new_ssm.append(s_new)
            new_aconv.append(ca)
            new_bconv.append(cb)
        else:
            o_i = layer // 2
            qkv = (h @ p['w_qkv_odd'][o_i]).reshape(n, length, 3, H_C, HD_C)
            q, k, v = qkv[:, :, 0], qkv[:, :, 1], qkv[:, :, 2]
            if sample:
                attn = dilated_attention_sample(q, k, v, kv_k[o_i], kv_v[o_i])
                new_k.append(k)
                new_v.append(v)
            else:
                attn = dilated_attention_prompt(q, k, v)
                keep = min(WINDOW_MAX, length)
                new_k.append(k[:, length - keep:])
                new_v.append(v[:, length - keep:])
            y = attn.astype(x.dtype).reshape(n, length, H_C * HD_C) @ p['w_out_odd'][o_i]
        x = x + g1 * y.astype(x.dtype)
        h = rms_norm(x, p['norm2'][layer]) * (1 + sc2) + sh2
        x = x + g2 * hier_moe(h, p['w_router_group'][layer], p['b_router_group'][layer],
                              p['w_router_expert'][layer], p['b_router_expert'][layer],
                              p['w_exp_gate'][layer], p['w_exp_up'][layer], p['w_exp_down'][layer])
    y_out = rms_norm(x, p['norm_f'])
    return (y_out, jnp.stack(new_ssm), jnp.stack(new_aconv), jnp.stack(new_bconv),
            jnp.stack(new_k), jnp.stack(new_v))

def setup_inputs(seed: int = 0) -> dict:
    key = jax.random.key(seed)
    ks = iter(jax.random.split(key, 40))
    f32 = jnp.float32
    d = D_MODEL
    w_buf = min(WINDOW_MAX, PAST_LEN)

    def nrm(shape, scale=1.0):
        return jax.random.normal(next(ks), shape, f32) * scale

    x_prompt = nrm((BATCH, SEQ, d))
    x_sample = nrm((DEC_BATCH, DEC_SEQ, d))
    state_a_ssm = nrm((N_EVEN, DEC_BATCH, H_A, DK_A, DV_A), DK_A ** -0.5)
    state_a_conv = nrm((N_EVEN, DEC_BATCH, CONV_A - 1, QKV_A))
    state_b_conv = nrm((N_EVEN, DEC_BATCH, CONV_B - 1, D_B))
    cache_c_k = nrm((N_ODD, DEC_BATCH, w_buf, H_C, HD_C))
    cache_c_v = nrm((N_ODD, DEC_BATCH, w_buf, H_C, HD_C))
    c_prompt = nrm((BATCH, d))
    c_sample = nrm((DEC_BATCH, d))
    w_ada = nrm((DEPTH, d, 6 * d), 0.5 * d ** -0.5)
    b_ada = nrm((DEPTH, 6 * d), 0.02)
    norm1 = 1.0 + nrm((DEPTH, d), 0.02)
    norm2 = 1.0 + nrm((DEPTH, d), 0.02)
    norm_f = 1.0 + nrm((d,), 0.02)
    w_in_even = nrm((N_EVEN, d, IN_EVEN), d ** -0.5)
    conv_a_w = nrm((N_EVEN, CONV_A, QKV_A), CONV_A ** -0.5)
    a_log = jnp.log(jax.random.uniform(next(ks), (N_EVEN, H_A), f32, 1.0, 16.0))
    dt = jnp.exp(jax.random.uniform(next(ks), (N_EVEN, H_A), f32, math.log(1e-3), math.log(1e-1)))
    dt_bias = dt + jnp.log(-jnp.expm1(-dt))
    o_gain_a = 1.0 + nrm((N_EVEN, DV_A), 0.02)
    conv_b_w = nrm((N_EVEN, CONV_B, D_B), CONV_B ** -0.5)
    w_out_even = nrm((N_EVEN, CAT_EVEN, d), CAT_EVEN ** -0.5)
    w_qkv_odd = nrm((N_ODD, d, 3 * H_C * HD_C), d ** -0.5)
    w_out_odd = nrm((N_ODD, H_C * HD_C, d), (H_C * HD_C) ** -0.5)
    w_router_group = nrm((DEPTH, d, N_GROUPS), d ** -0.5)
    b_router_group = nrm((DEPTH, N_GROUPS), 0.01)
    w_router_expert = nrm((DEPTH, d, N_GROUPS * E_PER_GROUP), d ** -0.5)
    b_router_expert = nrm((DEPTH, N_GROUPS * E_PER_GROUP), 0.01)
    w_exp_gate = nrm((DEPTH, N_GROUPS, E_PER_GROUP, d, D_EXPERT), d ** -0.5)
    w_exp_up = nrm((DEPTH, N_GROUPS, E_PER_GROUP, d, D_EXPERT), d ** -0.5)
    w_exp_down = nrm((DEPTH, N_GROUPS, E_PER_GROUP, D_EXPERT, d), D_EXPERT ** -0.5)
    return {
        'x_prompt': x_prompt, 'x_sample': x_sample,
        'state_a_ssm': state_a_ssm, 'state_a_conv': state_a_conv, 'state_b_conv': state_b_conv,
        'cache_c_k': cache_c_k, 'cache_c_v': cache_c_v,
        'c_prompt': c_prompt, 'c_sample': c_sample,
        'w_ada': w_ada, 'b_ada': b_ada, 'norm1': norm1, 'norm2': norm2, 'norm_f': norm_f,
        'w_in_even': w_in_even, 'conv_a_w': conv_a_w, 'a_log': a_log, 'dt_bias': dt_bias,
        'o_gain_a': o_gain_a, 'conv_b_w': conv_b_w, 'w_out_even': w_out_even,
        'w_qkv_odd': w_qkv_odd, 'w_out_odd': w_out_odd,
        'w_router_group': w_router_group, 'b_router_group': b_router_group,
        'w_router_expert': w_router_expert, 'b_router_expert': b_router_expert,
        'w_exp_gate': w_exp_gate, 'w_exp_up': w_exp_up, 'w_exp_down': w_exp_down,
    }

def reference(x_prompt, x_sample, state_a_ssm, state_a_conv, state_b_conv, cache_c_k, cache_c_v,
              c_prompt, c_sample, w_ada, b_ada, norm1, norm2, norm_f, w_in_even, conv_a_w, a_log,
              dt_bias, o_gain_a, conv_b_w, w_out_even, w_qkv_odd, w_out_odd, w_router_group,
              b_router_group, w_router_expert, b_router_expert, w_exp_gate, w_exp_up, w_exp_down):
    p = {
        'w_ada': w_ada, 'b_ada': b_ada, 'norm1': norm1, 'norm2': norm2, 'norm_f': norm_f,
        'w_in_even': w_in_even, 'conv_a_w': conv_a_w, 'a_log': a_log, 'dt_bias': dt_bias,
        'o_gain_a': o_gain_a, 'conv_b_w': conv_b_w, 'w_out_even': w_out_even,
        'w_qkv_odd': w_qkv_odd, 'w_out_odd': w_out_odd,
        'w_router_group': w_router_group, 'b_router_group': b_router_group,
        'w_router_expert': w_router_expert, 'b_router_expert': b_router_expert,
        'w_exp_gate': w_exp_gate, 'w_exp_up': w_exp_up, 'w_exp_down': w_exp_down,
    }
    nb = x_prompt.shape[0]
    zero_ssm = jnp.zeros((N_EVEN, nb, H_A, DK_A, DV_A), jnp.float32)
    zero_aconv = jnp.zeros((N_EVEN, nb, CONV_A - 1, QKV_A), x_prompt.dtype)
    zero_bconv = jnp.zeros((N_EVEN, nb, CONV_B - 1, D_B), x_prompt.dtype)
    y_prompt, ssm_p, aconv_p, bconv_p, k_p, v_p = trunk(
        x_prompt, c_prompt, zero_ssm, zero_aconv, zero_bconv, None, None, p, False)
    y_sample, ssm_s, aconv_s, bconv_s, k_s, v_s = trunk(
        x_sample, c_sample, state_a_ssm, state_a_conv, state_b_conv, cache_c_k, cache_c_v, p, True)
    return (y_prompt, y_sample, ssm_p, ssm_s, aconv_p, aconv_s, bconv_p, bconv_s, k_p, k_s, v_p, v_s)


_drawn_inputs = setup_inputs


def setup_inputs(seed=0):
    import zlib

    import numpy as np

    out = dict(_drawn_inputs(seed))
    spreads = {}
    factors = {'norm2': 4.385,
     'norm_f': 2.74,
     'o_gain_a': 8.0,
     'b_router_group': 8.0,
     'b_router_expert': 6.066}
    for name, (base, spread) in spreads.items():
        noise = np.random.default_rng([zlib.crc32(name.encode()), seed]).standard_normal(out[name].shape)
        drawn = base * np.exp(spread * noise) if base else spread * noise
        out[name] = jnp.asarray(drawn.astype(out[name].dtype))
    for name, factor in factors.items():
        out[name] = (out[name] * factor).astype(out[name].dtype)
    return out
```

```python
from contextlib import ExitStack

import numpy as np

import concourse.bass as bass
from concourse import mybir

F32 = mybir.dt.float32
I32 = mybir.dt.int32
ALU = mybir.AluOpType
ACT = mybir.ActivationFunctionType
AX = mybir.AxisListType

P = 128
D = 1024
C = D // P
NP_, NS, NB = 256, 64, 8
LS = NS // NB
T = NP_ + NS
TT = [(0, 128), (128, 128), (256, 64)]
NCOND = 1 + NB
H = 4
HIST = 3
EP, ES = HIST + NP_, HIST + LS
EW = EP + NB * ES
CW = EW - HIST
EPS = 1e-6
NG, NE, DE = 4, 8, 256
SLOTS = 128
R = 6
U = 2048
NEG = -1e30
NBANK = 8


def constants():
    i = np.arange(P)
    j = i[:, None]
    i = i[None, :]
    out = {"ident": j == i, "ones": np.ones((P, P)), "upto": j <= i, "after": j > i}
    for s in (1, 2, 4, 8, 16, 32, 64):
        out[f"lev{s}"] = (j // (2 * s) == i // (2 * s)) & (j // s % 2 == 0) & (i // s % 2 == 1)
    same = (j // LS == i // LS)[:, :NS]
    out["upto_s"] = same & (j <= i)[:, :NS]
    out["after_s"] = same & (j > i)[:, :NS]
    out["batch_rows"] = j // LS == np.arange(NB)[None, :]
    out["iota"] = np.broadcast_to(i, (P, P))
    out["iota8"] = np.broadcast_to(np.arange(8)[None, ::-1] + 1, (P, 8))
    out["eps"] = np.full((P, 1), EPS)
    out["one"] = np.ones((P, 1))
    return {k: np.asarray(v, np.float32) for k, v in out.items()}


def attention_constants():
    def count(d):
        return ((d >= 0) & (d <= 128)) * 1.0 + ((d >= 0) & (d <= 512) & (d % 4 == 0)) + ((d >= 0) & (d <= 2048) & (d % 16 == 0))
    p = np.arange(P)[:, None]
    k = np.arange(256)[None]
    col = np.arange(120)[None] - 56
    prompt = np.concatenate([count(p - k[:, :128]), count(p + 128 - k)], 1)
    cache = count(256 + p % LS - k)
    new = np.where((col >= 0) & (col < LS), count(p % LS - col), 0.0)
    out = {}
    for n, c in (("prompt", prompt), ("cache", cache), ("new", new)):
        out["cnt_" + n] = c
        out["neg_" + n] = np.where(c > 0, 0.0, NEG)
    return {k: np.asarray(v, np.float32) for k, v in out.items()}


def packed(tables):
    return np.ascontiguousarray(np.concatenate(list(tables.values()), 1))


def trunk_program(nc, I, O):
    at, n = {}, 0
    for k, v in constants().items():
        at[k] = (n, n + v.shape[1])
        n += v.shape[1]
    NCONST = n
    aat, n = {}, 0
    for k, v in attention_constants().items():
        aat[k] = (n, n + v.shape[1])
        n += v.shape[1]
    NACONST = n

    with ExitStack() as ctx:
        def sb(name, shape, dt=F32):
            return ctx.enter_context(nc.sbuf_tensor(name, shape, dt))

        def sem(name):
            return ctx.enter_context(nc.semaphore(name))

        ring = sb("ring", [P, R, U])
        const = sb("const", [P, NCONST])
        xT = sb("xT", [P, C, T])
        hT = sb("hT", [P, C, T])
        scratch = sb("scratch", [P, C, T])
        rstd = sb("rstd", [P, T])
        mod = sb("mod", [P, 6, C, NCOND])
        gainA = sb("gainA", [P, C, NCOND])
        cols = sb("cols", [P, C, 26])
        condT = sb("condT", [P, C, NCOND])
        small = sb("small", [P, 3, 40])
        flag = sb("flag", [1, 1], I32)
        gates = sb("gates", [P, 3, NG * NE])
        tiny = sb("tiny", [P, 512])
        ARENA = 28080
        arena = sb("arena", [P, ARENA])

        def K(name, rows=P):
            a, b = at[name]
            return const[0:rows, a:b]

        def modrow(l):
            return arena[0:NCOND, 13232:13232 + 1024].rearrange("p (u n) -> p u n", u=2) if l == 0 \
                else arena[0:NCOND, 0:1024].rearrange("p (u n) -> p u n", u=2)


        def carve(spec, base=0):
            out, n = {}, base
            for name, size in spec:
                out[name] = arena[:, n:n + size]
                n += size
            assert n <= ARENA, n
            return out

        A0 = carve([("ext", 12 * EW), ("cT", 12 * T), ("z", 4 * T), ("bx", 4 * EW), ("bg", 4 * T),
                    ("cg", 4 * T), ("cat", 8 * T), ("gam", 12 * P), ("AT", 12 * P), ("X", 12 * P),
                    ("qkg", 12 * P), ("XT", 12 * P), ("LT", 12 * P), ("PB", 12 * P), ("vb", 12 * P)])
        AT_AT = 12 * EW + 12 * T + 4 * T + 4 * EW + 4 * T + 4 * T + 8 * T + 12 * P
        ext = A0["ext"].rearrange("p (m e) -> p m e", e=EW)
        states = A0["ext"][:, 0:NB * H * P].rearrange("p (b h v) -> p b h v", b=NB, h=H)
        cT = A0["cT"].rearrange("p (m t) -> p m t", t=T)
        zT = A0["z"].rearrange("p (m t) -> p m t", t=T)
        bx = A0["bx"].rearrange("p (m e) -> p m e", e=EW)
        kb = A0["bx"][:, 0:H * T].rearrange("p (m t) -> p m t", t=T)
        bg = A0["bg"].rearrange("p (m t) -> p m t", t=T)
        cg = A0["cg"].rearrange("p (m t) -> p m t", t=T)
        qd = cg
        catT = A0["cat"].rearrange("p (m t) -> p m t", t=T)

        def sysview(name):
            return A0[name].rearrange("p (t h i) -> p t h i", t=3, h=H)
        gam, AT, X, qkg, XT, LT, PB, vb = [sysview(x) for x in ("gam", "AT", "X", "qkg", "XT", "LT", "PB", "vb")]
        kd = scratch[:, :, :].rearrange("p c t -> p (c t)")[:, 0:12 * P].rearrange("p (t h i) -> p t h i", t=3, h=H)
        uu, RR = LT, PB
        oT = cT[:, 0:H, :]
        LT_AT = AT_AT + 4 * 12 * P
        kTm = arena[:, AT_AT:AT_AT + H * NB * NS].rearrange("p (h b i) -> p h b i", h=H, b=NB)
        ue = arena[0:NS, AT_AT + 2048:AT_AT + 3072].rearrange("p (b v) -> p b v", b=NB)
        convacc = scratch[:, :, :].rearrange("p c t -> p (c t)")
        S0 = tiny[:, :].rearrange("p (h v) -> p h v", h=H)
        rowsA0 = arena[0:28, 20000:20000 + 1536]
        rowsB0 = arena[0:19, 21600:21600 + 512]
        rowsM0 = arena[0:26, 22200:22200 + D]
        xload = arena[:, 23300:23300 + 3 * D].rearrange("p (t d) -> p t d", t=3)
        colsA = sb("colsA", [P, 12, 28])
        colsB = sb("colsB", [P, 4, 19])
        colsO = sb("colsO", [P, 1])
        wab = sb("wab", [P, C, 8])
        dtb = sb("dtb", [P, 2, 4])
        wr = sb("wr", [P, 2, C, 36])
        br = sb("br", [P, 2, 36])
        gab = sb("gab", [P, 3, 8])
        gg = sb("gg", [P, 3, 4])
        sc8 = sb("sc8", [P, 3, 16])
        beta = sb("beta", [P, 3, 4])
        nbe = sb("nbe", [P, 3, 4])
        gcols = sb("gcols", [P, 3, 8])
        egc = sb("egc", [P, 3, 8])
        GAM_AT = AT_AT - 12 * P
        l2std = arena[:, GAM_AT:GAM_AT + 8 * T].rearrange("p (m t) -> p m t", t=T)
        bconv = A0["vb"][:, 0:2 * EW].rearrange("p (u e) -> p u e", u=2)
        osq = A0["bx"][:, 0:H * T].rearrange("p (m t) -> p m t", t=T)
        ostd = A0["gam"][:, 0:H * T].rearrange("p (m t) -> p m t", t=T)
        onehot = sb("onehot", [P, 3, NG])
        eG = hT[:, 0:H, :]
        stout = arena[0:27, LT_AT:LT_AT + 2048]
        stg = tiny[:, 0:12 * 27]
        stgb = tiny[:, 324:324 + 4 * 18]

        QB = C * (P + 16)
        A1 = carve([("qkv", 24 * T), ("vtok", 3 * D), ("Kc", 2 * 2 * D), ("Vc", 2 * 2 * D), ("KT", C * 256),
                    ("qbd", 2 * QB), ("sc", 2 * 384), ("pr", 2 * 384), ("pT", 2 * 384), ("msk", NACONST)])
        qkvT = A1["qkv"].rearrange("p (m t) -> p m t", t=T)
        vtok = A1["vtok"].rearrange("p (t d) -> p t d", t=3)
        ktok = scratch[:, :, :].rearrange("p c t -> p (c t)")[:, 0:2 * D].rearrange("p (u d) -> p u d", u=2)
        Kc = A1["Kc"].rearrange("p (u a d) -> p u a d", u=2, a=2)
        Vc = A1["Vc"].rearrange("p (u a d) -> p u a d", u=2, a=2)
        KT = A1["KT"].rearrange("p (c j) -> p c j", c=C)
        qbd = A1["qbd"].rearrange("p (u q) -> p u q", u=2)
        scr = A1["sc"].rearrange("p (u j) -> p u j", u=2)
        prb = A1["pr"].rearrange("p (u j) -> p u j", u=2)
        pT = A1["pT"].rearrange("p (u j) -> p u j", u=2)
        attnT = hT
        stat = sb("stat", [P, 2, 8])

        def KA(name):
            a, b = aat[name]
            return A1["msk"][:, a:b]

        AM = carve([("htok", 3 * D), ("hg", C * NG * SLOTS), ("perm", 3 * NG * SLOTS), ("permT", NG * T),
                    ("ys", NG * D), ("sg", 2 * DE), ("hid", 2 * DE), ("hidT", 2 * DE), ("ring2", 3 * U), ("rt", 600)])
        htok = AM["htok"].rearrange("p (t d) -> p t d", t=3)
        hg = AM["hg"].rearrange("p (c s) -> p c s", c=C)
        perm = AM["perm"].rearrange("p (t g s) -> p t g s", t=3, g=NG)
        permT = AM["permT"].rearrange("p (g t) -> p g t", g=NG)
        ys = AM["ys"].rearrange("p (g d) -> p g d", g=NG)
        sg = AM["sg"].rearrange("p (u f) -> p u f", u=2)
        hid = AM["hid"].rearrange("p (u f) -> p u f", u=2)
        hidT = AM["hidT"].rearrange("p (u f s) -> p u f s", u=2, f=2)
        ring2 = AM["ring2"].rearrange("p (u n) -> p u n", u=3)
        rt = AM["rt"]
        ytok = AM["htok"].rearrange("p (t d) -> p t d", t=3)
        rank = sb("rank", [P, 3, NG])
        gslot = sb("gslot", [P, NG * NE])

        bank = [ctx.enter_context(nc.psum_tensor(f"bank{i}", [P, 512], F32)) for i in range(NBANK)]

        tile_of, ntile = {}, 0

        def tiles(name, n):
            nonlocal ntile
            tile_of[name] = ntile
            ntile += n

        tiles("cols", 3)
        tiles("x", C)
        for l in range(2):
            tiles(f"ada{l}", 24)
            tiles(f"norm{l}1", 1)
            if l == 0:
                tiles("in_ab", 1)
                tiles("in", 28)
                tiles("st_out", 4)
                tiles("l2", 8)
                tiles("gcol", 1)
                tiles("grow", 3)
                tiles("brow", 3)
                tiles("vt", 3)
                tiles("kt", 3)
                tiles("at", 3)
                tiles("qk", 3)
                tiles("xt0", 3)
                tiles("lev", 3 * (2 * 6 + 2))
                tiles("dl0", 3)
                tiles("dl1", 4)
                tiles("dl2", 3)
                tiles("dstate", 8)
                tiles("onorm", 4)
            else:
                tiles("qkv", 24)
                tiles("ktok", 6)
                tiles("vtok", 6)
                tiles("attp", 16 * 2 + 8)
                tiles("atts", 8 * 7)
            tiles(f"out{l}", C)
            tiles(f"norm{l}2", 1)
            tiles(f"rt{l}", 1)
            tiles(f"ht{l}", 6)
            tiles(f"rk{l}", 1)
        tiles("normf", 1)
        tiles("y", 6)

        attp, atts = {}, {}
        for st in range(18):
            if st < 16:
                attp["S", st] = tile_of["attp"] + len(attp)
            if 1 <= st <= 16:
                attp["T", st - 1] = tile_of["attp"] + len(attp)
            if st >= 2 and st % 2 == 0:
                attp["O", st // 2 - 1] = tile_of["attp"] + len(attp)
        for b in range(NB + 1):
            for i in range(4 if b < NB else 0):
                atts["K", b, i] = tile_of["atts"] + len(atts)
            if b:
                atts["T", b - 1] = tile_of["atts"] + len(atts)
            if b < NB:
                atts["S", b] = tile_of["atts"] + len(atts)
            if b:
                atts["O", b - 1] = tile_of["atts"] + len(atts)
        bank_full = [sem(f"bank_full{i}") for i in range(NBANK)]

        def B(k):
            return bank[k % NBANK]

        def filled(ins, k):
            ins.then_inc(bank_full[k % NBANK], 1)

        def full(eng, k):
            eng.wait_ge(bank_full[k % NBANK], k // NBANK + 1)

        unit_of, nunit = {}, 0

        def units(name, n):
            nonlocal nunit
            unit_of[name] = nunit
            nunit += n

        units("ada0", 24)
        units("in", 14)
        units("out0", 4)
        units("moe0", 96)
        units("ada1", 24)
        units("qkv", 12)
        units("out1", 4)
        units("moe1", 96)
        
        unit_loaded = [sem(f"unit_loaded{i}") for i in range(R)]

        def need_unit(pe, n):
            pe.wait_ge(unit_loaded[n % R], 16 * (n // R + 1))

        def slot(n, width=256):
            return ring[:, n % R, :].rearrange("p (c n) -> p c n", n=width)

        ld_const, ld_rows, ld_x, ld_small = sem("ld_const"), sem("ld_rows"), sem("ld_x"), sem("ld_small")
        ld_states, ld_amask = sem("ld_states"), sem("ld_amask")
        ld_kc, ld_vc = [sem("ld_kc0"), sem("ld_kc1")], [sem("ld_vc0"), sem("ld_vc1")]
        sent = sem("sent")
        ktok_sent = sem("ktok_sent")
        NROWS, NSMALL = 10, 12
        vstep, astep, gstep = sem("vstep"), sem("astep"), sem("gstep")
        dve_results, act_results, pool_results = sem("dve_results"), sem("act_results"), sem("pool_results")
        LEVELS = [(s, [0, 1, 2] if s <= 4 else [0, 1]) for s in (2, 4, 8, 16, 32, 64)]

        DVE_ORDER = ["cols", "x0"]
        for l in range(2):
            DVE_ORDER += [(f"mod{l}", q) for q in range(12)] + [f"xn{l}1", f"hs{l}1"]
            if l == 0:
                DVE_ORDER += ["gab", "g_abs", "g_e"] + [("conv", m) for m in range(12)] + ["g"]
                DVE_ORDER += [("bx", m) for m in range(4)] + ["catb", "qk", "gcol", "gd0", "gd1", "gd2", "gam"]
                DVE_ORDER += ["kb0", "kb1", "kb2", "vb0", "vb1", "vb2", "kd0", "kd1", "kd2", "at0", "at1", "at2"]
                DVE_ORDER += [("xt", 1, t) for t in range(3)] + ["qkg0", "qkg1", "qkg2", "qd"]
                for s, ts in LEVELS:
                    DVE_ORDER += [("lt", s, t) for t in ts] + [(n, s, t) for t in ts for n in ("xt", "xi")]
                DVE_ORDER += ["ktm", "o0", "s1", "r1", "o1", "s2", "r2", "o2"]
                for h_ in range(H):
                    DVE_ORDER += [("ue", h_), ("st", 2 * h_), ("st", 2 * h_ + 1)]
                DVE_ORDER += ["orstd", "cat"]
            else:
                DVE_ORDER += [("vt", i) for i in range(6)]
                for h_ in range(17):
                    DVE_ORDER += [("amax", h_)] if h_ < 16 else []
                    DVE_ORDER += [("apr", h_ - 1)] if h_ else []
                for b in range(NB + 1):
                    DVE_ORDER += [("kt", b, 2), ("kt", b, 3)] if b < NB else []
                    DVE_ORDER += [("smax", b)] if b < NB else []
                    DVE_ORDER += [("sout", b - 1)] if b else []
                    DVE_ORDER += [("spr", b)] if b < NB else []
            DVE_ORDER += [(f"xo{l}", m) for m in range(C)] + [f"xn{l}2", f"hs{l}2"]
            DVE_ORDER += [f"rt{l}", f"rm{l}", f"oh{l}", f"rt2{l}", f"flag{l}", f"x{l}2"]
        DVE_ORDER += ["xnf"]
        ACT_ORDER = ["cond"]
        for l in range(2):
            ACT_ORDER += [(f"row{l}", q) for q in range(12)] + [f"sq{l}1", f"std{l}1", f"hp{l}1"]
            if l == 0:
                for m in range(24):
                    ACT_ORDER += [("ext", m)] if m < 12 else [("z", m)] if m < 16 else [("gt", m)]
                    ACT_ORDER += [("cv", m - 2)] if 2 <= m < 14 else []
                ACT_ORDER += ["g_ea", "g_eb", "qksq"] + [("so", i) for i in range(4)] + [("l2s", m) for m in range(8)]
                ACT_ORDER += ["eG0", "eG1", "eG2", "egc", "ge", "x0inv0", "x0inv1", "x0inv2"]
                for s, ts in LEVELS:
                    ACT_ORDER += [("pb", s, t) for t in ts]
                ACT_ORDER += ["u0", "u1", "u2", "osq"] + [("os", h_) for h_ in range(H)]
            else:
                ACT_ORDER += [("qkv", m) for m in range(24)] + [("ktok", i) for i in range(6)]
                for h_ in range(18):
                    ACT_ORDER += [("aexp", h_)] if h_ < 16 else []
                    ACT_ORDER += [("apT", h_ - 1)] if 1 <= h_ <= 16 else []
                    ACT_ORDER += [("aout", h_ // 2 - 1)] if h_ >= 2 and h_ % 2 == 1 else []
                for b in range(NB + 1):
                    ACT_ORDER += [("kt", b, 0), ("kt", b, 1)] if b < NB else []
                    ACT_ORDER += [("spT", b - 1)] if b else []
                    ACT_ORDER += [("sexp", b)] if b < NB else []
            ACT_ORDER += [f"sq{l}2", f"std{l}2", f"hp{l}2"] + [(f"ht{l}", i) for i in range(6)] + [f"re{l}", f"re2{l}"]
        ACT_ORDER += ["sqf", "stdf", "hpf"] + [("yt", i) for i in range(6)]
        POOL_ORDER = ["hist", "stg", "mixer0", "qbd0"] + [("qbd", b) for b in range(NB)] + ["mixer1"]
        ORDER = {"dve": (dve_results, {n: i for i, n in enumerate(DVE_ORDER)}),
                 "act": (act_results, {n: i for i, n in enumerate(ACT_ORDER)}),
                 "pool": (pool_results, {n: i for i, n in enumerate(POOL_ORDER)})}
        made = {"dve": 0, "act": 0, "pool": 0}

        def after(eng, who, name):
            s, order = ORDER[who]
            eng.wait_ge(s, order[name] + 1)

        def result(who, name, ins):
            s, order = ORDER[who]
            assert order[name] == made[who], (who, name, order[name], made[who])
            made[who] += 1
            ins.then_inc(s, 1)

        readers = {}

        def reads(name, *per_tile):
            for m, rs in enumerate(per_tile):
                readers[tile_of[name] + m] = rs if isinstance(rs, list) else [rs]

        reads("cols", *[("dve", "cols")] * 3)
        reads("x", *[("dve", "x0")] * C)
        for l in range(2):
            for q in range(12):
                readers[tile_of[f"ada{l}"] + (0 if q == 0 else 2 * q - 1)] = [("act", (f"row{l}", q))]
                readers[tile_of[f"ada{l}"] + (2 * q + 2 if q < 11 else 23)] = [("dve", (f"mod{l}", q))]
            for s in "12":
                reads(f"norm{l}{s}", ("act", f"std{l}{s}"))
            reads(f"out{l}", *[("dve", (f"xo{l}", m)) for m in range(C)])
            reads(f"rt{l}", ("dve", f"rt{l}"))
            reads(f"ht{l}", *[("act", (f"ht{l}", i)) for i in range(6)])
            reads(f"rk{l}", ("dve", f"flag{l}"))
        reads("in_ab", ("dve", "gab"))
        reads("in", *[("act", ("ext", m)) for m in range(12)], *[("act", ("z", m)) for m in range(12, 16)],
              *[("act", ("gt", m)) for m in range(16, 24)], *[("dve", ("bx", m)) for m in range(4)])
        reads("st_out", *[("act", ("so", i)) for i in range(4)])
        reads("l2", *[("act", ("l2s", m)) for m in range(8)])
        reads("gcol", ("dve", "gcol"))
        reads("grow", *[[("act", f"eG{t}"), ("dve", f"gd{t}")] for t in range(3)])
        for name, who, res in (("brow", "dve", "kb"), ("vt", "dve", "vb"), ("kt", "dve", "kd"), ("at", "dve", "at"),
                               ("qk", "dve", "qkg"), ("xt0", "act", "x0inv")):
            reads(name, *[(who, f"{res}{t}") for t in range(3)])
        k = tile_of["lev"]
        for s, ts in LEVELS:
            for t in ts:
                readers[k] = [("act", ("pb", s, t))]
                k += 1
            for t in ts:
                readers[k], readers[k + 1] = [("dve", ("xt", s, t))], [("dve", ("xi", s, t))]
                k += 2
        reads("dl0", ("act", "u0"), ("dve", "o0"), ("dve", "s1"))
        reads("dl1", ("dve", "r1"), ("act", "u1"), ("dve", "o1"), ("dve", "s2"))
        reads("dl2", ("dve", "r2"), ("act", "u2"), ("dve", "o2"))
        reads("dstate", *[("dve", ("st", j)) for j in range(8)])
        reads("onorm", *[("act", ("os", h_)) for h_ in range(H)])
        reads("qkv", *[("act", ("qkv", m)) for m in range(24)])
        reads("ktok", *[("act", ("ktok", i)) for i in range(6)])
        reads("vtok", *[("dve", ("vt", i)) for i in range(6)])
        for (kind, n), k in attp.items():
            readers[k] = [{"S": ("dve", ("amax", n)), "T": ("act", ("apT", n)), "O": ("act", ("aout", n))}[kind]]
        for key, k in atts.items():
            if key[0] == "K":
                readers[k] = [("act" if key[2] < 2 else "dve", ("kt", key[1], key[2]))]
            else:
                readers[k] = [{"S": ("dve", ("smax", key[1])), "T": ("act", ("spT", key[1])),
                               "O": ("dve", ("sout", key[1]))}[key[0]]]
        reads("normf", ("act", "stdf"))
        reads("y", *[("act", ("yt", i)) for i in range(6)])

        def claim(pe, k):
            if k >= NBANK:
                for who, name in readers[k - NBANK]:
                    after(pe, who, name)

        PASS = ("perm", "aux", "auxfree", "gsl", "gu", "silu", "hid", "tr", "hidT", "down", "yadd", "sc", "scfree")
        moe = {k: sem(f"moe_{k}") for k in PASS}
        more = [{k: sem(f"more{l}_{k}") for k in PASS + ("wl0", "wl1", "wl2", "step")} for l in range(2)]

        unit_tile = {}
        for l in range(2):
            for u in range(24):
                q = u // 2
                unit_tile[unit_of[f"ada{l}"] + u] = tile_of[f"ada{l}"] + (0 if q == 0 else 2 * q - 1)
            for u in range(4):
                unit_tile[unit_of[f"out{l}"] + u] = tile_of[f"out{l}"] + 2 * u + 1
        for u in range(14):
            unit_tile[unit_of["in"] + u] = tile_of["in"] + 2 * u + 1
        for u in range(12):
            unit_tile[unit_of["qkv"] + u] = tile_of["qkv"] + 2 * u + 1

        def wait_slot(sp, n):
            n -= R
            if n < 0:
                return
            if n in unit_tile:
                full(sp, unit_tile[n])
                return
            l = 0 if n < unit_of["ada1"] else 1
            wait_expert(sp, 32 * l + (n - unit_of[f"moe{l}"]) // 3, (n - unit_of[f"moe{l}"]) % 3)

        def wait_expert(sp, k, w):
            if w < 2:
                sp.wait_ge(moe["gu"], 2 * k + w + 1)
            else:
                sp.wait_ge(moe["down"], k + 1)

        gate_v = I["w_exp_gate"].rearrange("l g e (c p) f -> (l g e) p c f", p=P)
        up_v = I["w_exp_up"].rearrange("l g e (c p) f -> (l g e) p c f", p=P)
        down_v = I["w_exp_down"].rearrange("l g e (f p) d -> (l g e) p f d", p=P)
        expert_views = [(gate_v, 256), (up_v, 256), (down_v, D)]

        def wide(w, a):
            return w.rearrange("(c p) n -> p c n", p=P)[:, :, a:a + 256]

        block = ctx.enter_context(nc.Block())

        @block.sync
        def _(sp):
            def load(n, src, width=256):
                wait_slot(sp, n)
                sp.dma_start(slot(n, width), src).then_inc(unit_loaded[n % R], 16)

            def load_experts(l):
                base = unit_of[f"moe{l}"]
                for n in range(12):
                    view, width = expert_views[n % 3]
                    load(base + n, view[NG * NE * l + n // 3], width)
                with sp.Fori(1, NG * NE // 4) as q:
                    for n in range(12):
                        view, width = expert_views[n % 3]
                        wait_expert(sp, 4 * q + (32 * l + (n - R) // 3), (n - R) % 3)
                        src = view[bass.ds(4 * q + (NG * NE * l + n // 3), 1)].rearrange("a p c f -> p (a c) f")
                        sp.dma_start(slot(base + n, width), src).then_inc(unit_loaded[(base + n) % R], 16)
                after(sp, "dve", f"flag{l}")
                S = more[l]
                v = sp.value_load(flag[:, :], min_val=0, max_val=1)
                with sp.If(v >= 1):
                    for i in range(2):
                        if i == 0:
                            for w, (view, width) in enumerate(expert_views):
                                sp.dma_start(ring2[:, w, :].rearrange("p (c n) -> p c n", n=width),
                                             view[NG * NE * l]).then_inc(S[f"wl{w}"], 16)
                        with sp.Fori(1 - i, NG * NE) as e:
                            for w, (view, width) in enumerate(expert_views):
                                if w < 2:
                                    sp.wait_ge(S["gu"], 2 * e + (64 * i + w - 1))
                                else:
                                    sp.wait_ge(S["down"], e + 32 * i)
                                src = view[bass.ds(e + NG * NE * l, 1)].rearrange("a p c f -> p (a c) f")
                                sp.dma_start(ring2[:, w, :].rearrange("p (c n) -> p c n", n=width), src)\
                                  .then_inc(S[f"wl{w}"], 16)

            for l in range(2):
                for u in range(24):
                    load(unit_of[f"ada{l}"] + u, wide(I["w_ada"][l], 256 * u))
                if l == 0:
                    for u in range(14):
                        load(unit_of["in"] + u, wide(I["w_in_even"][0], 256 * u if u < 8 else 256 * u + 8))
                    for u in range(4):
                        load(unit_of["out0"] + u, wide(I["w_out_even"][0], 256 * u))
                else:
                    for u in range(12):
                        load(unit_of["qkv"] + u, wide(I["w_qkv_odd"][0], 256 * u))
                    for u in range(4):
                        load(unit_of["out1"] + u, wide(I["w_out_odd"][0], 256 * u))
                load_experts(l)

        @block.gpsimd
        def _(pool):
            pool.memset(ext[:, :, 0:HIST], 0.0)
            pool.memset(bx[:, :, 0:HIST], 0.0)
            after(pool, "dve", "cols")
            exts = ext[:, :, EP:EW].rearrange("p m (b e) -> p m b e", b=NB)
            bxs = bx[:, :, EP:EW].rearrange("p m (b e) -> p m b e", b=NB)
            pool.memset(bxs[:, :, :, 0:1], 0.0)
            for m in range(12):
                pool.tensor_copy(exts[:, m, :, 0:HIST], colsA[:, m, 0:24].rearrange("p (b j) -> p b j", b=NB))
            for m in range(4):
                ins = pool.tensor_copy(bxs[:, m, :, 1:HIST], colsB[:, m, 0:16].rearrange("p (b j) -> p b j", b=NB))
            result("pool", "hist", ins)
            after(pool, "act", ("ext", 11))
            after(pool, "dve", ("bx", 3))
            s27 = stg.rearrange("p (m r) -> p m r", m=12)
            s18 = stgb.rearrange("p (m r) -> p m r", m=4)
            pool.tensor_copy(s27[:, :, 0:3], ext[:, :, EP - 3:EP])
            for m in range(12):
                pool.tensor_copy(s27[:, m, 3:27].rearrange("p (b j) -> p b j", b=NB), exts[:, m, :, ES - 3:ES])
            pool.tensor_copy(s18[:, :, 0:2], bx[:, :, EP - 2:EP])
            for m in range(4):
                ins = pool.tensor_copy(s18[:, m, 2:18].rearrange("p (b j) -> p b j", b=NB), bxs[:, m, :, ES - 2:ES])
            result("pool", "stg", ins)
            after(pool, "pool", "stg")
            after(pool, "dve", ("conv", 11))
            for h in range(H):
                pool.dma_start(states[:, :, h, :], I["state_a_ssm"][0, :, h].rearrange("b k v -> k b v"))\
                    .then_inc(ld_states, 16)
            after(pool, "act", ("so", 3))
            for src, dst in ((stout[0:3, 0:1536], O["aconv_p"][0, 0]),
                             (stout[3:27, 0:1536], O["aconv_s"][0].rearrange("b j n -> (b j) n")),
                             (stout[0:2, 1536:2048], O["bconv_p"][0, 0]),
                             (stout[2:18, 1536:2048], O["bconv_s"][0].rearrange("b j n -> (b j) n"))):
                pool.dma_start(dst, src).then_inc(sent, 16)
            after(pool, "dve", "s2")
            pool.dma_start(O["ssm_p"][0, 0].rearrange("h k v -> k h v"), S0).then_inc(sent, 16)
            after(pool, "dve", ("st", 7))
            for h in range(H):
                pool.dma_start(O["ssm_s"][0, :, h].rearrange("b k v -> k b v"), states[:, :, h, :]).then_inc(sent, 16)
            pool.wait_ge(sent, 16 * 9)
            result("pool", "mixer0", pool.memset(stat[:, 0, 7:8], 0.0))
            after(pool, "dve", "x02")
            pool.dma_start(A1["msk"], I["amasks"]).then_inc(ld_amask, 16)

            def load_cache(b):
                if b >= 2:
                    after(pool, "dve", ("sout", b - 2))
                kv = [I[n][0, b].rearrange("(a p) h d -> p a (h d)", p=P) for n in ("cache_c_k", "cache_c_v")]
                pool.dma_start(Kc[:, b % 2], kv[0]).then_inc(ld_kc[b % 2], 16)
                pool.dma_start(Vc[:, b % 2], kv[1]).then_inc(ld_vc[b % 2], 16)

            load_cache(0)
            load_cache(1)
            result("pool", "qbd0", pool.memset(A1["qbd"], 0.0))
            after(pool, "pool", "qbd0")
            for i in range(6):
                t = i // 2
                a, n = TT[t]
                if i % 2 == 1:
                    after(pool, "act", ("ktok", i))
                    if t < 2:
                        dst = O["ck_p"][0, 0, a:a + n].rearrange("t h d -> t (h d)")
                    else:
                        dst = O["ck_s"][0].rearrange("b t h d -> (b t) (h d)")
                    pool.dma_start(dst, ktok[0:n, t % 2, :]).then_inc(ktok_sent if t == 0 else sent, 16)
            after(pool, "dve", ("vt", 5))
            for t, (a, n) in enumerate(TT):
                if t < 2:
                    dst = O["cv_p"][0, 0, a:a + n].rearrange("t h d -> t (h d)")
                else:
                    dst = O["cv_s"][0].rearrange("b t h d -> (b t) (h d)")
                pool.dma_start(dst, vtok[0:n, t, :]).then_inc(sent, 16)
            for b in range(NB):
                if b >= 2:
                    after(pool, "dve", ("sout", b - 2))
                for e in range(2):
                    r = slice(64 * e, 64 * e + 64)
                    cells = qbd[r, b % 2, :].rearrange("p (c w) -> p c w", w=P + 16)[:, :, 8 * e:8 * e + LS]
                    ins = pool.tensor_copy(cells, qkvT[r, 0:C, NP_ + LS * b:NP_ + LS * b + LS])
                result("pool", ("qbd", b), ins)
                after(pool, "pool", ("qbd", b))
                if b >= 2:
                    load_cache(b)
            pool.wait_ge(sent, 16 * 14)
            result("pool", "mixer1", pool.memset(stat[:, 1, 7:8], 0.0))
            for t, (a, n) in enumerate(TT):
                after(pool, "act", ("yt", 2 * t + 1))
                dst = O["y_p"][0, a:a + n] if t < 2 else O["y_s"].rearrange("b t d -> (b t) d")
                pool.dma_start(dst, ytok[0:n, t, :]).then_inc(sent, 16)
            pool.wait_ge(sent, 16 * 17)
            pool.wait_ge(ktok_sent, 16)

        @block.tensor
        def _(pe):
            def I_(n):
                return K("ident")[0:n, 0:n]

            def transposes(k, parts):
                claim(pe, k)
                for (a, b), src in parts:
                    ins = pe.transpose(B(k)[0:src.shape[1], a:b], src, I_(src.shape[0]))
                filled(ins, k)

            def project(name, n, rhs):
                for m in range(n):
                    u = unit_of[name] + m // 2
                    k = tile_of[name] + m
                    if m % 2 == 0:
                        need_unit(pe, u)
                    claim(pe, k)
                    for c in range(C):
                        w = slot(u)[:, c, P * (m % 2):P * (m % 2) + P]
                        ins = pe.matmul(B(k)[:, 0:T], w, rhs(c), start=(c == 0), stop=(c == C - 1))
                    filled(ins, k)

            def sums(k, parts, free=T):
                claim(pe, k)
                for c, p_ in enumerate(parts):
                    ins = pe.matmul(B(k)[:, 0:free], K("ones"), p_, start=(c == 0), stop=(c == len(parts) - 1))
                filled(ins, k)

            def norm(tag, k):
                after(pe, "act", f"sq{tag}")
                sums(k, [scratch[:, c, :] for c in range(C)])
                after(pe, "act", f"hp{tag}")
                if tag != "f":
                    after(pe, "dve", f"hs{tag}")

            def ada(l):
                base = tile_of[f"ada{l}"]

                def turn(q):
                    after(pe, "act", (f"row{l}", q))
                    k = base + (2 * q + 2 if q < 11 else 23)
                    transposes(k, [((NCOND * i, NCOND * i + NCOND), modrow(l)[:, q % 2, P * i:P * i + P]) for i in range(4)])

                for q in range(12):
                    k = base + (0 if q == 0 else 2 * q - 1)
                    claim(pe, k)
                    for j in range(2):
                        u = unit_of[f"ada{l}"] + 2 * q + j
                        need_unit(pe, u)
                        for c in range(C):
                            ins = pe.matmul(B(k)[0:NCOND, 256 * j:256 * j + 256], condT[:, c, :], slot(u)[:, c, :],
                                            start=(c == 0), stop=(c == C - 1))
                    filled(ins, k)
                    if q >= 1:
                        turn(q - 1)
                turn(11)

            def delta():
                k = tile_of["gcol"]
                after(pe, "dve", "g")
                claim(pe, k)
                for t, (a, n) in enumerate(TT):
                    up, af = (K("upto"), K("after")) if t < 2 else (K("upto_s", NS), K("after_s", NS))
                    pe.matmul(B(k)[0:n, 8 * t:8 * t + 4], up, gg[0:n, t, :], start=True, stop=True)
                    ins = pe.matmul(B(k)[0:n, 8 * t + 4:8 * t + 8], af, gg[0:n, t, :], start=True, stop=True)
                filled(ins, k)
                for t, (a, n) in enumerate(TT):
                    k = tile_of["grow"] + t
                    claim(pe, k)
                    up = K("upto") if t < 2 else K("upto_s", NS)
                    for h in range(H):
                        ins = pe.matmul(B(k)[:, n * h:n * h + n], gg[0:n, t, h:h + 1].to_broadcast([n, P]), up,
                                        start=True, stop=True)
                    filled(ins, k)
                for t, (a, n) in enumerate(TT):
                    k = tile_of["brow"] + t
                    claim(pe, k)
                    for h in range(H):
                        ins = pe.matmul(B(k)[:, n * h:n * h + n], beta[0:n, t, h:h + 1].to_broadcast([n, P]), I_(n),
                                        start=True, stop=True)
                    filled(ins, k)
                after(pe, "act", ("cv", 11))
                for t, (a, n) in enumerate(TT):
                    transposes(tile_of["vt"] + t, [((P * h, P * h + P), cT[:, 8 + h, a:a + n]) for h in range(H)])
                after(pe, "dve", "qk")
                for t, (a, n) in enumerate(TT):
                    transposes(tile_of["kt"] + t, [((P * h, P * h + P), cT[:, 4 + h, a:a + n]) for h in range(H)])
                after(pe, "dve", "kb2")
                for name, rhs in (("at", kb), ("qk", cT)):
                    for t, (a, n) in enumerate(TT):
                        k = tile_of[name] + t
                        claim(pe, k)
                        for h in range(H):
                            ins = pe.matmul(B(k)[0:n, n * h:n * h + n], cT[:, 4 + h, a:a + n], rhs[:, h, a:a + n],
                                            start=True, stop=True)
                        filled(ins, k)
                for t, (a, n) in enumerate(TT):
                    after(pe, "dve", ("xt", 1, t))
                    transposes(tile_of["xt0"] + t, [((n * h, n * h + n), XT[0:n, t, h, 0:n]) for h in range(H)])
                k = tile_of["lev"]

                def four(k, t, lhs, rhs):
                    n = TT[t][1]
                    claim(pe, k)
                    for h in range(H):
                        ins = pe.matmul(B(k)[0:n, n * h:n * h + n], lhs[0:n, t, h, 0:n], rhs[0:n, t, h, 0:n],
                                        start=True, stop=True)
                    filled(ins, k)

                for s, ts in LEVELS:
                    for t in ts:
                        after(pe, "dve", ("lt", s, t))
                        if s == 2:
                            after(pe, "act", f"x0inv{t}")
                        four(k, t, LT, X)
                        k += 1
                    for t in ts:
                        after(pe, "act", ("pb", s, t))
                        four(k, t, PB, XT)
                        four(k + 1, t, XT, PB)
                        k += 2
                after(pe, "dve", ("xi", 64, 1))
                for t in range(3):
                    a, n = TT[t]
                    k = tile_of[f"dl{t}"]
                    if t == 1:
                        after(pe, "dve", "s1")
                        claim(pe, k)
                        for h in range(H):
                            ins = pe.matmul(B(k)[0:n, P * h:P * h + P], cT[:, 4 + h, a:a + n], S0[:, h, :],
                                            start=True, stop=True)
                        filled(ins, k)
                        k += 1
                    elif t == 2:
                        after(pe, "dve", "ktm")
                        pe.wait_ge(ld_states, 64)
                        claim(pe, k)
                        for h in range(H):
                            for b in range(NB):
                                ins = pe.matmul(B(k)[0:n, P * h:P * h + P], kTm[:, h, b, :], states[:, b, h, :],
                                                start=(b == 0), stop=(b == NB - 1))
                        filled(ins, k)
                        k += 1
                    if t:
                        after(pe, "dve", f"r{t}")
                    claim(pe, k)
                    for h in range(H):
                        ins = pe.matmul(B(k)[0:n, P * h:P * h + P], XT[0:n, t, h, 0:n],
                                        (RR if t else vb)[0:n, t, h, :], start=True, stop=True)
                    filled(ins, k)
                    k += 1
                    after(pe, "act", f"u{t}")
                    claim(pe, k)
                    for h in range(H):
                        o = B(k)[:, n * h:n * h + n]
                        ins = pe.matmul(o, uu[0:n, t, h, :], qkg[0:n, t, h, 0:n], start=True, stop=(t != 1))
                        if t == 1:
                            ins = pe.matmul(o, S0[:, h, :], qd[:, h, a:a + n], start=False, stop=True)
                        if t == 2:
                            for b in range(NB):
                                ins = pe.matmul(o[:, LS * b:LS * b + LS], states[:, b, h, :],
                                                qd[:, h, a + LS * b:a + LS * b + LS], start=False, stop=True,
                                                skip_group_check=True)
                    filled(ins, k)
                    k += 1
                    if t < 2:
                        claim(pe, k)
                        for h in range(H):
                            ins = pe.matmul(B(k)[:, P * h:P * h + P], kd[0:n, t, h, :], uu[0:n, t, h, :],
                                            start=True, stop=True)
                        filled(ins, k)
                    else:
                        for h in range(H):
                            after(pe, "dve", ("ue", h))
                            for j in range(2):
                                k = tile_of["dstate"] + 2 * h + j
                                claim(pe, k)
                                filled(pe.matmul(B(k)[:, 0:512], kd[0:n, t, h, :],
                                                 ue[:, 4 * j:4 * j + 4, :].rearrange("p b v -> p (b v)"),
                                                 start=True, stop=True), k)

            def mixer0():
                k = tile_of["in_ab"]
                pe.wait_ge(ld_small, 16 * NSMALL)
                claim(pe, k)
                for t, (a, n) in enumerate(TT):
                    for c in range(C):
                        ins = pe.matmul(B(k)[0:n, 8 * t:8 * t + 8], hT[:, c, a:a + n], wab[:, c, :],
                                        start=(c == 0), stop=(c == C - 1))
                filled(ins, k)
                project("in", 28, lambda c: hT[:, c, :])
                after(pe, "pool", "stg")
                for i in range(3):
                    transposes(tile_of["st_out"] + i, [((P * j, P * j + P), stg[:, 27 * (4 * i + j):27 * (4 * i + j) + 27])
                                                       for j in range(4)])
                transposes(tile_of["st_out"] + 3, [((P * j, P * j + P), stgb[:, 18 * j:18 * j + 18]) for j in range(4)])
                after(pe, "act", "qksq")
                for m in range(8):
                    sums(tile_of["l2"] + m, [scratch[:, m, :]])
                delta()
                after(pe, "act", "osq")
                for h in range(H):
                    sums(tile_of["onorm"] + h, [osq[:, h, :]])
                after(pe, "dve", "cat")
                project("out0", C, lambda c: catT[:, c, :])

            def mixer1():
                project("qkv", 24, lambda c: hT[:, c, :])
                after(pe, "act", ("qkv", 23))
                for name, m0 in (("ktok", 8), ("vtok", 16)):
                    for i in range(6):
                        a, n = TT[i // 2]
                        transposes(tile_of[name] + i, [((P * j, P * j + P), qkvT[:, m0 + 4 * (i % 2) + j, a:a + n])
                                                       for j in range(4)])
                for st in range(18):
                    if st < 16:
                        c, r = st // 2, slice(64 * (st % 2), 64 * (st % 2) + 64)
                        kk = attp[("S", st)]
                        claim(pe, kk)
                        pe.matmul(B(kk)[:, 0:128], qkvT[r, c, 0:128], qkvT[r, 8 + c, 0:128], start=True, stop=True)
                        filled(pe.matmul(B(kk)[:, 128:384], qkvT[r, c, 128:256], qkvT[r, 8 + c, 0:256],
                                         start=True, stop=True), kk)
                    if 1 <= st <= 16:
                        h = st - 1
                        after(pe, "dve", ("apr", h))
                        transposes(attp[("T", h)], [((P * j, P * j + P), prb[:, h % 2, P * j:P * j + P]) for j in range(3)])
                    if st >= 2:
                        h = st - 2
                        kk = attp[("O", h // 2)]
                        if h == 0:
                            after(pe, "dve", ("vt", 5))
                        if h % 2 == 0:
                            claim(pe, kk)
                        after(pe, "act", ("apT", h))
                        r = slice(64 * (h % 2), 64 * (h % 2) + 64)
                        v = slice(64 * h, 64 * h + 64)
                        pe.matmul(B(kk)[r, 0:128], vtok[:, 0, v], pT[:, h % 2, 0:128], start=True, stop=True)
                        pe.matmul(B(kk)[r, 128:256], vtok[:, 0, v], pT[:, h % 2, 128:256], start=True, stop=False)
                        ins = pe.matmul(B(kk)[r, 128:256], vtok[:, 1, v], pT[:, h % 2, 256:384], start=False, stop=True)
                        if h % 2 == 1:
                            filled(ins, kk)
                for b in range(NB + 1):
                    u = b % 2
                    if b < NB:
                        pe.wait_ge(ld_kc[u], 16 * (b // 2 + 1))
                        for i in range(4):
                            transposes(atts["K", b, i], [((256 * j + P * a_, 256 * j + P * a_ + P),
                                                 Kc[:, u, a_, P * (2 * i + j):P * (2 * i + j) + P])
                                                for j in range(2) for a_ in range(2)])
                    if b:
                        after(pe, "dve", ("spr", b - 1))
                        transposes_s(atts[("T", b - 1)], (b - 1) % 2)
                    if b < NB:
                        kk = atts[("S", b)]
                        after(pe, "act", ("kt", b, 1))
                        after(pe, "dve", ("kt", b, 3))
                        after(pe, "pool", ("qbd", b))
                        claim(pe, kk)
                        for c in range(C):
                            pe.matmul(B(kk)[:, 0:256], qbd[:, u, P * c:P * c + P], KT[:, c, :],
                                      start=(c == 0), stop=(c == C - 1))
                        for c in range(C):
                            ins = pe.matmul(B(kk)[:, 256:320], qbd[:, u, P * c:P * c + P], qkvT[:, 8 + c, NP_:T],
                                            start=(c == 0), stop=(c == C - 1))
                        filled(ins, kk)
                    if b:
                        w = (b - 1) % 2
                        kk = atts[("O", b - 1)]
                        after(pe, "act", ("spT", b - 1))
                        pe.wait_ge(ld_vc[w], 16 * ((b - 1) // 2 + 1))
                        claim(pe, kk)
                        for c in range(C):
                            o = B(kk)[:, 16 * c:16 * c + 16]
                            q = slice(16 * c, 16 * c + 16)
                            for a_ in range(2):
                                pe.matmul(o, Vc[:, w, a_, P * c:P * c + P], pT[:, w, P * a_:P * a_ + P][:, q],
                                          start=(a_ == 0), stop=False)
                            ins = pe.matmul(o, vtok[0:NS, 2, P * c:P * c + P], pT[0:NS, w, 256:384][:, q],
                                            start=False, stop=True)
                        filled(ins, kk)
                after(pe, "act", ("aout", 7))
                after(pe, "dve", ("sout", NB - 1))
                project("out1", C, lambda c: attnT[:, c, :])

            def transposes_s(k, u):
                claim(pe, k)
                for j in range(2):
                    pe.transpose(B(k)[:, P * j:P * j + P], prb[:, u, P * j:P * j + P], I_(P))
                filled(pe.transpose(B(k)[0:NS, 256:384], prb[:, u, 256:320], I_(P)), k)

            def router(l):
                k = tile_of[f"rt{l}"]
                claim(pe, k)
                for t, (a, n) in enumerate(TT):
                    for c in range(C):
                        ins = pe.matmul(B(k)[0:n, 36 * t:36 * t + 36], hT[:, c, a:a + n], wr[:, l, c, :],
                                        start=(c == 0), stop=(c == C - 1))
                filled(ins, k)
                for i in range(6):
                    a, n = TT[i // 2]
                    transposes(tile_of[f"ht{l}"] + i, [((P * j, P * j + P), hT[:, 4 * (i % 2) + j, a:a + n])
                                                       for j in range(4)])
                k = tile_of[f"rk{l}"]
                after(pe, "dve", f"oh{l}")
                claim(pe, k)
                for t, (a, n) in enumerate(TT):
                    for t2 in range(t + 1):
                        n2 = TT[t2][1]
                        m = K("ones", n2)[:, 0:n] if t2 < t else K("upto", n)[:, 0:n]
                        pe.matmul(B(k)[0:n, 4 * t:4 * t + 4], m, onehot[0:n2, t2, :], start=(t2 == 0), stop=(t2 == t))
                for t, (a, n) in enumerate(TT):
                    ins = pe.matmul(B(k)[:, 16:20], K("ones", n), onehot[0:n, t, :], start=(t == 0), stop=(t == 2))
                filled(ins, k)

            def expert_pass(S, i, units_at, unit_wait):
                pe.wait_ge(S["perm"], i + 1)
                for a in range(12):
                    n = 12 * i + a
                    bk = bank[5 + a % 2]
                    if n >= 2:
                        pe.wait_ge(S["auxfree"], n - 1)
                    if a < 4:
                        for t, (x, m) in enumerate(TT):
                            ins = pe.transpose(bk[:, x:x + m], perm[0:m, t, a, :], I_(m))
                    else:
                        for t, (x, m) in enumerate(TT):
                            ins = pe.matmul(bk[:, :], htok[0:m, t, P * (a - 4):P * (a - 4) + P],
                                            perm[0:m, t, :, :].rearrange("p g s -> p (g s)"),
                                            start=(t == 0), stop=(t == 2))
                    ins.then_inc(S["aux"], 1)
                for g in range(NG):
                    for t, (x, m) in enumerate(TT):
                        ins = pe.matmul(bank[7][:, NE * g:NE * g + NE], perm[0:m, t, g, :],
                                        gates[0:m, t, NE * g:NE * g + NE], start=(t == 0), stop=(t == 2))
                ins.then_inc(S["gsl"], 1)
                pe.wait_ge(S["auxfree"], 12 * i + 12)

                for g in range(NG):
                    with pe.Fori(0, 2) as j:
                        def gate_up(u, w):
                            k0 = 32 * i + 8 * g + u
                            if w == 0:
                                pe.wait_ge(S["hid"], 4 * j + (k0 + 1))
                            unit_wait(g, u, w, j)
                            wt = units_at(g, u, w)
                            for c in range(C):
                                ins = pe.matmul(bank[u % 2 + 5 * w][:, 0:256], hg[:, c, P * g:P * g + P],
                                                wt[:, c, :], start=(c == 0), stop=(c == C - 1))
                            ins.then_inc(S["gu"], 1)

                        def turn(u):
                            pe.wait_ge(S["hid"], 4 * j + (32 * i + 8 * g + u + 3))
                            for f in range(2):
                                ins = pe.transpose(bank[2][:, 256 * (u % 2) + P * f:256 * (u % 2) + P * f + P],
                                                   hid[:, u % 2, P * f:P * f + P], I_(P))
                            ins.then_inc(S["tr"], 1)

                        def down(u):
                            if u == 0:
                                pe.wait_ge(S["yadd"], j + (8 * i + 2 * g + 1))
                            pe.wait_ge(S["hidT"], 4 * j + (32 * i + 8 * g + u + 1))
                            unit_wait(g, u, 2, j)
                            wt = units_at(g, u, 2)
                            for d in range(2):
                                for f in range(2):
                                    ins = pe.matmul(bank[3 + d][:, :], hidT[:, u % 2, f, :], wt[:, f, 512 * d:512 * d + 512],
                                                    start=(u == 0 and f == 0), stop=(u == 3 and f == 1))
                            ins.then_inc(S["down"], 1)

                        gate_up(0, 0)
                        gate_up(0, 1)
                        for u in range(1, 4):
                            gate_up(u, 0)
                            turn(u - 1)
                            gate_up(u, 1)
                            down(u - 1)
                        turn(3)
                        down(3)
                pe.wait_ge(S["yadd"], 8 * i + 9)
                for m in range(C):
                    n = 8 * i + m
                    if m >= 2 or i:
                        pe.wait_ge(S["scfree"], n - 1)
                    for g in range(NG):
                        ins = pe.matmul(bank[5 + m % 2][:, 0:T], ys[:, g, P * m:P * m + P], permT[:, g, :],
                                        start=(g == 0), stop=(g == NG - 1))
                    ins.then_inc(S["sc"], 1)

            def experts(l):
                k = tile_of[f"rk{l}"] + 1
                for b in range(NBANK):
                    claim(pe, k + b)
                base = unit_of[f"moe{l}"]

                def at_(g, u, w):
                    return slot(base + 24 * g + 3 * u + w, D if w == 2 else 256)

                def wait(g, u, w, j):
                    n = base + 24 * g + 3 * u + w
                    pe.wait_ge(unit_loaded[n % R], 16 * (12 // R) * j + 16 * (n // R + 1))

                expert_pass(moe, l, at_, wait)
                S = more[l]
                after(pe, "dve", f"flag{l}")
                v = pe.value_load(flag[:, :], min_val=0, max_val=1)
                with pe.If(v >= 1):
                    for i in range(2):
                        def at2(g, u, w):
                            return ring2[:, w, :].rearrange("p (c n) -> p c n", n=D if w == 2 else 256)

                        def wait2(g, u, w, j, i=i):
                            pe.wait_ge(S[f"wl{w}"], 64 * j + 16 * (32 * i + 8 * g + u + 1))

                        expert_pass(S, i, at2, wait2)
                after(pe, "dve", f"x{l}2")

            pe.wait_ge(ld_const, 16)
            pe.wait_ge(ld_rows, 16 * NROWS)
            k = tile_of["cols"]
            transposes(k, [((26 * c, 26 * c + 26), rowsM0[:, P * c:P * c + P]) for c in range(C)])
            transposes(k + 1, [((28 * m, 28 * m + 28), rowsA0[:, P * m:P * m + P]) for m in range(12)])
            transposes(k + 2, [((19 * m, 19 * m + 19), rowsB0[:, P * m:P * m + P]) for m in range(4)])
            pe.wait_ge(ld_x, 48)
            for c in range(C):
                transposes(tile_of["x"] + c, [((a, a + n), xload[0:n, t, P * c:P * c + P]) for t, (a, n) in enumerate(TT)])
            after(pe, "act", "cond")
            for l in range(2):
                ada(l)
                norm(f"{l}1", tile_of[f"norm{l}1"])
                if l == 0:
                    mixer0()
                else:
                    mixer1()
                norm(f"{l}2", tile_of[f"norm{l}2"])
                router(l)
                experts(l)
            norm("f", tile_of["normf"])
            for i in range(6):
                a, n = TT[i // 2]
                transposes(tile_of["y"] + i, [((P * j, P * j + P), hT[:, 4 * (i % 2) + j, a:a + n]) for j in range(4)])
        def samples(ap):
            return ap.rearrange("p (b t) -> p b t", b=NB)

        def sequences(flat):
            return flat[:, EP:EW].rearrange("p (b e) -> p b e", b=NB)[:, :, 0:LS]

        @block.scalar
        def _(act):
            steps = [0]

            def link(ins):
                steps[0] += 1
                ins.then_inc(astep, 1)
                act.wait_ge(astep, steps[0])

            act.dma_start(const[:, :], I["masks"]).then_inc(ld_const, 16)
            for t, (a, n) in enumerate(TT):
                src = I["x_prompt"][0, a:a + n] if t < 2 else I["x_sample"].rearrange("b t d -> (b t) d")
                act.dma_start(xload[0:n, t, :], src).then_inc(ld_x, 16)
            for dst, src in ((rowsM0[0:2], I["norm1"]), (rowsM0[2:4], I["norm2"]),
                             (rowsM0[4:5], I["norm_f"].rearrange("(a d) -> a d", a=1)),
                             (rowsM0[5:17], I["b_ada"].rearrange("l (j d) -> (l j) d", d=D)),
                             (rowsM0[17:18], I["c_prompt"]), (rowsM0[18:26], I["c_sample"]),
                             (rowsA0[0:24], I["state_a_conv"][0].rearrange("b j n -> (b j) n")),
                             (rowsA0[24:28], I["conv_a_w"][0]),
                             (rowsB0[0:16], I["state_b_conv"][0].rearrange("b j n -> (b j) n")),
                             (rowsB0[16:19], I["conv_b_w"][0])):
                act.dma_start(dst, src).then_inc(ld_rows, 16)
            with nc.allow_non_contiguous_dma(reason="a column of 128 gains"):
                act.dma_start(colsO[:, :], I["o_gain_a"].rearrange("a p -> p a")).then_inc(ld_small, 16)
            act.dma_start(wab[:, :, :], I["w_in_even"][0].rearrange("(c p) n -> p c n", p=P)[:, :, 2048:2056])\
               .then_inc(ld_small, 16)
            act.dma_start(dtb[:, 0, :], I["dt_bias"][0:1].to_broadcast([P, 4])).then_inc(ld_small, 16)
            act.dma_start(dtb[:, 1, :], I["a_log"][0:1].to_broadcast([P, 4])).then_inc(ld_small, 16)
            for l in range(2):
                act.dma_start(wr[:, l, :, 0:4], I["w_router_group"][l].rearrange("(c p) n -> p c n", p=P))\
                   .then_inc(ld_small, 16)
                act.dma_start(wr[:, l, :, 4:36], I["w_router_expert"][l].rearrange("(c p) n -> p c n", p=P))\
                   .then_inc(ld_small, 16)
                act.dma_start(br[:, l, 0:4], I["b_router_group"][l:l + 1].to_broadcast([P, 4])).then_inc(ld_small, 16)
                act.dma_start(br[:, l, 4:36], I["b_router_expert"][l:l + 1].to_broadcast([P, 32])).then_inc(ld_small, 16)

            def copy(dst, src):
                return act.activation(dst, src, ACT.Copy)

            def norm(tag, k):
                if tag[1:] == "2":
                    after(act, "pool", f"mixer{tag[0]}")
                after(act, "dve", {"01": "x0", "02": ("xo0", 7), "11": "x02", "12": ("xo1", 7), "f": "x12"}[tag])
                result("act", f"sq{tag}", act.activation(scratch[:, :, :], xT[:, :, :], ACT.Square))
                full(act, k)
                result("act", f"std{tag}", act.activation(rstd[:, :], B(k)[:, 0:T], ACT.Sqrt, scale=1.0 / D,
                                                          bias=K("eps")))
                after(act, "dve", f"xn{tag}")
                for c in range(C):
                    if tag == "f":
                        ins = act.activation(hT[:, c, :], scratch[:, c, :], ACT.Copy, scale=cols[:, c, 4:5])
                    else:
                        j = 0 if tag[1] == "1" else 3
                        ins = act.activation(hT[:, c, 0:NP_], scratch[:, c, 0:NP_], ACT.Identity,
                                             scale=gainA[:, c, 0:1], bias=mod[:, j, c, 0:1])
                result("act", f"hp{tag}", ins)

            def mixer0():
                exts = ext[:, :, EP:EW].rearrange("p m (b e) -> p m b e", b=NB)
                after(act, "pool", "hist")
                acc = convacc[:, 0:2 * EW].rearrange("p (u e) -> p u e", u=2)
                for m in range(24):
                    k = tile_of["in"] + m
                    full(act, k)
                    ps = B(k)
                    if m < 12:
                        copy(ext[:, m, HIST:EP], ps[:, 0:NP_])
                        result("act", ("ext", m), copy(exts[:, m, :, HIST:], samples(ps[:, NP_:T])))
                    elif m < 16:
                        result("act", ("z", m), act.activation(zT[:, m - 12, :], ps[:, 0:T], ACT.Silu))
                    else:
                        dst = bg[:, m - 16, :] if m < 20 else cg[:, m - 20, :]
                        result("act", ("gt", m), copy(dst, ps[:, 0:T]))
                    if 2 <= m < 14:
                        v = m - 2
                        after(act, "dve", ("conv", v))
                        s = acc[:, v % 2, :]
                        act.activation(cT[:, v, 0:NP_], s[:, 0:NP_], ACT.Silu)
                        ins = act.activation(samples(cT[:, v, NP_:T]), sequences(s), ACT.Silu)
                        result("act", ("cv", v), ins)
                after(act, "dve", "g_abs")
                link(act.activation(sc8[:, :, 4:8], sc8[:, :, 0:4], ACT.Exp, scale=-1.0))
                link(act.activation(sc8[:, :, 4:8], sc8[:, :, 4:8], ACT.Ln, bias=K("one")))
                result("act", "g_ea", act.activation(dtb[:, 1, :], dtb[:, 1, :], ACT.Exp))
                result("act", "g_eb", act.activation(sc8[:, :, 8:12], gab[:, :, 4:8], ACT.Exp, scale=-1.0))
                after(act, "act", ("cv", 11))
                result("act", "qksq", act.activation(scratch[:, :, :], cT[:, 0:8, :], ACT.Square))
                for i in range(4):
                    k = tile_of["st_out"] + i
                    full(act, k)
                    n = 27 if i < 3 else 18
                    result("act", ("so", i), copy(stout[0:n, 512 * i:512 * i + 512], B(k)[0:n, :]))
                for m in range(8):
                    k = tile_of["l2"] + m
                    full(act, k)
                    result("act", ("l2s", m), act.activation(l2std[:, m, :], B(k)[:, 0:T], ACT.Sqrt, bias=K("eps")))
                for t, (a, n) in enumerate(TT):
                    k = tile_of["grow"] + t
                    full(act, k)
                    result("act", f"eG{t}", act.activation(eG[:, :, a:a + n],
                                                           B(k)[:, 0:H * n].rearrange("p (h i) -> p h i", h=H), ACT.Exp))
                after(act, "dve", "gcol")
                result("act", "egc", act.activation(egc[:, :, :], gcols[:, :, :], ACT.Exp))
                after(act, "dve", "gd2")
                act.activation(gam[:, 0:2, :, :], gam[:, 0:2, :, :], ACT.Exp)
                result("act", "ge", act.activation(gam[0:NS, 2, :, 0:NS], gam[0:NS, 2, :, 0:NS], ACT.Exp))
                for t, (a, n) in enumerate(TT):
                    k = tile_of["xt0"] + t
                    full(act, k)
                    result("act", f"x0inv{t}", copy(X[0:n, t, :, 0:n], B(k)[0:n, 0:H * n].rearrange("p (h i) -> p h i", h=H)))
                k = tile_of["lev"]
                for s, ts in LEVELS:
                    for t in ts:
                        n = TT[t][1]
                        full(act, k)
                        result("act", ("pb", s, t), copy(PB[0:n, t, :, 0:n],
                                                         B(k)[0:n, 0:H * n].rearrange("p (h i) -> p h i", h=H)))
                        k += 1
                    k += 2 * len(ts)
                for t, (a, n) in enumerate(TT):
                    k = tile_of[f"dl{t}"] + (1 if t else 0)
                    full(act, k)
                    result("act", f"u{t}", copy(uu[0:n, t, :, :], B(k)[0:n, :].rearrange("p (h v) -> p h v", h=H)))
                after(act, "dve", "o2")
                result("act", "osq", act.activation(osq, oT, ACT.Square))
                for h in range(H):
                    k = tile_of["onorm"] + h
                    full(act, k)
                    result("act", ("os", h), act.activation(ostd[:, h, :], B(k)[:, 0:T], ACT.Sqrt, scale=1.0 / P,
                                                            bias=K("eps")))

            def mixer1():
                for m in range(24):
                    k = tile_of["qkv"] + m
                    full(act, k)
                    result("act", ("qkv", m), copy(qkvT[:, m, :], B(k)[:, 0:T]))
                for i in range(6):
                    k = tile_of["ktok"] + i
                    n = TT[i // 2][1]
                    full(act, k)
                    if i == 4:
                        act.wait_ge(ktok_sent, 16)
                    result("act", ("ktok", i), copy(ktok[0:n, i // 2 % 2, 512 * (i % 2):512 * (i % 2) + 512], B(k)[0:n, :]))
                for st in range(18):
                    if st < 16:
                        h, u = st, st % 2
                        after(act, "dve", ("amax", h))
                        act.activation(prb[:, u, 0:128], scr[:, u, 0:128], ACT.Exp, bias=stat[:, u, 2:3], scale=0.125)
                        result("act", ("aexp", h), act.activation(prb[:, u, 128:384], scr[:, u, 128:384], ACT.Exp,
                                                                  bias=stat[:, u, 3:4], scale=0.125))
                    if 1 <= st <= 16:
                        h = st - 1
                        k = attp["T", h]
                        full(act, k)
                        result("act", ("apT", h), copy(pT[:, h % 2, :], B(k)[:, 0:384]))
                    if st >= 2 and st % 2 == 1:
                        o = st // 2 - 1
                        k = attp["O", o]
                        full(act, k)
                        result("act", ("aout", o), copy(attnT[:, o, 0:NP_], B(k)[:, 0:NP_]))
                for b in range(NB + 1):
                    if b < NB:
                        for i in range(2):
                            k = atts["K", b, i]
                            full(act, k)
                            result("act", ("kt", b, i), copy(KT[:, 2 * i:2 * i + 2, :],
                                                             B(k)[:, :].rearrange("p (c j) -> p c j", c=2)))
                    if b:
                        k = atts["T", b - 1]
                        u = (b - 1) % 2
                        full(act, k)
                        copy(pT[:, u, 0:256], B(k)[:, 0:256])
                        result("act", ("spT", b - 1), copy(pT[0:NS, u, 256:384], B(k)[0:NS, 256:384]))
                    if b < NB:
                        u = b % 2
                        after(act, "dve", ("smax", b))
                        result("act", ("sexp", b), act.activation(prb[:, u, 0:T], scr[:, u, 0:T], ACT.Exp,
                                                                  bias=stat[:, u, 2:3], scale=0.125))

            def expert_pass(S, i):
                for a in range(12):
                    act.wait_ge(S["aux"], 12 * i + a + 1)
                    src = bank[5 + a % 2]
                    if a < 4:
                        ins = copy(permT[:, a, :], src[:, 0:T])
                    else:
                        ins = copy(hg[:, a - 4, :], src[:, :])
                    ins.then_inc(S["auxfree"], 1)
                for g in range(NG):
                    with act.Fori(0, 2) as j:
                        def silu(u):
                            act.wait_ge(S["gu"], 8 * j + (2 * (32 * i + 8 * g + u) + 1))
                            act.activation(sg[:, u % 2, :], bank[u % 2][:, 0:256], ACT.Silu).then_inc(S["silu"], 1)

                        def turn(u):
                            act.wait_ge(S["tr"], 4 * j + (32 * i + 8 * g + u + 1))
                            copy(hidT[:, u % 2, :, :].rearrange("p f s -> p (f s)"),
                                 bank[2][:, 256 * (u % 2):256 * (u % 2) + 256]).then_inc(S["hidT"], 1)

                        silu(0)
                        for u in range(1, 4):
                            silu(u)
                            turn(u - 1)
                        turn(3)

            def experts(l):
                for i in range(6):
                    k = tile_of[f"ht{l}"] + i
                    n = TT[i // 2][1]
                    full(act, k)
                    result("act", (f"ht{l}", i), copy(htok[0:n, i // 2, 512 * (i % 2):512 * (i % 2) + 512], B(k)[0:n, :]))
                after(act, "dve", f"rm{l}")
                result("act", f"re{l}", act.activation(rt[:, 60:72], rt[:, 48:60], ACT.Exp))
                after(act, "dve", f"rt2{l}")
                result("act", f"re2{l}", act.activation(rt[:, 303:306], rt[:, 300:303], ACT.Exp))
                expert_pass(moe, l)
                after(act, "dve", f"flag{l}")
                v = act.value_load(flag[:, :], min_val=0, max_val=1)
                with act.If(v >= 1):
                    for i in range(2):
                        expert_pass(more[l], i)

            after(act, "dve", "cols")
            result("act", "cond", act.activation(condT[:, :, :], cols[:, :, 17:26], ACT.Silu))
            for l in range(2):
                for q in range(12):
                    k = tile_of[f"ada{l}"] + (0 if q == 0 else 2 * q - 1)
                    full(act, k)
                    result("act", (f"row{l}", q), copy(modrow(l)[:, q % 2, :], B(k)[0:NCOND, :]))
                norm(f"{l}1", tile_of[f"norm{l}1"])
                (mixer0 if l == 0 else mixer1)()
                norm(f"{l}2", tile_of[f"norm{l}2"])
                experts(l)
            norm("f", tile_of["normf"])
            for i in range(6):
                k = tile_of["y"] + i
                n = TT[i // 2][1]
                full(act, k)
                result("act", ("yt", i), copy(ytok[0:n, i // 2, 512 * (i % 2):512 * (i % 2) + 512], B(k)[0:n, :]))

        @block.vector
        def _(dve):
            steps = [0]

            def link(ins):
                steps[0] += 1
                ins.then_inc(vstep, 1)
                dve.wait_ge(vstep, steps[0])

            def mul(out, a, b):
                return dve.tensor_tensor(out, a, b, ALU.mult)

            def add(out, a, b):
                return dve.tensor_tensor(out, a, b, ALU.add)

            def stt(out, a, s, b, op0, op1, **kw):
                return dve.scalar_tensor_tensor(out, a, s, b, op0, op1, **kw)

            def b3(ap, n):
                return ap.unsqueeze(len(ap.shape)).to_broadcast(list(ap.shape) + [n])

            def mid(ap, n):
                s = list(ap.shape)
                return ap.unsqueeze(2).to_broadcast([s[0], s[1], n, s[2]])

            def norm(tag, k):
                if tag != "f":
                    l, half = int(tag[0]), int(tag[1])
                    j = 0 if half == 1 else 3
                    gi = l if half == 1 else 2 + l
                    stt(gainA[:, :, :], mod[:, j + 1, :, :], 1.0, cols[:, :, gi:gi + 1].to_broadcast([P, C, NCOND]),
                        ALU.add, ALU.mult)
                after(dve, "act", f"std{tag}")
                link(dve.reciprocal(rstd[:, :], rstd[:, :]))
                result("dve", f"xn{tag}", mul(scratch[:, :, :], xT[:, :, :],
                                              rstd[:, :].unsqueeze(1).to_broadcast([P, C, T])))
                if tag == "f":
                    return
                after(dve, "dve", f"xn{tag}")
                for c in range(C):
                    ins = mul(samples(hT[:, c, NP_:T]), samples(scratch[:, c, NP_:T]), b3(gainA[:, c, 1:NCOND], LS))
                link(ins)
                for c in range(C):
                    ins = add(samples(hT[:, c, NP_:T]), samples(hT[:, c, NP_:T]), b3(mod[:, j, c, 1:NCOND], LS))
                result("dve", f"hs{tag}", ins)

            def residual(m, ps, gate):
                stt(xT[:, m, 0:NP_], ps[:, 0:NP_], mod[:, gate, m, 0:1], xT[:, m, 0:NP_], ALU.mult, ALU.add)
                tmp = rstd[:, NS * (m % 4):NS * (m % 4) + NS]
                return tmp, mul(samples(tmp), samples(ps[:, NP_:T]), b3(mod[:, gate, m, 1:NCOND], LS))

            def mixer0():
                k = tile_of["in_ab"]
                link(dve.memset(gab[:, :, :], 0.0))
                dve.wait_ge(ld_small, 16 * NSMALL)
                full(dve, k)
                dve.tensor_copy(gab[:, 0:2, :], B(k)[:, 0:16].rearrange("p (t n) -> p t n", t=2))
                result("dve", "gab", dve.tensor_copy(gab[0:NS, 2, :], B(k)[0:NS, 16:24]))
                after(dve, "dve", "gab")
                link(add(sc8[:, :, 12:16], gab[:, :, 0:4], dtb[:, 0:1, :].to_broadcast([P, 3, 4])))
                link(dve.tensor_scalar(sc8[:, :, 8:12], sc8[:, :, 12:16], -1.0, None, ALU.mult))
                result("dve", "g_abs", dve.tensor_tensor(sc8[:, :, 0:4], sc8[:, :, 12:16], sc8[:, :, 8:12], ALU.max))
                result("dve", "g_e", dve.tensor_scalar(gg[:, :, :], sc8[:, :, 12:16], 0.0, None, ALU.max))
                after(dve, "pool", "hist")
                acc = convacc[:, 0:2 * EW].rearrange("p (u e) -> p u e", u=2)
                for m in range(12):
                    after(dve, "act", ("ext", m))
                    if m >= 2:
                        after(dve, "act", ("cv", m - 2))
                    o = acc[:, m % 2, :]
                    link(dve.tensor_scalar(o[:, 0:CW], ext[:, m, 0:CW], colsA[:, m, 24:25], None, ALU.mult))
                    for j in range(1, 4):
                        ins = stt(o[:, 0:CW], ext[:, m, j:j + CW], colsA[:, m, 24 + j:25 + j], o[:, 0:CW], ALU.mult, ALU.add)
                        if j < 3:
                            link(ins)
                    result("dve", ("conv", m), ins)
                after(dve, "act", "g_eb")
                link(add(gg[:, :, :], gg[:, :, :], sc8[:, :, 4:8]))
                link(dve.tensor_scalar(sc8[:, :, 8:12], sc8[:, :, 8:12], 1.0, None, ALU.add))
                dve.reciprocal(beta[:, :, :], sc8[:, :, 8:12])
                result("dve", "g", stt(gg[:, :, :], gg[:, :, :], -1.0, dtb[:, 1:2, :].to_broadcast([P, 3, 4]),
                                       ALU.mult, ALU.mult))
                bxs = bx[:, :, EP:EW].rearrange("p m (b e) -> p m b e", b=NB)
                after(dve, "act", ("gt", 23))
                for m in range(4):
                    k = tile_of["in"] + 24 + m
                    full(dve, k)
                    mul(bx[:, m, HIST:EP], B(k)[:, 0:NP_], cg[:, m, 0:NP_])
                    result("dve", ("bx", m), mul(bxs[:, m, :, HIST:], samples(B(k)[:, NP_:T]), samples(cg[:, m, NP_:T])))
                after(dve, "dve", ("bx", 3))
                for m in range(4):
                    o = bconv[:, m % 2, :]
                    link(dve.tensor_scalar(o[:, 0:CW], bx[:, m, 1:1 + CW], colsB[:, m, 16:17], None, ALU.mult))
                    for j in range(1, 3):
                        link(stt(o[:, 0:CW], bx[:, m, 1 + j:1 + j + CW], colsB[:, m, 16 + j:17 + j], o[:, 0:CW],
                                 ALU.mult, ALU.add))
                    mul(catT[:, 4 + m, 0:NP_], o[:, 0:NP_], bg[:, m, 0:NP_])
                    ins = mul(samples(catT[:, 4 + m, NP_:T]), sequences(o), samples(bg[:, m, NP_:T]))
                result("dve", "catb", ins)
                after(dve, "act", ("l2s", 7))
                link(dve.reciprocal(l2std[:, :, :], l2std[:, :, :]))
                stt(cT[:, 0:4, :], cT[:, 0:4, :], float(P) ** -0.5, l2std[:, 0:4, :], ALU.mult, ALU.mult)
                result("dve", "qk", mul(cT[:, 4:8, :], cT[:, 4:8, :], l2std[:, 4:8, :]))
                k = tile_of["gcol"]
                link(dve.memset(gcols[:, :, :], 0.0))
                full(dve, k)
                dve.tensor_copy(gcols[:, 0:2, :], B(k)[:, 0:16].rearrange("p (t n) -> p t n", t=2))
                result("dve", "gcol", dve.tensor_copy(gcols[0:NS, 2, :], B(k)[0:NS, 16:24]))
                after(dve, "dve", "gcol")
                for t, (a, n) in enumerate(TT):
                    k = tile_of["grow"] + t
                    full(dve, k)
                    after(dve, "act", f"eG{t}")
                    for h in range(H):
                        ins = dve.tensor_scalar(gam[0:n, t, h, 0:n], B(k)[0:n, n * h:n * h + n], gcols[0:n, t, h:h + 1],
                                                0.0, ALU.subtract, ALU.min)
                    result("dve", f"gd{t}", ins)
                after(dve, "act", "ge")
                for t, (a, n) in enumerate(TT):
                    m_ = K("upto") if t < 2 else K("upto_s", NS)
                    ins = mul(gam[0:n, t, :, 0:n], gam[0:n, t, :, 0:n], m_.unsqueeze(1).to_broadcast([n, H, n]))
                result("dve", "gam", ins)
                after(dve, "dve", "qk")
                for t, (a, n) in enumerate(TT):
                    k = tile_of["brow"] + t
                    full(dve, k)
                    result("dve", f"kb{t}", mul(kb[:, :, a:a + n], cT[:, 4:8, a:a + n],
                                                B(k)[:, 0:H * n].rearrange("p (h i) -> p h i", h=H)))
                for t, (a, n) in enumerate(TT):
                    k = tile_of["vt"] + t
                    full(dve, k)
                    result("dve", f"vb{t}", mul(vb[0:n, t, :, :], B(k)[0:n, :].rearrange("p (h v) -> p h v", h=H),
                                                b3(beta[0:n, t, :], P)))
                after(dve, "act", "egc")
                link(stt(nbe[:, :, :], egc[:, :, 0:4], -1.0, beta[:, :, :], ALU.mult, ALU.mult))
                for t, (a, n) in enumerate(TT):
                    k = tile_of["kt"] + t
                    full(dve, k)
                    result("dve", f"kd{t}", mul(kd[0:n, t, :, :], B(k)[0:n, :].rearrange("p (h v) -> p h v", h=H),
                                                b3(egc[0:n, t, 4:8], P)))
                after(dve, "dve", "gam")

                def system(k, n):
                    return B(k)[0:n, 0:H * n].rearrange("p (h i) -> p h i", h=H)

                def level(s, n):
                    return K(f"lev{s}", n)[:, 0:n].unsqueeze(1).to_broadcast([n, H, n])

                for t, (a, n) in enumerate(TT):
                    k = tile_of["at"] + t
                    full(dve, k)
                    result("dve", f"at{t}", mul(AT[0:n, t, :, 0:n], system(k, n), gam[0:n, t, :, 0:n]))
                after(dve, "dve", "at2")
                for t, (a, n) in enumerate(TT):
                    link(mul(XT[0:n, t, :, 0:n], AT[0:n, t, :, 0:n], level(1, n)))
                    result("dve", ("xt", 1, t), dve.tensor_tensor(
                        XT[0:n, t, :, 0:n], K("ident", n)[:, 0:n].unsqueeze(1).to_broadcast([n, H, n]),
                        XT[0:n, t, :, 0:n], ALU.subtract))
                for t, (a, n) in enumerate(TT):
                    k = tile_of["qk"] + t
                    full(dve, k)
                    result("dve", f"qkg{t}", mul(qkg[0:n, t, :, 0:n], system(k, n), gam[0:n, t, :, 0:n]))
                result("dve", "qd", mul(qd, cT[:, 0:4, :], eG))
                dve.wait_ge(sent, 16 * 4)
                k = tile_of["lev"]
                for s, ts in LEVELS:
                    for t in ts:
                        n = TT[t][1]
                        result("dve", ("lt", s, t), mul(LT[0:n, t, :, 0:n], AT[0:n, t, :, 0:n], level(s, n)))
                    if s == 2:
                        for t in range(3):
                            after(dve, "act", f"x0inv{t}")
                    for q, t in enumerate(ts):
                        n = TT[t][1]
                        k1 = k + len(ts) + 2 * q
                        full(dve, k1)
                        full(dve, k1 + 1)
                        result("dve", ("xt", s, t), dve.tensor_tensor(XT[0:n, t, :, 0:n], XT[0:n, t, :, 0:n],
                                                                      system(k1, n), ALU.subtract))
                        result("dve", ("xi", s, t), dve.tensor_tensor(X[0:n, t, :, 0:n], X[0:n, t, :, 0:n],
                                                                      system(k1 + 1, n), ALU.subtract))
                        after(dve, "dve", ("xi", s, t))
                    k += 3 * len(ts)
                link(dve.memset(kTm, 0.0))
                for h in range(H):
                    own = arena[:, AT_AT + NB * NS * h:AT_AT + NB * NS * h + NB * (NS + LS)]
                    ins = dve.tensor_copy(own.rearrange("p (b w) -> p b w", b=NB)[:, :, 0:LS], samples(cT[:, 4 + h, NP_:T]))
                result("dve", "ktm", ins)

                def heads(ap):
                    return ap.rearrange("p (h v) -> p h v", h=H)

                for t, (a, n) in enumerate(TT):
                    k = tile_of[f"dl{t}"]
                    if t:
                        full(dve, k)
                        for h in range(H):
                            ins = stt(RR[0:n, t, h, :], B(k)[0:n, P * h:P * h + P], nbe[0:n, t, h:h + 1],
                                      vb[0:n, t, h, :], ALU.mult, ALU.add)
                        result("dve", f"r{t}", ins)
                        k += 1
                    full(dve, k + 1)
                    result("dve", f"o{t}", dve.tensor_copy(oT[:, :, a:a + n],
                                                           B(k + 1)[:, 0:H * n].rearrange("p (h i) -> p h i", h=H)))
                    if t == 0:
                        full(dve, k + 2)
                        result("dve", "s1", dve.tensor_copy(S0, heads(B(k + 2)[:, :])))
                        after(dve, "dve", "s1")
                    if t == 1:
                        full(dve, k + 2)
                        for h in range(H):
                            ins = stt(S0[:, h, :], S0[:, h, :], eG[:, h, 255:256], B(k + 2)[:, P * h:P * h + P],
                                      ALU.mult, ALU.add)
                        result("dve", "s2", ins)
                for h in range(H):
                    after(dve, "act", "u2")
                    if h:
                        full(dve, tile_of["dstate"] + 2 * h - 1)
                    result("dve", ("ue", h), mul(ue, uu[0:NS, 2, h, :].unsqueeze(1).to_broadcast([NS, NB, P]),
                                                 b3(K("batch_rows", NS), P)))
                    dec = eG[:, h, NP_ + LS - 1:T:LS]
                    link(mul(states[:, :, h, :], states[:, :, h, :], b3(dec, P)))
                    for j in range(2):
                        k = tile_of["dstate"] + 2 * h + j
                        full(dve, k)
                        st = states[:, 4 * j:4 * j + 4, h, :]
                        result("dve", ("st", 2 * h + j), add(st, st, B(k)[:, :].rearrange("p (b v) -> p b v", b=4)))
                after(dve, "act", ("os", H - 1))
                result("dve", "orstd", dve.reciprocal(ostd, ostd))
                after(dve, "dve", "orstd")
                link(mul(oT, oT, ostd))
                result("dve", "cat", stt(catT[:, 0:4, :], oT, colsO[:, 0:1], zT, ALU.mult, ALU.mult))

            def mixer1():
                for i in range(6):
                    k = tile_of["vtok"] + i
                    n = TT[i // 2][1]
                    full(dve, k)
                    result("dve", ("vt", i), dve.tensor_copy(vtok[0:n, i // 2, 512 * (i % 2):512 * (i % 2) + 512], B(k)[0:n, :]))
                dve.wait_ge(ld_amask, 16)
                for st in range(17):
                    if st < 16:
                        h, u = st, st % 2
                        k = attp["S", h]
                        full(dve, k)
                        link(add(scr[:, u, :], B(k)[:, 0:384], KA("neg_prompt")))
                        dve.tensor_reduce(stat[:, u, 0:1], scr[:, u, 0:128], AX.X, ALU.max)
                        link(dve.tensor_reduce(stat[:, u, 1:2], scr[:, u, 128:384], AX.X, ALU.max))
                        result("dve", ("amax", h), dve.tensor_scalar(stat[:, u, 2:4], stat[:, u, 0:2], -0.125, None, ALU.mult))
                    if st:
                        h, u = st - 1, (st - 1) % 2
                        after(dve, "act", ("aexp", h))
                        for r, (x, y) in enumerate(((0, 128), (128, 384))):
                            ins = stt(prb[:, u, x:y], prb[:, u, x:y], 1.0, KA("cnt_prompt")[:, x:y], ALU.mult, ALU.mult,
                                      accum_out=stat[:, u, 4 + r:5 + r])
                        link(ins)
                        link(dve.reciprocal(stat[:, u, 4:6], stat[:, u, 4:6]))
                        dve.tensor_scalar(prb[:, u, 0:128], prb[:, u, 0:128], stat[:, u, 4:5], None, ALU.mult)
                        result("dve", ("apr", h), dve.tensor_scalar(prb[:, u, 128:384], prb[:, u, 128:384],
                                                                    stat[:, u, 5:6], None, ALU.mult))
                for b in range(NB + 1):
                    if b < NB:
                        for i in range(2, 4):
                            k = atts["K", b, i]
                            full(dve, k)
                            result("dve", ("kt", b, i), dve.tensor_copy(KT[:, 2 * i:2 * i + 2, :],
                                                                        B(k)[:, :].rearrange("p (c j) -> p c j", c=2)))
                        u = b % 2
                        k = atts["S", b]
                        full(dve, k)
                        add(scr[:, u, 0:256], B(k)[:, 0:256], KA("neg_cache"))
                        link(add(scr[:, u, 256:320], B(k)[:, 256:320], KA("neg_new")[:, 56 - LS * b:120 - LS * b]))
                        link(dve.tensor_reduce(stat[:, u, 0:1], scr[:, u, 0:T], AX.X, ALU.max))
                        result("dve", ("smax", b), dve.tensor_scalar(stat[:, u, 2:3], stat[:, u, 0:1], -0.125, None, ALU.mult))
                    if b:
                        k = atts["O", b - 1]
                        full(dve, k)
                        a = NP_ + LS * (b - 1)
                        for e in range(2):
                            r = slice(64 * e, 64 * e + 64)
                            ins = dve.tensor_copy(attnT[r, :, a:a + LS],
                                                  B(k)[r, 0:128].rearrange("p (c q) -> p c q", c=C)[:, :, LS * e:LS * e + LS])
                        result("dve", ("sout", b - 1), ins)
                    if b < NB:
                        after(dve, "act", ("sexp", b))
                        stt(prb[:, u, 0:256], prb[:, u, 0:256], 1.0, KA("cnt_cache"), ALU.mult, ALU.mult,
                            accum_out=stat[:, u, 4:5])
                        link(stt(prb[:, u, 256:320], prb[:, u, 256:320], 1.0, KA("cnt_new")[:, 56 - LS * b:120 - LS * b],
                                 ALU.mult, ALU.mult, accum_out=stat[:, u, 5:6]))
                        link(add(stat[:, u, 6:7], stat[:, u, 4:5], stat[:, u, 5:6]))
                        link(dve.reciprocal(stat[:, u, 6:7], stat[:, u, 6:7]))
                        result("dve", ("spr", b), dve.tensor_scalar(prb[:, u, 0:T], prb[:, u, 0:T], stat[:, u, 6:7],
                                                                    None, ALU.mult))

            def router(l):
                k = tile_of[f"rt{l}"]
                lg = small[:, :, 0:36]
                full(dve, k)
                dve.tensor_copy(small[:, 0:2, 0:36], B(k)[:, 0:72].rearrange("p (t n) -> p t n", t=2))
                result("dve", f"rt{l}", dve.tensor_copy(small[0:NS, 2, 0:36], B(k)[0:NS, 72:108]))
                after(dve, "dve", f"rt{l}")
                link(add(lg, lg, br[:, l:l + 1, :].to_broadcast([P, 3, 36])))
                lg4 = small[:, :, 0:4]

                def v3(a, n):
                    return rt[:, a:a + 3 * n].rearrange("p (t n) -> p t n", t=3)

                iota = K("iota8")

                def first_of(out, vals, top, tmp, topv, n):
                    link(dve.tensor_reduce(top, vals, AX.X, ALU.max))
                    link(dve.tensor_tensor(tmp, vals, b3(top, n), ALU.is_equal))
                    link(mul(tmp, tmp, iota[:, 0:n].unsqueeze(1).to_broadcast([P, 3, n])))
                    link(dve.tensor_reduce(topv, tmp, AX.X, ALU.max))
                    return dve.tensor_tensor(out, tmp, b3(topv, n), ALU.is_equal)

                gmax, tmp4, topv = rt[:, 0:3], v3(3, 4), rt[:, 15:18]
                oh_ins = first_of(onehot[:, :, :], lg4, gmax, tmp4, topv, 4)
                link(oh_ins)
                result("dve", f"rm{l}", dve.tensor_tensor(v3(48, 4), lg4, b3(gmax, 4), ALU.subtract))
                prod = rt[:, 100:196].rearrange("p (t g e) -> p t g e", t=3, g=NG)
                for t in range(3):
                    ins = mul(prod[:, t], small[:, t, 4:36].rearrange("p (g e) -> p g e", g=NG), b3(onehot[:, t, :], NE))
                result("dve", f"oh{l}", ins)
                after(dve, "dve", f"oh{l}")
                el, tmp8, oh1, oh2 = v3(200, 8), v3(224, 8), v3(248, 8), v3(272, 8)
                link(dve.tensor_reduce(el, prod.rearrange("p t g e -> p t e g"), AX.X, ALU.add))
                m1, m2 = rt[:, 296:299], rt[:, 309:312]
                link(first_of(oh1, el, m1, tmp8, topv, 8))
                link(stt(el, oh1, NEG, el, ALU.mult, ALU.add))
                link(first_of(oh2, el, m2, tmp8, topv, 8))
                result("dve", f"rt2{l}", dve.tensor_tensor(rt[:, 300:303], m2, m1, ALU.subtract))
                after(dve, "act", f"re2{l}")
                psum_, r_, w1, w2 = rt[:, 18:21], rt[:, 303:306], rt[:, 24:27], rt[:, 27:30]
                link(dve.tensor_reduce(psum_, v3(60, 4), AX.X, ALU.add))
                link(dve.tensor_scalar(w1, r_, 1.0, None, ALU.add))
                link(mul(w1, w1, psum_))
                link(dve.reciprocal(w1, w1))
                link(mul(w2, w1, r_))
                link(mul(oh1, oh1, b3(w1, 8)))
                link(mul(oh2, oh2, b3(w2, 8)))
                link(add(oh1, oh1, oh2))
                for t in range(3):
                    mul(gates[:, t, :].rearrange("p (g e) -> p g e", g=NG),
                        oh1[:, t, :].unsqueeze(1).to_broadcast([P, NG, NE]), b3(onehot[:, t, :], NE))
                k = tile_of[f"rk{l}"]
                link(dve.memset(rank[:, :, :], -2000.0))
                full(dve, k)
                dve.tensor_scalar(rank[:, 0:2, :], B(k)[:, 0:8].rearrange("p (t n) -> p t n", t=2), 1000.0, None, ALU.add)
                link(dve.tensor_scalar(rank[0:NS, 2, :], B(k)[0:NS, 8:12], 1000.0, None, ALU.add))
                link(mul(rank[:, :, :], rank[:, :, :], onehot[:, :, :]))
                dve.tensor_scalar(rank[:, :, :], rank[:, :, :], -1001.0, None, ALU.add)
                link(dve.tensor_reduce(rt[0:1, 30:31], B(k)[0:1, 16:20], AX.X, ALU.max))
                result("dve", f"flag{l}", dve.tensor_scalar(flag[:, :], rt[0:1, 30:31], SLOTS + 0.5, None, ALU.is_gt))

            def expert_pass(S, i, first, link):
                if not first:
                    link(dve.tensor_scalar(rank[:, :, :], rank[:, :, :], -float(SLOTS), None, ALU.add))
                for t in range(3):
                    ins = dve.tensor_tensor(perm[:, t, :, :], K("iota").unsqueeze(1).to_broadcast([P, NG, SLOTS]),
                                            b3(rank[:, t, :], SLOTS), ALU.is_equal)
                ins.then_inc(S["perm"], 1)
                link(dve.memset(AM["ys"], 0.0))
                dve.wait_ge(S["gsl"], i + 1)
                ins = dve.tensor_copy(gslot[:, :], bank[7][:, 0:NG * NE])
                if i == 0:
                    ins.then_inc(S["hid"], 2)
                    dve.wait_ge(S["hid"], 2)
                    dve.memset(stat[:, 0, 6:7], 0.0).then_inc(S["yadd"], 1)
                else:
                    link(ins)
                for g in range(NG):
                    with dve.Fori(0, 2) as j:
                        for u in range(4):
                            k0 = 32 * i + 8 * g + u
                            dve.wait_ge(S["silu"], 4 * j + (k0 + 1))
                            dve.wait_ge(S["gu"], 8 * j + 2 * (k0 + 1))
                            gate = gslot[:, bass.ds(4 * j + (8 * g + u), 1)]
                            stt(hid[:, u % 2, :], sg[:, u % 2, :], gate, bank[5 + u % 2][:, 0:256], ALU.mult, ALU.mult)\
                                .then_inc(S["hid"], 1)
                        dve.wait_ge(S["down"], 4 * j + (32 * i + 8 * g + 4))
                        dve.wait_ge(S["yadd"], j + (8 * i + 2 * g + 1))
                        add(ys[:, g, 0:512], ys[:, g, 0:512], bank[3][:, :])
                        add(ys[:, g, 512:1024], ys[:, g, 512:1024], bank[4][:, :]).then_inc(S["yadd"], 1)
                for m in range(C):
                    dve.wait_ge(S["sc"], 8 * i + m + 1)
                    ps = bank[5 + m % 2]
                    tmp, ins = residual(m, ps, 5)
                    ins.then_inc(S["scfree"], 1)
                    dve.wait_ge(S["scfree"], 8 * i + m + 1)
                    ins = add(xT[:, m, NP_:T], xT[:, m, NP_:T], tmp)
                link(ins)

            def experts(l):
                expert_pass(moe, l, True, link)
                S = more[l]
                v = dve.value_load(flag[:, :], min_val=0, max_val=1)
                with dve.If(v >= 1):
                    more_steps = [0]

                    def link2(ins):
                        more_steps[0] += 1
                        ins.then_inc(S["step"], 1)
                        dve.wait_ge(S["step"], more_steps[0])

                    for i in range(2):
                        expert_pass(S, i, False, link2)
                result("dve", f"x{l}2", dve.tensor_copy(stat[:, 0, 0:1], xT[:, C - 1, T - 1:T]))

            k = tile_of["cols"]
            dve.memset(small[:, :, :], 0.0)
            full(dve, k + 2)
            dve.tensor_copy(cols[:, :, :], B(k)[:, 0:26 * C].rearrange("p (c n) -> p c n", c=C))
            dve.tensor_copy(colsA[:, :, :], B(k + 1)[:, 0:28 * 12].rearrange("p (c n) -> p c n", c=12))
            result("dve", "cols", dve.tensor_copy(colsB[:, :, :], B(k + 2)[:, 0:19 * 4].rearrange("p (c n) -> p c n", c=4)))
            for c in range(C):
                k = tile_of["x"] + c
                full(dve, k)
                ins = dve.tensor_copy(xT[:, c, :], B(k)[:, 0:T])
            result("dve", "x0", ins)
            for l in range(2):
                for q in range(12):
                    k = tile_of[f"ada{l}"] + (2 * q + 2 if q < 11 else 23)
                    full(dve, k)
                    j, c0 = q // 2, 4 * (q % 2)
                    bias = cols[:, c0:c0 + 4, 5 + 6 * l + j:6 + 6 * l + j].to_broadcast([P, 4, NCOND])
                    result("dve", (f"mod{l}", q), add(mod[:, j, c0:c0 + 4, :],
                                                      B(k)[:, 0:4 * NCOND].rearrange("p (c n) -> p c n", c=4), bias))
                after(dve, "dve", (f"mod{l}", 11))
                norm(f"{l}1", tile_of[f"norm{l}1"])
                (mixer0 if l == 0 else mixer1)()
                for m in range(C):
                    k = tile_of[f"out{l}"] + m
                    full(dve, k)
                    tmp, ins = residual(m, B(k), 2)
                    link(ins)
                    result("dve", (f"xo{l}", m), add(xT[:, m, NP_:T], xT[:, m, NP_:T], tmp))
                after(dve, "dve", (f"xo{l}", C - 1))
                after(dve, "pool", f"mixer{l}")
                norm(f"{l}2", tile_of[f"norm{l}2"])
                router(l)
                experts(l)
                after(dve, "dve", f"x{l}2")
            norm("f", tile_of["normf"])

        assert made == {"dve": len(DVE_ORDER), "act": len(ACT_ORDER), "pool": len(POOL_ORDER)}, made


_INS = ["x_prompt", "x_sample", "state_a_ssm", "state_a_conv", "state_b_conv", "cache_c_k", "cache_c_v",
        "c_prompt", "c_sample", "w_ada", "b_ada", "norm1", "norm2", "norm_f", "w_in_even", "conv_a_w", "a_log",
        "dt_bias", "o_gain_a", "conv_b_w", "w_out_even", "w_qkv_odd", "w_out_odd", "w_router_group",
        "b_router_group", "w_router_expert", "b_router_expert", "w_exp_gate", "w_exp_up", "w_exp_down"]
_OUTS = {"y_p": (1, 256, 1024), "y_s": (8, 8, 1024), "ssm_p": (1, 1, 4, 128, 128), "ssm_s": (1, 8, 4, 128, 128),
         "aconv_p": (1, 1, 3, 1536), "aconv_s": (1, 8, 3, 1536), "bconv_p": (1, 1, 2, 512), "bconv_s": (1, 8, 2, 512),
         "ck_p": (1, 1, 256, 16, 64), "ck_s": (1, 8, 8, 16, 64), "cv_p": (1, 1, 256, 16, 64), "cv_s": (1, 8, 8, 16, 64)}


def kernel(**inputs):
    import numpy as _np
    import concourse.bacc as _bacc
    from concourse import mybir as _mybir
    from concourse.bass_utils import run_bass_kernel_spmd as _run

    nc = _bacc.Bacc("TRN2", target_bir_lowering=False, num_devices=1)
    given = {name: _np.ascontiguousarray(inputs[name]) for name in _INS}
    given["masks"] = packed(constants())
    given["amasks"] = packed(attention_constants())
    arrays = {f"in_{name}_dram": a for name, a in given.items()}
    ins = {name: nc.dram_tensor(f"in_{name}_dram", a.shape, _mybir.dt.from_np(a.dtype), kind="ExternalInput").ap()
           for name, a in given.items()}
    outs = {name: nc.dram_tensor(f"out_{name}_dram", shape, _mybir.dt.float32, kind="ExternalOutput").ap()
            for name, shape in _OUTS.items()}
    trunk_program(nc, ins, outs)
    r = _run(nc, [arrays], core_ids=[0])
    return tuple(r.results[0][f"out_{name}_dram"] for name in _OUTS)
```

```python
from contextlib import ExitStack

import numpy as np

import concourse.bass as bass
from concourse import mybir

F32 = mybir.dt.float32
I32 = mybir.dt.int32
ALU = mybir.AluOpType
ACT = mybir.ActivationFunctionType
AX = mybir.AxisListType

P = 128
D = 1024
C = D // P
NP_, NS, NB = 256, 64, 8
LS = NS // NB
T = NP_ + NS
TT = [(0, 128), (128, 128), (256, 64)]
NCOND = 1 + NB
H = 4
HIST = 3
EP, ES = HIST + NP_, HIST + LS
EW = EP + NB * ES
CW = EW - HIST
EPS = 1e-6
NG, NE, DE = 4, 8, 256
SLOTS = 128
R = 6
U = 2048
NEG = -1e30
NBANK = 8


def constants():
    i = np.arange(P)
    j = i[:, None]
    i = i[None, :]
    out = {"ident": j == i, "ones": np.ones((P, P)), "upto": j <= i, "after": j > i}
    for s in (1, 2, 4, 8, 16, 32, 64):
        out[f"lev{s}"] = (j // (2 * s) == i // (2 * s)) & (j // s % 2 == 0) & (i // s % 2 == 1)
    same = (j // LS == i // LS)[:, :NS]
    out["upto_s"] = same & (j <= i)[:, :NS]
    out["after_s"] = same & (j > i)[:, :NS]
    out["batch_rows"] = j // LS == np.arange(NB)[None, :]
    out["iota"] = np.broadcast_to(i, (P, P))
    out["iota8"] = np.broadcast_to(np.arange(8)[None, ::-1] + 1, (P, 8))
    out["eps"] = np.full((P, 1), EPS)
    out["one"] = np.ones((P, 1))
    return {k: np.asarray(v, np.float32) for k, v in out.items()}


def attention_constants():
    def count(d):
        return ((d >= 0) & (d <= 128)) * 1.0 + ((d >= 0) & (d <= 512) & (d % 4 == 0)) + ((d >= 0) & (d <= 2048) & (d % 16 == 0))
    p = np.arange(P)[:, None]
    k = np.arange(256)[None]
    col = np.arange(120)[None] - 56
    prompt = np.concatenate([count(p - k[:, :128]), count(p + 128 - k)], 1)
    cache = count(256 + p % LS - k)
    new = np.where((col >= 0) & (col < LS), count(p % LS - col), 0.0)
    out = {}
    for n, c in (("prompt", prompt), ("cache", cache), ("new", new)):
        out["cnt_" + n] = c
        out["neg_" + n] = np.where(c > 0, 0.0, NEG)
    return {k: np.asarray(v, np.float32) for k, v in out.items()}


def packed(tables):
    return np.ascontiguousarray(np.concatenate(list(tables.values()), 1))


def trunk_program(nc, I, O):
    at, n = {}, 0
    for k, v in constants().items():
        at[k] = (n, n + v.shape[1])
        n += v.shape[1]
    NCONST = n
    aat, n = {}, 0
    for k, v in attention_constants().items():
        aat[k] = (n, n + v.shape[1])
        n += v.shape[1]
    NACONST = n

    with ExitStack() as ctx:
        def sb(name, shape, dt=F32):
            return ctx.enter_context(nc.sbuf_tensor(name, shape, dt))

        def sem(name):
            return ctx.enter_context(nc.semaphore(name))

        ring = sb("ring", [P, R, U])
        const = sb("const", [P, NCONST])
        xT = sb("xT", [P, C, T])
        hT = sb("hT", [P, C, T])
        scratch = sb("scratch", [P, C, T])
        rstd = sb("rstd", [P, T])
        mod = sb("mod", [P, 2, 6, C, NCOND])
        gainA = sb("gainA", [P, C, NCOND])
        cols = sb("cols", [P, C, 26])
        condT = sb("condT", [P, C, NCOND])
        small = sb("small", [P, 3, 40])
        flag = sb("flag", [1, 1], I32)
        gates = sb("gates", [P, 3, NG * NE])
        tiny = sb("tiny", [P, 512])
        ARENA = 28080
        arena = sb("arena", [P, ARENA])

        def K(name, rows=P):
            a, b = at[name]
            return const[0:rows, a:b]

        modrows = [x[0:NCOND, :].rearrange("p (u n) -> p u n", u=2) for x in
                   (hT[:, :, :].rearrange("p c t -> p (c t)")[:, 2048:2560], tiny[:, :])]

        def modrow(l, u):
            return modrows[l == 1 and u >= HEAD_UNITS][:, u % 2, :]



        def carve(spec, base=0):
            out, n = {}, base
            for name, size in spec:
                out[name] = arena[:, n:n + size]
                n += size
            assert n <= ARENA, n
            return out

        A0 = carve([("ext", 12 * EW), ("cT", 12 * T), ("z", 4 * T), ("bx", 4 * EW), ("bg", 4 * T),
                    ("cg", 4 * T), ("cat", 8 * T), ("gam", 12 * P), ("AT", 12 * P), ("X", 12 * P),
                    ("qkg", 12 * P), ("XT", 12 * P), ("LT", 12 * P), ("PB", 12 * P), ("vb", 12 * P)])
        AT_AT = 12 * EW + 12 * T + 4 * T + 4 * EW + 4 * T + 4 * T + 8 * T + 12 * P
        ext = A0["ext"].rearrange("p (m e) -> p m e", e=EW)
        states = A0["ext"][:, 0:NB * H * P].rearrange("p (b h v) -> p b h v", b=NB, h=H)
        cT = A0["cT"].rearrange("p (m t) -> p m t", t=T)
        zT = A0["z"].rearrange("p (m t) -> p m t", t=T)
        bx = A0["bx"].rearrange("p (m e) -> p m e", e=EW)
        bg = A0["bg"].rearrange("p (m t) -> p m t", t=T)
        cg = A0["cg"].rearrange("p (m t) -> p m t", t=T)
        catT = A0["cat"].rearrange("p (m t) -> p m t", t=T)

        def sysview(name):
            return A0[name].rearrange("p (t h i) -> p t h i", t=3, h=H)
        gam, AT, X, qkg, XT, LT, PB, vb = [sysview(x) for x in ("gam", "AT", "X", "qkg", "XT", "LT", "PB", "vb")]
        kd = scratch[:, :, :].rearrange("p c t -> p (c t)")[:, 0:12 * P].rearrange("p (t h i) -> p t h i", t=3, h=H)
        eG = A0["cat"][:, 0:H * T].rearrange("p (m t) -> p m t", t=T)
        kb = A0["LT"][:, 0:H * T].rearrange("p (m t) -> p m t", t=T)
        qd = cT[:, 0:H, :]
        uu, RR = LT, PB
        oT = cT[:, 0:H, :]
        kTm = arena[:, AT_AT:AT_AT + H * NB * NS].rearrange("p (h b i) -> p h b i", h=H, b=NB)
        ue = arena[0:NS, AT_AT + 2048:AT_AT + 3072].rearrange("p (b v) -> p b v", b=NB)
        convacc = A0["gam"][:, 0:2 * EW].rearrange("p (u e) -> p u e", u=2)
        S0 = tiny[:, :].rearrange("p (h v) -> p h v", h=H)
        rowsA0 = arena[0:28, 20000:20000 + 1536]
        rowsB0 = arena[0:19, 21600:21600 + 512]
        rowsM0 = arena[0:26, 22200:22200 + D]
        xload = arena[:, 23300:23300 + 3 * D].rearrange("p (t d) -> p t d", t=3)
        colsA = sb("colsA", [P, 12, 28])
        colsB = sb("colsB", [P, 4, 19])
        colsO = sb("colsO", [P, 1])
        wab = sb("wab", [P, C, 8])
        dtb = sb("dtb", [P, 2, 4])
        wr = [sb("wr", [P, C, 36]), arena[:, 27200:27200 + C * 36].rearrange("p (c n) -> p c n", c=C)]
        br = [sb("br", [P, 36]), arena[:, 27500:27536]]
        gab = sb("gab", [P, 3, 8])
        gg = sb("gg", [P, 3, 4])
        sc8 = sb("sc8", [P, 3, 16])
        beta = sb("beta", [P, 3, 4])
        nbe = sb("nbe", [P, 3, 4])
        gcols = sb("gcols", [P, 3, 8])
        egc = sb("egc", [P, 3, 8])
        bconv = scratch[:, :, :].rearrange("p c t -> p (c t)")[:, 12 * P:12 * P + 2 * EW].rearrange("p (u e) -> p u e", u=2)
        osq = A0["bx"][:, 0:H * T].rearrange("p (m t) -> p m t", t=T)
        l2col = sb("l2col", [P, 3, 8])
        oncol = sb("oncol", [P, 3, H])
        onehot = sb("onehot", [P, 3, NG])
        stout = hT[:, :, :].rearrange("p c t -> p (c t)")[0:27, 0:2048]
        stg = tiny[:, 0:12 * 27]
        stgb = tiny[:, 324:324 + 4 * 18]

        QB = C * (P + 16)
        A1 = carve([("qkv", 24 * T), ("vtok", 3 * D), ("Kc", 2 * D), ("Vc", 2 * 2 * D), ("KT", C * 256),
                    ("qbd", 2 * QB), ("sc", 2 * 384), ("pr", 2 * 384), ("pT", 2 * 384), ("scS", 2 * T), ("prS", 2 * T),
                    ("pTS", 2 * 384), ("msk", NACONST)])
        qkvT = A1["qkv"].rearrange("p (m t) -> p m t", t=T)
        vtok = A1["vtok"].rearrange("p (t d) -> p t d", t=3)
        ktok = scratch[:, :, :].rearrange("p c t -> p (c t)")[:, 0:2 * D].rearrange("p (u d) -> p u d", u=2)
        Kc = A1["Kc"].rearrange("p (a d) -> p a d", a=2)
        Vc = A1["Vc"].rearrange("p (u a d) -> p u a d", u=2, a=2)
        KT = A1["KT"].rearrange("p (c j) -> p c j", c=C)
        qbd = A1["qbd"].rearrange("p (u q) -> p u q", u=2)
        scr = A1["sc"].rearrange("p (u j) -> p u j", u=2)
        prb = A1["pr"].rearrange("p (u j) -> p u j", u=2)
        pT = A1["pT"].rearrange("p (u j) -> p u j", u=2)
        scrS, prbS, pTS = [A1[n].rearrange("p (u j) -> p u j", u=2) for n in ("scS", "prS", "pTS")]
        attnT = hT
        stat = sb("stat", [P, 2, 8])
        statS = sb("statS", [P, 2, 8])

        def KA(name):
            a, b = aat[name]
            return A1["msk"][:, a:b]

        AM = carve([("htok", 3 * D), ("hg", C * NG * SLOTS), ("perm", 3 * NG * SLOTS), ("permT", NG * T),
                    ("ys", NG * D), ("sg", 2 * DE), ("hid", 2 * DE), ("hidT", 2 * DE), ("ring2", 3 * U), ("rt", 600)])
        htok = AM["htok"].rearrange("p (t d) -> p t d", t=3)
        hg = AM["hg"].rearrange("p (c s) -> p c s", c=C)
        perm = AM["perm"].rearrange("p (t g s) -> p t g s", t=3, g=NG)
        permT = AM["permT"].rearrange("p (g t) -> p g t", g=NG)
        ys = AM["ys"].rearrange("p (g d) -> p g d", g=NG)
        sg = AM["sg"].rearrange("p (u f) -> p u f", u=2)
        hid = AM["hid"].rearrange("p (u f) -> p u f", u=2)
        hidT = AM["hidT"].rearrange("p (u f s) -> p u f s", u=2, f=2)
        ring2 = AM["ring2"].rearrange("p (u n) -> p u n", u=3)
        rt = AM["rt"]
        ytok = AM["htok"].rearrange("p (t d) -> p t d", t=3)
        rank = sb("rank", [P, 3, NG])
        gslot = sb("gslot", [P, NG * NE])

        bank = [ctx.enter_context(nc.psum_tensor(f"bank{i}", [P, 512], F32)) for i in range(NBANK)]

        tile_of, ntile = {}, 0

        def tiles(name, n):
            nonlocal ntile
            tile_of[name] = ntile
            ntile += n

        schedule = {"head": [], "mixer0": [], "mixer1": []}
        readers = {}
        LEVELS = [(s, [0, 1, 2] if s <= 4 else [0, 1]) for s in (2, 4, 8, 16, 32, 64)]

        def fills(part, step, *read_by):
            nonlocal ntile
            schedule[part].append(("pe", step))
            tile_of[step] = ntile
            readers[ntile] = list(read_by)
            ntile += 1

        def makes(part, who, *steps):
            schedule[part] += [(who, step) for step in steps]

        def steps_of(part, who):
            return [step for w, step in schedule[part] if w == who]

        def ada_rows(part, l, u):
            fills(part, ("row", l, u), ("act", ("row", l, u)))
            makes(part, "act", ("row", l, u))

        def ada_turn(part, l, u):
            fills(part, ("turn", l, u), ("dve", ("mod", l, u)))
            makes(part, "dve", ("mod", l, u))

        def plan_head():
            fills("head", ("cols", 0), ("dve", ("cols", 0)))
            makes("head", "dve", ("cols", 0))
            makes("head", "act", ("cond",))
            for u in range(HEAD_UNITS):
                ada_rows("head", 0, u)
                if u >= 1:
                    ada_turn("head", 0, u - 1)
                if u == 2:
                    for i in (1, 2):
                        fills("head", ("cols", i), ("dve", ("cols", i)))
                        makes("head", "dve", ("cols", i))
                    for c in range(C):
                        fills("head", ("x", c), ("dve", ("x", c)))
                        makes("head", "dve", ("x", c))
            ada_turn("head", 0, HEAD_UNITS - 1)

        def plan_mixer0():
            M = "mixer0"

            def project_in(m):
                fills(M, ("in", m), ("act", ("ext", m)) if m < 12 else ("act", ("z", m)) if m < 16
                      else ("act", ("gt", m)) if m < 24 else ("dve", ("bx", m - 24)))
                if m < 12:
                    makes(M, "act", ("ext", m))
                    makes(M, "dve", ("conv", m))
                elif m < 24:
                    makes(M, "act", ("z", m) if m < 16 else ("gt", m))
                else:
                    makes(M, "dve", ("bx", m - 24))
                if 2 <= m < 14:
                    makes(M, "act", ("cv", m - 2))
                if 2 <= m < 10:
                    makes(M, "act", ("sq", m - 2))

            rest_units = [(0, u) for u in range(HEAD_UNITS, 24)] + [(1, u) for u in range(HEAD_UNITS)]
            done = {"in": 22, "unit": 0}

            def fill(n=1):
                for _ in range(n):
                    if done["in"] < 28:
                        project_in(done["in"])
                        done["in"] += 1
                        continue
                    i = done["unit"]
                    if i > len(rest_units):
                        return
                    if i:
                        ada_turn(M, *rest_units[i - 1])
                    if i < len(rest_units):
                        ada_rows(M, *rest_units[i])
                    if i < 4:
                        makes(M, "dve", ("catb", i))
                    if 4 <= i < 8:
                        fills(M, ("st", i - 4), ("act", ("so", i - 4)))
                        makes(M, "act", ("so", i - 4))
                    done["unit"] += 1

            fills(M, ("ab",), ("dve", ("gab",)))
            makes(M, "dve", ("gab",), ("gabs",), ("gmax",))
            makes(M, "act", ("gea",), ("geb",))
            for m in range(22):
                project_in(m)
                if m == 1:
                    makes(M, "dve", ("g",))
                if m == 14:
                    fills(M, ("gcol",), ("dve", ("gcol",)))
                    makes(M, "dve", ("gcol",))
                    makes(M, "act", ("egc",))
                    for t in range(3):
                        fills(M, ("grow", t), ("act", ("eG", t)), ("dve", ("gd", t)))
                        makes(M, "act", ("eG", t))
                        makes(M, "dve", ("gd", t))
                    makes(M, "act", ("ge",))
                    makes(M, "dve", ("gam",))
                if m == 15:
                    fills(M, ("l2ss",), ("act", ("l2s",)))
                    makes(M, "act", ("l2s",))
                    makes(M, "dve", ("l2r",))
                if m in (16, 17):
                    for j in range(4 * (m - 16), 4 * (m - 16) + 4):
                        fills(M, ("l2bc", j), ("dve", ("qn", j)))
                        makes(M, "dve", ("qn", j))
                for at_m, tile, res in ((18, "brow", "kb"), (18, "vt", "vb"), (19, "kt", "kd"), (20, "at", "at"),
                                        (21, "qk", "qkg")):
                    if m == at_m:
                        if tile == "kt":
                            makes(M, "dve", ("nbe",))
                        for t in range(3):
                            fills(M, (tile, t), ("dve", (res, t)))
                            makes(M, "dve", (res, t))
                if m == 20:
                    makes(M, "dve", *[("xt1", t) for t in range(3)])
                if m == 21:
                    makes(M, "dve", ("qd",))
                    for t in range(3):
                        fills(M, ("xt0", t), ("act", ("x0", t)))
                        makes(M, "act", ("x0", t))
            for s, ts in LEVELS:
                makes(M, "dve", *[("lt", s, t) for t in ts])
                for t in ts:
                    fills(M, ("P", s, t), ("act", ("pb", s, t)))
                    makes(M, "act", ("pb", s, t))
                fill()
                for t in ts:
                    fills(M, ("XPt", s, t), ("dve", ("xt", s, t)))
                    fills(M, ("XP", s, t), ("dve", ("xi", s, t)))
                    makes(M, "dve", ("xt", s, t), ("xi", s, t))
                fill()
            makes(M, "dve", ("ktm",))

            def solve(t):
                fills(M, ("u", t), ("act", ("u", t)))
                makes(M, "act", ("u", t))

            def from_state(t):
                fills(M, ("kS", t), ("dve", ("r", t)))
                makes(M, "dve", ("r", t))

            def outputs(t):
                fills(M, ("o", t), ("dve", ("o", t)))
                makes(M, "dve", ("o", t))

            def prompt_state(t):
                fills(M, ("s", t), ("dve", ("s", t)))
                makes(M, "dve", ("s", t))

            def sample_states(h):
                makes(M, "dve", ("ue", h))
                for j in range(2):
                    fills(M, ("ds", h, j), ("dve", ("ds", h, j)))
                    makes(M, "dve", ("ds", h, j))

            solve(0)
            from_state(2)
            fill(3)
            outputs(0)
            prompt_state(0)
            solve(2)
            fill(3)
            from_state(1)
            outputs(2)
            fill(3)
            solve(1)
            sample_states(0)
            fill(3)
            outputs(1)
            prompt_state(1)
            makes(M, "act", ("osq",))
            sample_states(1)
            fill(3)
            fills(M, ("onss",), ("act", ("ons",)))
            makes(M, "act", ("ons",))
            makes(M, "dve", ("onr",))
            sample_states(2)
            fill(3)
            for h_ in range(H):
                fills(M, ("onbc", h_), ("dve", ("on", h_)))
                makes(M, "dve", ("on", h_))
            sample_states(3)
            fill(len(rest_units))
            makes(M, "dve", ("cat",))

        def plan_mixer1():
            M = "mixer1"
            for st in range(18):
                b = st // 2
                if st < 16:
                    fills(M, ("S", st), ("dve", ("amax", st)))
                    makes(M, "dve", ("amax", st))
                    makes(M, "act", ("aexp", st))
                if b < NB and st % 2 == 0:
                    for i in range(4):
                        who = "act" if i < 2 else "dve"
                        fills(M, ("K", b, i), (who, ("kt", b, i)))
                        makes(M, who, ("kt", b, i))
                if b < NB and st % 2 == 1:
                    fills(M, ("Ss", b), ("dve", ("smax", b)))
                    makes(M, "dve", ("smax", b))
                    makes(M, "act", ("sexp", b))
                if 1 <= st <= 16:
                    makes(M, "dve", ("apr", st - 1))
                    fills(M, ("T", st - 1), ("act", ("apT", st - 1)))
                    makes(M, "act", ("apT", st - 1))
                if b >= 1 and st % 2 == 0:
                    makes(M, "dve", ("spr", b - 1))
                    fills(M, ("Ts", b - 1), ("act", ("spT", b - 1)))
                    makes(M, "act", ("spT", b - 1))
                if st >= 2:
                    h_ = st - 2
                    if h_ % 2 == 0:
                        fills(M, ("O", h_), ("act", ("aout", h_ // 2)))
                    else:
                        schedule[M].append(("pe", ("O", h_)))
                        tile_of["O", h_] = tile_of["O", h_ - 1]
                        makes(M, "act", ("aout", h_ // 2))
                if st < 17:
                    if HEAD_UNITS + st < 24:
                        ada_rows(M, 1, HEAD_UNITS + st)
                    if st:
                        ada_turn(M, 1, HEAD_UNITS + st - 1)
                if b >= 1 and st % 2 == 1:
                    fills(M, ("Os", b - 1), ("dve", ("sout", b - 1)))
                    makes(M, "dve", ("sout", b - 1))

        HEAD_UNITS = 8
        plan_head()
        for l in range(2):
            tiles(f"norm{l}1", 1)
            if l == 0:
                plan_mixer0()
            else:
                tiles("qkv", 24)
                tiles("ktok", 6)
                tiles("vtok", 6)
                plan_mixer1()
            tiles(f"out{l}", C)
            tiles(f"norm{l}2", 1)
            tiles(f"rt{l}", 1)
            tiles(f"ht{l}", 6)
            tiles(f"rk{l}", 1)
        tiles("normf", 1)
        tiles("y", 6)

        bank_full = [sem(f"bank_full{i}") for i in range(NBANK)]

        def B(k):
            return bank[k % NBANK]

        def filled(ins, k):
            ins.then_inc(bank_full[k % NBANK], 1)

        def full(eng, k):
            eng.wait_ge(bank_full[k % NBANK], k // NBANK + 1)

        unit_of, nunit = {}, 0

        def units(name, n):
            nonlocal nunit
            unit_of[name] = nunit
            nunit += n

        units("ada0", HEAD_UNITS)
        units("in", 14)
        units("ada_rest", 24)
        units("out0", 4)
        units("moe0", 96)
        units("qkv", 12)
        units("ada_late", 24 - HEAD_UNITS)
        units("out1", 4)
        units("moe1", 96)
        
        unit_loaded = [sem(f"unit_loaded{i}") for i in range(R)]

        def ada_unit(l, u):
            n = 24 * l + u
            if n < HEAD_UNITS:
                return unit_of["ada0"] + n
            return unit_of["ada_rest"] + n - HEAD_UNITS if n < HEAD_UNITS + 24 else unit_of["ada_late"] + n - HEAD_UNITS - 24

        def need_unit(pe, n):
            pe.wait_ge(unit_loaded[n % R], 16 * (n // R + 1))

        def slot(n, width=256):
            return ring[:, n % R, :].rearrange("p (c n) -> p c n", n=width)

        ld_const, ld_rowsM, ld_rows = sem("ld_const"), sem("ld_rowsM"), sem("ld_rows")
        ld_x, ld_small, ld_router1 = sem("ld_x"), sem("ld_small"), sem("ld_router1")
        ld_states, ld_amask = sem("ld_states"), sem("ld_amask")
        ld_kc, ld_vc = sem("ld_kc"), [sem("ld_vc0"), sem("ld_vc1")]
        sent = sem("sent")
        ktok_sent = sem("ktok_sent")
        NROWSM, NROWS, NSMALL = 6, 4, 8
        vstep, astep, gstep = sem("vstep"), sem("astep"), sem("gstep")
        dve_results, act_results, pool_results = sem("dve_results"), sem("act_results"), sem("pool_results")

        DVE_ORDER = steps_of("head", "dve")
        for l in range(2):
            DVE_ORDER += [f"xa{l}1", f"xn{l}1", f"hs{l}1"]
            if l == 0:
                DVE_ORDER += steps_of("mixer0", "dve")
            else:
                DVE_ORDER += [("vt", i) for i in range(6)]
                DVE_ORDER += steps_of("mixer1", "dve")
            DVE_ORDER += [(f"xo{l}", m) for m in range(C)] + [f"xa{l}2", f"xn{l}2", f"hs{l}2"]
            DVE_ORDER += [f"rt{l}", f"rm{l}", f"oh{l}", f"rt2{l}", f"flag{l}", f"x{l}2"]
        DVE_ORDER += ["xaf", "xnf"]
        ACT_ORDER = steps_of("head", "act")
        for l in range(2):
            ACT_ORDER += [(f"sq{l}1", c) for c in range(C)] + [f"std{l}1", f"hp{l}1"]
            if l == 0:
                ACT_ORDER += steps_of("mixer0", "act")
            else:
                ACT_ORDER += [("qkv", m) for m in range(24)] + [("ktok", i) for i in range(6)]
                ACT_ORDER += steps_of("mixer1", "act")
            ACT_ORDER += [(f"sq{l}2", c) for c in range(C)] + [f"std{l}2", f"hp{l}2"] + [(f"ht{l}", i) for i in range(6)] + [f"re{l}", f"re2{l}"]
        ACT_ORDER += [("sqf", c) for c in range(C)] + ["stdf", "hpf"] + [("yt", i) for i in range(6)]
        POOL_ORDER = ["hist", "stg", "mixer0", "qbd0"] + [("qbd", b) for b in range(NB)] + ["mixer1"]
        ORDER = {"dve": (dve_results, {n: i for i, n in enumerate(DVE_ORDER)}),
                 "act": (act_results, {n: i for i, n in enumerate(ACT_ORDER)}),
                 "pool": (pool_results, {n: i for i, n in enumerate(POOL_ORDER)})}
        made = {"dve": 0, "act": 0, "pool": 0}

        def after(eng, who, name):
            s, order = ORDER[who]
            eng.wait_ge(s, order[name] + 1)

        def result(who, name, ins):
            s, order = ORDER[who]
            assert order[name] == made[who], (who, name, order[name], made[who])
            made[who] += 1
            ins.then_inc(s, 1)

        def reads(name, *per_tile):
            for m, rs in enumerate(per_tile):
                readers[tile_of[name] + m] = rs if isinstance(rs, list) else [rs]

        for l in range(2):
            for s in "12":
                reads(f"norm{l}{s}", ("act", f"std{l}{s}"))
            reads(f"out{l}", *[("dve", (f"xo{l}", m)) for m in range(C)])
            reads(f"rt{l}", ("dve", f"rt{l}"))
            reads(f"ht{l}", *[("act", (f"ht{l}", i)) for i in range(6)])
            reads(f"rk{l}", ("dve", f"flag{l}"))
        reads("qkv", *[("act", ("qkv", m)) for m in range(24)])
        reads("ktok", *[("act", ("ktok", i)) for i in range(6)])
        reads("vtok", *[("dve", ("vt", i)) for i in range(6)])
        reads("normf", ("act", "stdf"))
        reads("y", *[("act", ("yt", i)) for i in range(6)])

        def claim(pe, k):
            if k >= NBANK:
                for who, name in readers[k - NBANK]:
                    after(pe, who, name)

        PASS = ("perm", "aux", "auxfree", "gsl", "gu", "silu", "hid", "tr", "hidT", "down", "yadd", "sc", "scfree")
        moe = {k: sem(f"moe_{k}") for k in PASS}
        more = [{k: sem(f"more{l}_{k}") for k in PASS + ("wl0", "wl1", "wl2", "step")} for l in range(2)]

        unit_tile = {}
        for l in range(2):
            for u in range(24):
                unit_tile[ada_unit(l, u)] = tile_of["row", l, u]
            for u in range(4):
                unit_tile[unit_of[f"out{l}"] + u] = tile_of[f"out{l}"] + 2 * u + 1
        for u in range(14):
            unit_tile[unit_of["in"] + u] = tile_of["in", 2 * u + 1]
        for u in range(12):
            unit_tile[unit_of["qkv"] + u] = tile_of["qkv"] + 2 * u + 1

        def wait_slot(sp, n):
            n -= R
            if n < 0:
                return
            if n in unit_tile:
                full(sp, unit_tile[n])
                return
            l = 0 if n < unit_of["qkv"] else 1
            wait_expert(sp, 32 * l + (n - unit_of[f"moe{l}"]) // 3, (n - unit_of[f"moe{l}"]) % 3)

        def wait_expert(sp, k, w):
            if w < 2:
                sp.wait_ge(moe["gu"], 2 * k + w + 1)
            else:
                sp.wait_ge(moe["down"], k + 1)

        gate_v = I["w_exp_gate"].rearrange("l g e (c p) f -> (l g e) p c f", p=P)
        up_v = I["w_exp_up"].rearrange("l g e (c p) f -> (l g e) p c f", p=P)
        down_v = I["w_exp_down"].rearrange("l g e (f p) d -> (l g e) p f d", p=P)
        expert_views = [(gate_v, 256), (up_v, 256), (down_v, D)]

        def wide(w, a):
            return w.rearrange("(c p) n -> p c n", p=P)[:, :, a:a + 256]

        def load_router(eng, l, s):
            for dst, src in ((wr[l][:, :, 0:4], I["w_router_group"][l].rearrange("(c p) n -> p c n", p=P)),
                             (wr[l][:, :, 4:36], I["w_router_expert"][l].rearrange("(c p) n -> p c n", p=P)),
                             (br[l][:, 0:4], I["b_router_group"][l:l + 1].to_broadcast([P, 4])),
                             (br[l][:, 4:36], I["b_router_expert"][l:l + 1].to_broadcast([P, 32]))):
                eng.dma_start(dst, src).then_inc(s, 16)

        block = ctx.enter_context(nc.Block())

        @block.sync
        def _(sp):
            def load(n, src, width=256):
                wait_slot(sp, n)
                sp.dma_start(slot(n, width), src).then_inc(unit_loaded[n % R], 16)

            def load_experts(l):
                base = unit_of[f"moe{l}"]
                for n in range(12):
                    view, width = expert_views[n % 3]
                    load(base + n, view[NG * NE * l + n // 3], width)
                with sp.Fori(1, NG * NE // 4) as q:
                    for n in range(12):
                        view, width = expert_views[n % 3]
                        wait_expert(sp, 4 * q + (32 * l + (n - R) // 3), (n - R) % 3)
                        src = view[bass.ds(4 * q + (NG * NE * l + n // 3), 1)].rearrange("a p c f -> p (a c) f")
                        sp.dma_start(slot(base + n, width), src).then_inc(unit_loaded[(base + n) % R], 16)
                after(sp, "dve", f"flag{l}")
                S = more[l]
                v = sp.value_load(flag[:, :], min_val=0, max_val=1)
                with sp.If(v >= 1):
                    for i in range(2):
                        if i == 0:
                            for w, (view, width) in enumerate(expert_views):
                                sp.dma_start(ring2[:, w, :].rearrange("p (c n) -> p c n", n=width),
                                             view[NG * NE * l]).then_inc(S[f"wl{w}"], 16)
                        with sp.Fori(1 - i, NG * NE) as e:
                            for w, (view, width) in enumerate(expert_views):
                                if w < 2:
                                    sp.wait_ge(S["gu"], 2 * e + (64 * i + w - 1))
                                else:
                                    sp.wait_ge(S["down"], e + 32 * i)
                                src = view[bass.ds(e + NG * NE * l, 1)].rearrange("a p c f -> p (a c) f")
                                sp.dma_start(ring2[:, w, :].rearrange("p (c n) -> p c n", n=width), src)\
                                  .then_inc(S[f"wl{w}"], 16)

            for dst, src in ((rowsM0[0:2], I["norm1"]), (rowsM0[2:4], I["norm2"]),
                             (rowsM0[4:5], I["norm_f"].rearrange("(a d) -> a d", a=1)),
                             (rowsM0[5:17], I["b_ada"].rearrange("l (j d) -> (l j) d", d=D)),
                             (rowsM0[17:18], I["c_prompt"]), (rowsM0[18:26], I["c_sample"])):
                sp.dma_start(dst, src).then_inc(ld_rowsM, 16)
            for l in range(2):
                if l == 0:
                    for u in range(HEAD_UNITS):
                        load(ada_unit(0, u), wide(I["w_ada"][0], 256 * u))
                    for u in range(14):
                        load(unit_of["in"] + u, wide(I["w_in_even"][0], 256 * u if u < 8 else 256 * u + 8))
                    for n in range(HEAD_UNITS, HEAD_UNITS + 24):
                        load(ada_unit(0, n), wide(I["w_ada"][n // 24], 256 * (n % 24)))
                    for u in range(4):
                        load(unit_of["out0"] + u, wide(I["w_out_even"][0], 256 * u))
                else:
                    for u in range(12):
                        load(unit_of["qkv"] + u, wide(I["w_qkv_odd"][0], 256 * u))
                    for u in range(HEAD_UNITS, 24):
                        load(ada_unit(1, u), wide(I["w_ada"][1], 256 * u))
                    for u in range(4):
                        load(unit_of["out1"] + u, wide(I["w_out_odd"][0], 256 * u))
                load_experts(l)

        @block.gpsimd
        def _(pool):
            pool.memset(ext[:, :, 0:HIST], 0.0)
            pool.memset(bx[:, :, 0:HIST], 0.0)
            after(pool, "dve", ("cols", 2))
            exts = ext[:, :, EP:EW].rearrange("p m (b e) -> p m b e", b=NB)
            bxs = bx[:, :, EP:EW].rearrange("p m (b e) -> p m b e", b=NB)
            pool.memset(bxs[:, :, :, 0:1], 0.0)
            for m in range(12):
                pool.tensor_copy(exts[:, m, :, 0:HIST], colsA[:, m, 0:24].rearrange("p (b j) -> p b j", b=NB))
            for m in range(4):
                ins = pool.tensor_copy(bxs[:, m, :, 1:HIST], colsB[:, m, 0:16].rearrange("p (b j) -> p b j", b=NB))
            result("pool", "hist", ins)
            after(pool, "act", ("ext", 11))
            after(pool, "dve", ("bx", 3))
            s27 = stg.rearrange("p (m r) -> p m r", m=12)
            s18 = stgb.rearrange("p (m r) -> p m r", m=4)
            pool.tensor_copy(s27[:, :, 0:3], ext[:, :, EP - 3:EP])
            for m in range(12):
                pool.tensor_copy(s27[:, m, 3:27].rearrange("p (b j) -> p b j", b=NB), exts[:, m, :, ES - 3:ES])
            pool.tensor_copy(s18[:, :, 0:2], bx[:, :, EP - 2:EP])
            for m in range(4):
                ins = pool.tensor_copy(s18[:, m, 2:18].rearrange("p (b j) -> p b j", b=NB), bxs[:, m, :, ES - 2:ES])
            result("pool", "stg", ins)
            after(pool, "pool", "stg")
            after(pool, "dve", ("conv", 11))
            for h in range(H):
                pool.dma_start(states[:, :, h, :], I["state_a_ssm"][0, :, h].rearrange("b k v -> k b v"))\
                    .then_inc(ld_states, 16)
            after(pool, "act", ("so", 3))
            for src, dst in ((stout[0:3, 0:1536], O["aconv_p"][0, 0]),
                             (stout[3:27, 0:1536], O["aconv_s"][0].rearrange("b j n -> (b j) n")),
                             (stout[0:2, 1536:2048], O["bconv_p"][0, 0]),
                             (stout[2:18, 1536:2048], O["bconv_s"][0].rearrange("b j n -> (b j) n"))):
                pool.dma_start(dst, src).then_inc(sent, 16)
            after(pool, "dve", ("s", 1))
            pool.dma_start(O["ssm_p"][0, 0].rearrange("h k v -> k h v"), S0).then_inc(sent, 16)
            after(pool, "dve", ("ds", H - 1, 1))
            for h in range(H):
                pool.dma_start(O["ssm_s"][0, :, h].rearrange("b k v -> k b v"), states[:, :, h, :]).then_inc(sent, 16)
            pool.wait_ge(sent, 16 * 9)
            result("pool", "mixer0", pool.memset(stat[:, 0, 7:8], 0.0))
            after(pool, "dve", "x02")
            pool.dma_start(A1["msk"], I["amasks"]).then_inc(ld_amask, 16)
            load_router(pool, 1, ld_router1)

            def load_cache(b):
                kv = [I[n][0, b].rearrange("(a p) h d -> p a (h d)", p=P) for n in ("cache_c_k", "cache_c_v")]
                if b >= 1:
                    after(pool, "act", ("kt", b - 1, 1))
                    after(pool, "dve", ("kt", b - 1, 3))
                pool.dma_start(Kc, kv[0]).then_inc(ld_kc, 16)
                if b >= 2:
                    after(pool, "dve", ("sout", b - 2))
                pool.dma_start(Vc[:, b % 2], kv[1]).then_inc(ld_vc[b % 2], 16)

            load_cache(0)
            result("pool", "qbd0", pool.memset(A1["qbd"], 0.0))
            after(pool, "pool", "qbd0")
            for i in range(6):
                t = i // 2
                a, n = TT[t]
                if i % 2 == 1:
                    after(pool, "act", ("ktok", i))
                    if t < 2:
                        dst = O["ck_p"][0, 0, a:a + n].rearrange("t h d -> t (h d)")
                    else:
                        dst = O["ck_s"][0].rearrange("b t h d -> (b t) (h d)")
                    pool.dma_start(dst, ktok[0:n, t % 2, :]).then_inc(ktok_sent if t == 0 else sent, 16)
            after(pool, "dve", ("vt", 5))
            for t, (a, n) in enumerate(TT):
                if t < 2:
                    dst = O["cv_p"][0, 0, a:a + n].rearrange("t h d -> t (h d)")
                else:
                    dst = O["cv_s"][0].rearrange("b t h d -> (b t) (h d)")
                pool.dma_start(dst, vtok[0:n, t, :]).then_inc(sent, 16)
            for b in range(NB):
                if b >= 2:
                    after(pool, "dve", ("smax", b - 2))
                for e in range(2):
                    r = slice(64 * e, 64 * e + 64)
                    cells = qbd[r, b % 2, :].rearrange("p (c w) -> p c w", w=P + 16)[:, :, 8 * e:8 * e + LS]
                    ins = pool.tensor_copy(cells, qkvT[r, 0:C, NP_ + LS * b:NP_ + LS * b + LS])
                result("pool", ("qbd", b), ins)
                after(pool, "pool", ("qbd", b))
                if b + 1 < NB:
                    load_cache(b + 1)
            pool.wait_ge(sent, 16 * 14)
            result("pool", "mixer1", pool.memset(stat[:, 1, 7:8], 0.0))
            for t, (a, n) in enumerate(TT):
                after(pool, "act", ("yt", 2 * t + 1))
                dst = O["y_p"][0, a:a + n] if t < 2 else O["y_s"].rearrange("b t d -> (b t) d")
                pool.dma_start(dst, ytok[0:n, t, :]).then_inc(sent, 16)
            pool.wait_ge(sent, 16 * 17)
            pool.wait_ge(ktok_sent, 16)

        @block.tensor
        def _(pe):
            def I_(n):
                return K("ident")[0:n, 0:n]

            def transposes(k, parts):
                claim(pe, k)
                for (a, b), src in parts:
                    ins = pe.transpose(B(k)[0:src.shape[1], a:b], src, I_(src.shape[0]))
                filled(ins, k)

            def project(name, n, rhs):
                for m in range(n):
                    project_chunk(name, m, tile_of[name] + m, rhs)

            def project_chunk(name, m, k, rhs):
                u = unit_of[name] + m // 2
                if m % 2 == 0:
                    need_unit(pe, u)
                claim(pe, k)
                for c in range(C):
                    w = slot(u)[:, c, P * (m % 2):P * (m % 2) + P]
                    ins = pe.matmul(B(k)[:, 0:T], w, rhs(c), start=(c == 0), stop=(c == C - 1))
                filled(ins, k)

            def norm_sum(tag, c):
                k = tile_of[f"norm{tag}"]
                if c == 0:
                    claim(pe, k)
                after(pe, "act", (f"sq{tag}", c))
                ins = pe.matmul(B(k)[:, 0:T], K("ones"), scratch[:, c, :], start=(c == 0), stop=(c == C - 1))
                if c == C - 1:
                    filled(ins, k)

            def project_out(l, rhs):
                for m in range(C):
                    project_chunk(f"out{l}", m, tile_of[f"out{l}"] + m, rhs)
                    if m >= 2:
                        norm_sum(f"{l}2", m - 2)
                norm_sum(f"{l}2", C - 2)
                norm_sum(f"{l}2", C - 1)

            def norm(tag):
                if tag[1:] != "2":
                    for c in range(C):
                        norm_sum(tag, c)
                after(pe, "act", f"hp{tag}")
                if tag != "f":
                    after(pe, "dve", f"hs{tag}")

            def ada_step(what, l, u):
                k = tile_of[what, l, u]
                if what == "turn":
                    after(pe, "act", ("row", l, u))
                    transposes(k, [((NCOND * i, NCOND * i + NCOND), modrow(l, u)[:, P * i:P * i + P]) for i in range(2)])
                    return
                claim(pe, k)
                need_unit(pe, ada_unit(l, u))
                for c in range(C):
                    ins = pe.matmul(B(k)[0:NCOND, 0:256], condT[:, c, :], slot(ada_unit(l, u))[:, c, :],
                                    start=(c == 0), stop=(c == C - 1))
                filled(ins, k)

            def head():
                for what, *i in steps_of("head", "pe"):
                    k = tile_of[(what, *i)]
                    if what == "cols":
                        rows, n, m = ((rowsM0, 26, C), (rowsA0, 28, 12), (rowsB0, 19, 4))[i[0]]
                        if i[0] == 0:
                            pe.wait_ge(ld_const, 16)
                            pe.wait_ge(ld_rowsM, 16 * NROWSM)
                        else:
                            pe.wait_ge(ld_rows, 16 * NROWS)
                        transposes(k, [((n * c, n * c + n), rows[:, P * c:P * c + P]) for c in range(m)])
                    elif what == "x":
                        c, = i
                        pe.wait_ge(ld_x, 48)
                        transposes(k, [((a, a + n), xload[0:n, t, P * c:P * c + P]) for t, (a, n) in enumerate(TT)])
                    else:
                        if (what, *i) == ("row", 0, 0):
                            after(pe, "act", ("cond",))
                        ada_step(what, *i)

            def mixer0():
                def four(k, n, lhs, rhs):
                    claim(pe, k)
                    for h in range(H):
                        ins = pe.matmul(B(k)[0:n, n * h:n * h + n], lhs(h), rhs(h), start=True, stop=True)
                    filled(ins, k)

                def spread(k, col, up, n):
                    claim(pe, k)
                    for h in range(H):
                        ins = pe.matmul(B(k)[:, n * h:n * h + n], col[0:n, h:h + 1].to_broadcast([n, P]), up,
                                        start=True, stop=True)
                    filled(ins, k)

                def spread_tokens(k, col):
                    claim(pe, k)
                    for t, (a, n) in enumerate(TT):
                        ins = pe.matmul(B(k)[:, a:a + n], col(t, n).to_broadcast([n, P]), I_(n), start=True, stop=True)
                    filled(ins, k)

                def token_sums(k, sq, m):
                    claim(pe, k)
                    for t, (a, n) in enumerate(TT):
                        for j in range(m):
                            ins = pe.matmul(B(k)[0:n, m * t + j:m * t + j + 1], sq[:, j, a:a + n], K("ones")[:, 0:1],
                                            start=True, stop=True)
                    filled(ins, k)

                for what, *i in steps_of("mixer0", "pe"):
                    k = tile_of[(what, *i)]
                    t = i[-1] if i else 0
                    a, n = TT[t] if t < 3 else TT[0]
                    up = K("upto") if n == P else K("upto_s", NS)
                    if what in ("row", "turn"):
                        ada_step(what, *i)
                    elif what == "ab":
                        pe.wait_ge(ld_small, 16 * NSMALL)
                        claim(pe, k)
                        for t, (a, n) in enumerate(TT):
                            for c in range(C):
                                ins = pe.matmul(B(k)[0:n, 8 * t:8 * t + 8], hT[:, c, a:a + n], wab[:, c, :],
                                                start=(c == 0), stop=(c == C - 1))
                        filled(ins, k)
                    elif what == "in":
                        project_chunk("in", i[0], k, lambda c: hT[:, c, :])
                    elif what == "gcol":
                        after(pe, "dve", ("g",))
                        claim(pe, k)
                        for t, (a, n) in enumerate(TT):
                            up, af = (K("upto"), K("after")) if t < 2 else (K("upto_s", NS), K("after_s", NS))
                            pe.matmul(B(k)[0:n, 8 * t:8 * t + 4], up, gg[0:n, t, :], start=True, stop=True)
                            ins = pe.matmul(B(k)[0:n, 8 * t + 4:8 * t + 8], af, gg[0:n, t, :], start=True, stop=True)
                        filled(ins, k)
                    elif what == "grow":
                        spread(k, gg[:, t, :], up, n)
                    elif what == "l2ss":
                        after(pe, "act", ("sq", 7))
                        token_sums(k, scratch, 8)
                    elif what == "l2bc":
                        after(pe, "dve", ("l2r",))
                        spread_tokens(k, lambda t, n, m=i[0]: l2col[0:n, t, m:m + 1])
                    elif what == "brow":
                        spread(k, beta[:, t, :], I_(n), n)
                    elif what == "vt":
                        after(pe, "act", ("cv", 11))
                        transposes(k, [((P * h, P * h + P), cT[:, 8 + h, a:a + n]) for h in range(H)])
                    elif what == "kt":
                        after(pe, "dve", ("qn", 7))
                        transposes(k, [((P * h, P * h + P), cT[:, 4 + h, a:a + n]) for h in range(H)])
                    elif what in ("at", "qk"):
                        after(pe, "dve", ("kb", 2))
                        rhs = kb if what == "at" else cT
                        four(k, n, lambda h: cT[:, 4 + h, a:a + n], lambda h: rhs[:, h, a:a + n])
                    elif what == "xt0":
                        after(pe, "dve", ("xt1", t))
                        transposes(k, [((n * h, n * h + n), XT[0:n, t, h, 0:n]) for h in range(H)])
                    elif what == "P":
                        after(pe, "dve", ("lt", *i))
                        if i[0] == 2:
                            after(pe, "act", ("x0", t))
                        four(k, n, lambda h: LT[0:n, t, h, 0:n], lambda h: X[0:n, t, h, 0:n])
                    elif what == "XPt":
                        after(pe, "act", ("pb", *i))
                        four(k, n, lambda h: PB[0:n, t, h, 0:n], lambda h: XT[0:n, t, h, 0:n])
                    elif what == "XP":
                        four(k, n, lambda h: XT[0:n, t, h, 0:n], lambda h: PB[0:n, t, h, 0:n])
                    elif what == "u":
                        after(pe, "dve", ("r", t) if t else ("xi", 64, 1))
                        claim(pe, k)
                        for h in range(H):
                            ins = pe.matmul(B(k)[0:n, P * h:P * h + P], XT[0:n, t, h, 0:n],
                                            (RR if t else vb)[0:n, t, h, :], start=True, stop=True)
                        filled(ins, k)
                    elif what == "kS" and t == 1:
                        after(pe, "dve", ("s", 0))
                        claim(pe, k)
                        for h in range(H):
                            ins = pe.matmul(B(k)[0:n, P * h:P * h + P], cT[:, 4 + h, a:a + n], S0[:, h, :],
                                            start=True, stop=True)
                        filled(ins, k)
                    elif what == "kS":
                        after(pe, "dve", ("ktm",))
                        pe.wait_ge(ld_states, 64)
                        claim(pe, k)
                        for h in range(H):
                            for b in range(NB):
                                ins = pe.matmul(B(k)[0:n, P * h:P * h + P], kTm[:, h, b, :], states[:, b, h, :],
                                                start=(b == 0), stop=(b == NB - 1))
                        filled(ins, k)
                    elif what == "o":
                        after(pe, "act", ("u", t))
                        claim(pe, k)
                        for h in range(H):
                            o = B(k)[:, n * h:n * h + n]
                            ins = pe.matmul(o, uu[0:n, t, h, :], qkg[0:n, t, h, 0:n], start=True, stop=(t != 1))
                            if t == 1:
                                ins = pe.matmul(o, S0[:, h, :], qd[:, h, a:a + n], start=False, stop=True)
                            if t == 2:
                                for b in range(NB):
                                    ins = pe.matmul(o[:, LS * b:LS * b + LS], states[:, b, h, :],
                                                    qd[:, h, a + LS * b:a + LS * b + LS], start=False, stop=True,
                                                    skip_group_check=True)
                        filled(ins, k)
                    elif what == "s":
                        claim(pe, k)
                        for h in range(H):
                            ins = pe.matmul(B(k)[:, P * h:P * h + P], kd[0:n, t, h, :], uu[0:n, t, h, :],
                                            start=True, stop=True)
                        filled(ins, k)
                    elif what == "ds":
                        h, j = i
                        after(pe, "dve", ("ue", h))
                        claim(pe, k)
                        filled(pe.matmul(B(k)[:, 0:512], kd[0:NS, 2, h, :],
                                         ue[:, 4 * j:4 * j + 4, :].rearrange("p b v -> p (b v)"),
                                         start=True, stop=True), k)
                    elif what == "st":
                        after(pe, "pool", "stg")
                        j0 = i[0]
                        transposes(k, [((P * j, P * j + P), stg[:, 27 * (4 * j0 + j):27 * (4 * j0 + j) + 27] if j0 < 3
                                        else stgb[:, 18 * j:18 * j + 18]) for j in range(4)])
                    elif what == "onss":
                        after(pe, "act", ("osq",))
                        token_sums(k, osq, H)
                    elif what == "onbc":
                        after(pe, "dve", ("onr",))
                        spread_tokens(k, lambda t, n, h=i[0]: oncol[0:n, t, h:h + 1])
                after(pe, "dve", ("cat",))
                project_out(0, lambda c: catT[:, c, :])

            def mixer1():
                project("qkv", 24, lambda c: hT[:, c, :])
                after(pe, "act", ("qkv", 23))
                for name, m0 in (("ktok", 8), ("vtok", 16)):
                    for i in range(6):
                        a, n = TT[i // 2]
                        transposes(tile_of[name] + i, [((P * j, P * j + P), qkvT[:, m0 + 4 * (i % 2) + j, a:a + n])
                                                       for j in range(4)])
                for what, *i in steps_of("mixer1", "pe"):
                    k = tile_of[(what, *i)]
                    n = i[0]
                    u = n % 2
                    if what in ("row", "turn"):
                        ada_step(what, *i)
                    if what == "S":
                        c, r = n // 2, slice(64 * u, 64 * u + 64)
                        claim(pe, k)
                        pe.matmul(B(k)[:, 0:128], qkvT[r, c, 0:128], qkvT[r, 8 + c, 0:128], start=True, stop=True)
                        filled(pe.matmul(B(k)[:, 128:384], qkvT[r, c, 128:256], qkvT[r, 8 + c, 0:256],
                                         start=True, stop=True), k)
                    elif what == "T":
                        after(pe, "dve", ("apr", n))
                        transposes(k, [((P * j, P * j + P), prb[:, u, P * j:P * j + P]) for j in range(3)])
                    elif what == "O":
                        if n == 0:
                            after(pe, "dve", ("vt", 5))
                        if u == 0:
                            claim(pe, k)
                        after(pe, "act", ("apT", n))
                        r = slice(64 * u, 64 * u + 64)
                        v = slice(64 * n, 64 * n + 64)
                        pe.matmul(B(k)[r, 0:128], vtok[:, 0, v], pT[:, u, 0:128], start=True, stop=True)
                        pe.matmul(B(k)[r, 128:256], vtok[:, 0, v], pT[:, u, 128:256], start=True, stop=False)
                        ins = pe.matmul(B(k)[r, 128:256], vtok[:, 1, v], pT[:, u, 256:384], start=False, stop=True)
                        if u == 1:
                            filled(ins, k)
                    elif what == "K":
                        pe.wait_ge(ld_kc, 16 * (n + 1))
                        transposes(k, [((256 * j + P * a_, 256 * j + P * a_ + P),
                                        Kc[:, a_, P * (2 * i[1] + j):P * (2 * i[1] + j) + P])
                                       for j in range(2) for a_ in range(2)])
                    elif what == "Ss":
                        after(pe, "act", ("kt", n, 1))
                        after(pe, "dve", ("kt", n, 3))
                        after(pe, "pool", ("qbd", n))
                        claim(pe, k)
                        for c in range(C):
                            pe.matmul(B(k)[:, 0:256], qbd[:, u, P * c:P * c + P], KT[:, c, :],
                                      start=(c == 0), stop=(c == C - 1))
                        for c in range(C):
                            ins = pe.matmul(B(k)[:, 256:320], qbd[:, u, P * c:P * c + P], qkvT[:, 8 + c, NP_:T],
                                            start=(c == 0), stop=(c == C - 1))
                        filled(ins, k)
                    elif what == "Ts":
                        after(pe, "dve", ("spr", n))
                        claim(pe, k)
                        for j in range(2):
                            pe.transpose(B(k)[:, P * j:P * j + P], prbS[:, u, P * j:P * j + P], I_(P))
                        filled(pe.transpose(B(k)[0:NS, 256:384], prbS[:, u, 256:320], I_(P)), k)
                    elif what == "Os":
                        after(pe, "act", ("spT", n))
                        pe.wait_ge(ld_vc[u], 16 * (n // 2 + 1))
                        claim(pe, k)
                        for c in range(C):
                            o = B(k)[:, 16 * c:16 * c + 16]
                            q = slice(16 * c, 16 * c + 16)
                            for a_ in range(2):
                                pe.matmul(o, Vc[:, u, a_, P * c:P * c + P], pTS[:, u, P * a_:P * a_ + P][:, q],
                                          start=(a_ == 0), stop=False)
                            ins = pe.matmul(o, vtok[0:NS, 2, P * c:P * c + P], pTS[0:NS, u, 256:384][:, q],
                                            start=False, stop=True)
                        filled(ins, k)
                after(pe, "act", ("aout", 7))
                after(pe, "dve", ("sout", NB - 1))
                project_out(1, lambda c: attnT[:, c, :])

            def router(l):
                k = tile_of[f"rt{l}"]
                if l == 1:
                    pe.wait_ge(ld_router1, 64)
                claim(pe, k)
                for t, (a, n) in enumerate(TT):
                    for c in range(C):
                        ins = pe.matmul(B(k)[0:n, 36 * t:36 * t + 36], hT[:, c, a:a + n], wr[l][:, c, :],
                                        start=(c == 0), stop=(c == C - 1))
                filled(ins, k)
                for i in range(6):
                    a, n = TT[i // 2]
                    transposes(tile_of[f"ht{l}"] + i, [((P * j, P * j + P), hT[:, 4 * (i % 2) + j, a:a + n])
                                                       for j in range(4)])
                k = tile_of[f"rk{l}"]
                after(pe, "dve", f"oh{l}")
                claim(pe, k)
                for t, (a, n) in enumerate(TT):
                    for t2 in range(t + 1):
                        n2 = TT[t2][1]
                        m = K("ones", n2)[:, 0:n] if t2 < t else K("upto", n)[:, 0:n]
                        pe.matmul(B(k)[0:n, 4 * t:4 * t + 4], m, onehot[0:n2, t2, :], start=(t2 == 0), stop=(t2 == t))
                for t, (a, n) in enumerate(TT):
                    ins = pe.matmul(B(k)[:, 16:20], K("ones", n), onehot[0:n, t, :], start=(t == 0), stop=(t == 2))
                filled(ins, k)

            def expert_pass(S, i, units_at, unit_wait):
                pe.wait_ge(S["perm"], i + 1)
                for a in range(12):
                    n = 12 * i + a
                    bk = bank[5 + a % 2]
                    if n >= 2:
                        pe.wait_ge(S["auxfree"], n - 1)
                    if a < 4:
                        for t, (x, m) in enumerate(TT):
                            ins = pe.transpose(bk[:, x:x + m], perm[0:m, t, a, :], I_(m))
                    else:
                        for t, (x, m) in enumerate(TT):
                            ins = pe.matmul(bk[:, :], htok[0:m, t, P * (a - 4):P * (a - 4) + P],
                                            perm[0:m, t, :, :].rearrange("p g s -> p (g s)"),
                                            start=(t == 0), stop=(t == 2))
                    ins.then_inc(S["aux"], 1)
                for g in range(NG):
                    for t, (x, m) in enumerate(TT):
                        ins = pe.matmul(bank[7][:, NE * g:NE * g + NE], perm[0:m, t, g, :],
                                        gates[0:m, t, NE * g:NE * g + NE], start=(t == 0), stop=(t == 2))
                ins.then_inc(S["gsl"], 1)
                pe.wait_ge(S["auxfree"], 12 * i + 12)

                for g in range(NG):
                    with pe.Fori(0, 2) as j:
                        def gate_up(u, w):
                            k0 = 32 * i + 8 * g + u
                            if w == 0:
                                pe.wait_ge(S["hid"], 4 * j + (k0 + 1))
                            unit_wait(g, u, w, j)
                            wt = units_at(g, u, w)
                            for c in range(C):
                                ins = pe.matmul(bank[u % 2 + 5 * w][:, 0:256], hg[:, c, P * g:P * g + P],
                                                wt[:, c, :], start=(c == 0), stop=(c == C - 1))
                            ins.then_inc(S["gu"], 1)

                        def turn(u):
                            pe.wait_ge(S["hid"], 4 * j + (32 * i + 8 * g + u + 3))
                            for f in range(2):
                                ins = pe.transpose(bank[2][:, 256 * (u % 2) + P * f:256 * (u % 2) + P * f + P],
                                                   hid[:, u % 2, P * f:P * f + P], I_(P))
                            ins.then_inc(S["tr"], 1)

                        def down(u):
                            if u == 0:
                                pe.wait_ge(S["yadd"], j + (8 * i + 2 * g + 1))
                            pe.wait_ge(S["hidT"], 4 * j + (32 * i + 8 * g + u + 1))
                            unit_wait(g, u, 2, j)
                            wt = units_at(g, u, 2)
                            for d in range(2):
                                for f in range(2):
                                    ins = pe.matmul(bank[3 + d][:, :], hidT[:, u % 2, f, :], wt[:, f, 512 * d:512 * d + 512],
                                                    start=(u == 0 and f == 0), stop=(u == 3 and f == 1))
                            ins.then_inc(S["down"], 1)

                        gate_up(0, 0)
                        gate_up(0, 1)
                        for u in range(1, 4):
                            gate_up(u, 0)
                            turn(u - 1)
                            gate_up(u, 1)
                            down(u - 1)
                        turn(3)
                        down(3)
                pe.wait_ge(S["yadd"], 8 * i + 9)
                for m in range(C):
                    n = 8 * i + m
                    if m >= 2 or i:
                        pe.wait_ge(S["scfree"], n - 1)
                    for g in range(NG):
                        ins = pe.matmul(bank[5 + m % 2][:, 0:T], ys[:, g, P * m:P * m + P], permT[:, g, :],
                                        start=(g == 0), stop=(g == NG - 1))
                    ins.then_inc(S["sc"], 1)

            def experts(l):
                k = tile_of[f"rk{l}"] + 1
                for b in range(NBANK):
                    claim(pe, k + b)
                base = unit_of[f"moe{l}"]

                def at_(g, u, w):
                    return slot(base + 24 * g + 3 * u + w, D if w == 2 else 256)

                def wait(g, u, w, j):
                    n = base + 24 * g + 3 * u + w
                    pe.wait_ge(unit_loaded[n % R], 16 * (12 // R) * j + 16 * (n // R + 1))

                expert_pass(moe, l, at_, wait)
                S = more[l]
                after(pe, "dve", f"flag{l}")
                v = pe.value_load(flag[:, :], min_val=0, max_val=1)
                with pe.If(v >= 1):
                    for i in range(2):
                        def at2(g, u, w):
                            return ring2[:, w, :].rearrange("p (c n) -> p c n", n=D if w == 2 else 256)

                        def wait2(g, u, w, j, i=i):
                            pe.wait_ge(S[f"wl{w}"], 64 * j + 16 * (32 * i + 8 * g + u + 1))

                        expert_pass(S, i, at2, wait2)
                after(pe, "dve", f"x{l}2")

            head()
            for l in range(2):
                norm(f"{l}1")
                if l == 0:
                    mixer0()
                else:
                    mixer1()
                norm(f"{l}2")
                router(l)
                experts(l)
            norm("f")
            for i in range(6):
                a, n = TT[i // 2]
                transposes(tile_of["y"] + i, [((P * j, P * j + P), hT[:, 4 * (i % 2) + j, a:a + n]) for j in range(4)])
        def samples(ap):
            return ap.rearrange("p (b t) -> p b t", b=NB)

        def sequences(flat):
            return flat[:, EP:EW].rearrange("p (b e) -> p b e", b=NB)[:, :, 0:LS]

        @block.scalar
        def _(act):
            steps = [0]

            def link(ins):
                steps[0] += 1
                ins.then_inc(astep, 1)
                act.wait_ge(astep, steps[0])

            act.dma_start(const[:, :], I["masks"]).then_inc(ld_const, 16)
            for t, (a, n) in enumerate(TT):
                src = I["x_prompt"][0, a:a + n] if t < 2 else I["x_sample"].rearrange("b t d -> (b t) d")
                act.dma_start(xload[0:n, t, :], src).then_inc(ld_x, 16)
            for dst, src in ((rowsA0[0:24], I["state_a_conv"][0].rearrange("b j n -> (b j) n")),
                             (rowsA0[24:28], I["conv_a_w"][0]),
                             (rowsB0[0:16], I["state_b_conv"][0].rearrange("b j n -> (b j) n")),
                             (rowsB0[16:19], I["conv_b_w"][0])):
                act.dma_start(dst, src).then_inc(ld_rows, 16)
            with nc.allow_non_contiguous_dma(reason="a column of 128 gains"):
                act.dma_start(colsO[:, :], I["o_gain_a"].rearrange("a p -> p a")).then_inc(ld_small, 16)
            act.dma_start(wab[:, :, :], I["w_in_even"][0].rearrange("(c p) n -> p c n", p=P)[:, :, 2048:2056])\
               .then_inc(ld_small, 16)
            act.dma_start(dtb[:, 0, :], I["dt_bias"][0:1].to_broadcast([P, 4])).then_inc(ld_small, 16)
            act.dma_start(dtb[:, 1, :], I["a_log"][0:1].to_broadcast([P, 4])).then_inc(ld_small, 16)
            load_router(act, 0, ld_small)

            def copy(dst, src):
                return act.activation(dst, src, ACT.Copy)

            def norm(tag, k):
                if tag == "12":
                    after(act, "pool", "mixer1")
                for c in range(C):
                    after(act, "dve", {"01": ("x", c), "02": ("xo0", c), "11": "x02", "12": ("xo1", c), "f": "x12"}[tag])
                    result("act", (f"sq{tag}", c), act.activation(scratch[:, c, :], xT[:, c, :], ACT.Square))
                full(act, k)
                result("act", f"std{tag}", act.activation(rstd[:, :], B(k)[:, 0:T], ACT.Sqrt, scale=1.0 / D,
                                                          bias=K("eps")))
                if tag == "02":
                    after(act, "pool", "mixer0")
                for c in range(C):
                    if c % 4 == 0:
                        after(act, "dve", f"xn{tag}" if c else f"xa{tag}")
                    if tag == "f":
                        ins = act.activation(hT[:, c, :], scratch[:, c, :], ACT.Copy, scale=cols[:, c, 4:5])
                    else:
                        j = 0 if tag[1] == "1" else 3
                        ins = act.activation(hT[:, c, 0:NP_], scratch[:, c, 0:NP_], ACT.Identity,
                                             scale=gainA[:, c, 0:1], bias=mod[:, int(tag[0]), j, c, 0:1])
                result("act", f"hp{tag}", ins)

            def ada_row(l, u):
                k = tile_of["row", l, u]
                full(act, k)
                if (l, u) != (0, 0) and (l, u) != (0, 1):
                    v = 24 * l + u - 2
                    full(act, tile_of["turn", v // 24, v % 24])
                result("act", ("row", l, u), copy(modrow(l, u), B(k)[0:NCOND, 0:256]))

            def mixer0():
                exts = ext[:, :, EP:EW].rearrange("p m (b e) -> p m b e", b=NB)
                after(act, "pool", "hist")

                def heads(ap, n):
                    return ap[0:n, 0:H * n].rearrange("p (h i) -> p h i", h=H)

                for what, *i in steps_of("mixer0", "act"):
                    step = (what, *i)
                    t = i[-1] if i else 0
                    a, n = TT[t] if t < 3 else TT[0]
                    if what == "row":
                        ada_row(*i)
                    elif what == "gea":
                        after(act, "dve", ("gabs",))
                        link(act.activation(sc8[:, :, 4:8], sc8[:, :, 0:4], ACT.Exp, scale=-1.0))
                        link(act.activation(sc8[:, :, 4:8], sc8[:, :, 4:8], ACT.Ln, bias=K("one")))
                        result("act", step, act.activation(dtb[:, 1, :], dtb[:, 1, :], ACT.Exp))
                    elif what == "geb":
                        result("act", step, act.activation(sc8[:, :, 8:12], gab[:, :, 4:8], ACT.Exp, scale=-1.0))
                    elif what == "ext":
                        m, = i
                        k = tile_of["in", m]
                        full(act, k)
                        copy(ext[:, m, HIST:EP], B(k)[:, 0:NP_])
                        result("act", step, copy(exts[:, m, :, HIST:], samples(B(k)[:, NP_:T])))
                    elif what == "z":
                        k = tile_of["in", i[0]]
                        full(act, k)
                        result("act", step, act.activation(zT[:, i[0] - 12, :], B(k)[:, 0:T], ACT.Silu))
                    elif what == "gt":
                        m, = i
                        k = tile_of["in", m]
                        full(act, k)
                        result("act", step, copy(bg[:, m - 16, :] if m < 20 else cg[:, m - 20, :], B(k)[:, 0:T]))
                    elif what == "cv":
                        v, = i
                        after(act, "dve", ("conv", v))
                        acc = convacc[:, v % 2, :]
                        act.activation(cT[:, v, 0:NP_], acc[:, 0:NP_], ACT.Silu)
                        result("act", step, act.activation(samples(cT[:, v, NP_:T]), sequences(acc), ACT.Silu))
                    elif what == "sq":
                        after(act, "act", ("cv", i[0]))
                        result("act", step, act.activation(scratch[:, i[0], :], cT[:, i[0], :], ACT.Square))
                    elif what == "egc":
                        after(act, "dve", ("gcol",))
                        result("act", step, act.activation(egc[:, :, :], gcols[:, :, :], ACT.Exp))
                    elif what == "eG":
                        k = tile_of["grow", t]
                        full(act, k)
                        result("act", step, act.activation(eG[:, :, a:a + n], B(k)[:, 0:H * n]
                                                           .rearrange("p (h i) -> p h i", h=H), ACT.Exp))
                    elif what == "ge":
                        after(act, "dve", ("gd", 2))
                        act.activation(gam[:, 0:2, :, :], gam[:, 0:2, :, :], ACT.Exp)
                        result("act", step, act.activation(gam[0:NS, 2, :, 0:NS], gam[0:NS, 2, :, 0:NS], ACT.Exp))
                    elif what in ("l2s", "ons"):
                        k, col, m, scale = ((tile_of["l2ss",], l2col, 8, 1.0) if what == "l2s" else
                                            (tile_of["onss",], oncol, H, 1.0 / P))
                        full(act, k)
                        act.activation(col[:, 0:2, :], B(k)[:, 0:2 * m].rearrange("p (t m) -> p t m", t=2), ACT.Sqrt,
                                       bias=K("eps"), scale=scale)
                        result("act", step, act.activation(col[0:NS, 2, :], B(k)[0:NS, 2 * m:3 * m], ACT.Sqrt,
                                                           bias=K("eps", NS), scale=scale))
                    elif what == "x0":
                        k = tile_of["xt0", t]
                        full(act, k)
                        result("act", step, copy(X[0:n, t, :, 0:n], heads(B(k), n)))
                    elif what == "pb":
                        k = tile_of["P", i[0], t]
                        full(act, k)
                        result("act", step, copy(PB[0:n, t, :, 0:n], heads(B(k), n)))
                    elif what == "u":
                        k = tile_of["u", t]
                        full(act, k)
                        result("act", step, copy(uu[0:n, t, :, :], B(k)[0:n, :].rearrange("p (h v) -> p h v", h=H)))
                    elif what == "so":
                        k = tile_of["st", i[0]]
                        full(act, k)
                        n = 27 if i[0] < 3 else 18
                        result("act", step, copy(stout[0:n, 512 * i[0]:512 * i[0] + 512], B(k)[0:n, :]))
                    elif what == "osq":
                        after(act, "dve", ("o", 2))
                        after(act, "dve", ("o", 1))
                        after(act, "dve", ("catb", 3))
                        result("act", step, act.activation(osq, oT, ACT.Square))

            def mixer1():
                for m in range(24):
                    k = tile_of["qkv"] + m
                    full(act, k)
                    result("act", ("qkv", m), copy(qkvT[:, m, :], B(k)[:, 0:T]))
                for i in range(6):
                    k = tile_of["ktok"] + i
                    n = TT[i // 2][1]
                    full(act, k)
                    if i == 4:
                        act.wait_ge(ktok_sent, 16)
                    result("act", ("ktok", i), copy(ktok[0:n, i // 2 % 2, 512 * (i % 2):512 * (i % 2) + 512], B(k)[0:n, :]))
                for what, *i in steps_of("mixer1", "act"):
                    step = (what, *i)
                    n = i[0]
                    u = n % 2
                    if what == "row":
                        ada_row(*i)
                    if what == "aexp":
                        after(act, "dve", ("amax", n))
                        act.activation(prb[:, u, 0:128], scr[:, u, 0:128], ACT.Exp, bias=stat[:, u, 2:3], scale=0.125)
                        result("act", step, act.activation(prb[:, u, 128:384], scr[:, u, 128:384], ACT.Exp,
                                                           bias=stat[:, u, 3:4], scale=0.125))
                    elif what == "apT":
                        k = tile_of["T", n]
                        full(act, k)
                        result("act", step, copy(pT[:, u, :], B(k)[:, 0:384]))
                    elif what == "aout":
                        k = tile_of["O", 2 * n]
                        full(act, k)
                        result("act", step, copy(attnT[:, n, 0:NP_], B(k)[:, 0:NP_]))
                    elif what == "kt":
                        k = tile_of["K", n, i[1]]
                        full(act, k)
                        if n:
                            full(act, tile_of["Ss", n - 1])
                        result("act", step, copy(KT[:, 2 * i[1]:2 * i[1] + 2, :],
                                                 B(k)[:, :].rearrange("p (c j) -> p c j", c=2)))
                    elif what == "sexp":
                        after(act, "dve", ("smax", n))
                        result("act", step, act.activation(prbS[:, u, 0:T], scrS[:, u, 0:T], ACT.Exp,
                                                           bias=statS[:, u, 2:3], scale=0.125))
                    elif what == "spT":
                        k = tile_of["Ts", n]
                        full(act, k)
                        copy(pTS[:, u, 0:256], B(k)[:, 0:256])
                        result("act", step, copy(pTS[0:NS, u, 256:384], B(k)[0:NS, 256:384]))

            def expert_pass(S, i):
                for a in range(12):
                    act.wait_ge(S["aux"], 12 * i + a + 1)
                    src = bank[5 + a % 2]
                    if a < 4:
                        ins = copy(permT[:, a, :], src[:, 0:T])
                    else:
                        ins = copy(hg[:, a - 4, :], src[:, :])
                    ins.then_inc(S["auxfree"], 1)
                for g in range(NG):
                    with act.Fori(0, 2) as j:
                        def silu(u):
                            act.wait_ge(S["gu"], 8 * j + (2 * (32 * i + 8 * g + u) + 1))
                            act.activation(sg[:, u % 2, :], bank[u % 2][:, 0:256], ACT.Silu).then_inc(S["silu"], 1)

                        def turn(u):
                            act.wait_ge(S["tr"], 4 * j + (32 * i + 8 * g + u + 1))
                            copy(hidT[:, u % 2, :, :].rearrange("p f s -> p (f s)"),
                                 bank[2][:, 256 * (u % 2):256 * (u % 2) + 256]).then_inc(S["hidT"], 1)

                        silu(0)
                        for u in range(1, 4):
                            silu(u)
                            turn(u - 1)
                        turn(3)

            def experts(l):
                for i in range(6):
                    k = tile_of[f"ht{l}"] + i
                    n = TT[i // 2][1]
                    full(act, k)
                    result("act", (f"ht{l}", i), copy(htok[0:n, i // 2, 512 * (i % 2):512 * (i % 2) + 512], B(k)[0:n, :]))
                after(act, "dve", f"rm{l}")
                result("act", f"re{l}", act.activation(rt[:, 60:72], rt[:, 48:60], ACT.Exp))
                after(act, "dve", f"rt2{l}")
                result("act", f"re2{l}", act.activation(rt[:, 303:306], rt[:, 300:303], ACT.Exp))
                expert_pass(moe, l)
                after(act, "dve", f"flag{l}")
                v = act.value_load(flag[:, :], min_val=0, max_val=1)
                with act.If(v >= 1):
                    for i in range(2):
                        expert_pass(more[l], i)

            for what, *i in steps_of("head", "act"):
                if what == "cond":
                    after(act, "dve", ("cols", 0))
                    result("act", ("cond",), act.activation(condT[:, :, :], cols[:, :, 17:26], ACT.Silu))
                else:
                    ada_row(*i)
            for l in range(2):
                norm(f"{l}1", tile_of[f"norm{l}1"])
                (mixer0 if l == 0 else mixer1)()
                norm(f"{l}2", tile_of[f"norm{l}2"])
                experts(l)
            norm("f", tile_of["normf"])
            for i in range(6):
                k = tile_of["y"] + i
                n = TT[i // 2][1]
                full(act, k)
                result("act", ("yt", i), copy(ytok[0:n, i // 2, 512 * (i % 2):512 * (i % 2) + 512], B(k)[0:n, :]))

        @block.vector
        def _(dve):
            steps = [0]

            def link(ins):
                steps[0] += 1
                ins.then_inc(vstep, 1)
                dve.wait_ge(vstep, steps[0])

            def mul(out, a, b):
                return dve.tensor_tensor(out, a, b, ALU.mult)

            def add(out, a, b):
                return dve.tensor_tensor(out, a, b, ALU.add)

            def stt(out, a, s, b, op0, op1, **kw):
                return dve.scalar_tensor_tensor(out, a, s, b, op0, op1, **kw)

            def b3(ap, n):
                return ap.unsqueeze(len(ap.shape)).to_broadcast(list(ap.shape) + [n])

            def mid(ap, n):
                s = list(ap.shape)
                return ap.unsqueeze(2).to_broadcast([s[0], s[1], n, s[2]])

            def norm(tag, k):
                if tag != "f":
                    l = int(tag[0])
                    j = 0 if tag[1] == "1" else 3
                    gi = l if tag[1] == "1" else 2 + l
                    stt(gainA[:, :, :], mod[:, l, j + 1, :, :], 1.0, cols[:, :, gi:gi + 1].to_broadcast([P, C, NCOND]),
                        ALU.add, ALU.mult)
                after(dve, "act", f"std{tag}")
                link(dve.reciprocal(rstd[:, :], rstd[:, :]))
                for res, c in (("xa", 0), ("xn", C // 2)):
                    half = slice(c, c + C // 2)
                    result("dve", f"{res}{tag}", mul(scratch[:, half, :], xT[:, half, :],
                                                     rstd[:, :].unsqueeze(1).to_broadcast([P, C // 2, T])))
                if tag == "f":
                    return
                after(dve, "dve", f"xn{tag}")
                for c in range(C):
                    ins = mul(samples(hT[:, c, NP_:T]), samples(scratch[:, c, NP_:T]), b3(gainA[:, c, 1:NCOND], LS))
                link(ins)
                for c in range(C):
                    ins = add(samples(hT[:, c, NP_:T]), samples(hT[:, c, NP_:T]), b3(mod[:, l, j, c, 1:NCOND], LS))
                result("dve", f"hs{tag}", ins)

            def residual(l, m, ps, gate):
                stt(xT[:, m, 0:NP_], ps[:, 0:NP_], mod[:, l, gate, m, 0:1], xT[:, m, 0:NP_], ALU.mult, ALU.add)
                tmp = rstd[:, NS * (m % 4):NS * (m % 4) + NS]
                return tmp, mul(samples(tmp), samples(ps[:, NP_:T]), b3(mod[:, l, gate, m, 1:NCOND], LS))

            def mod_step(l, u):
                k = tile_of["turn", l, u]
                full(dve, k)
                j, c0 = u // 4, 2 * (u % 4)
                bias = cols[:, c0:c0 + 2, 5 + 6 * l + j:6 + 6 * l + j].to_broadcast([P, 2, NCOND])
                result("dve", ("mod", l, u), add(mod[:, l, j, c0:c0 + 2, :],
                                                 B(k)[:, 0:2 * NCOND].rearrange("p (c n) -> p c n", c=2), bias))

            def mixer0():
                bxs = bx[:, :, EP:EW].rearrange("p m (b e) -> p m b e", b=NB)

                def system(k, n):
                    return B(k)[0:n, 0:H * n].rearrange("p (h i) -> p h i", h=H)

                def level(s, n):
                    return K(f"lev{s}", n)[:, 0:n].unsqueeze(1).to_broadcast([n, H, n])

                def heads(ap):
                    return ap.rearrange("p (h v) -> p h v", h=H)

                for what, *i in steps_of("mixer0", "dve"):
                    step = (what, *i)
                    t = i[-1] if i else 0
                    a, n = TT[t] if t < 3 else TT[0]
                    if what == "mod":
                        mod_step(*i)
                    elif what == "gab":
                        k = tile_of["ab",]
                        dve.memset(gcols[:, :, :], 0.0)
                        link(dve.memset(gab[:, :, :], 0.0))
                        dve.wait_ge(ld_small, 16 * NSMALL)
                        full(dve, k)
                        dve.tensor_copy(gab[:, 0:2, :], B(k)[:, 0:16].rearrange("p (t n) -> p t n", t=2))
                        result("dve", step, dve.tensor_copy(gab[0:NS, 2, :], B(k)[0:NS, 16:24]))
                    elif what == "gabs":
                        after(dve, "dve", ("gab",))
                        link(add(sc8[:, :, 12:16], gab[:, :, 0:4], dtb[:, 0:1, :].to_broadcast([P, 3, 4])))
                        link(dve.tensor_scalar(sc8[:, :, 8:12], sc8[:, :, 12:16], -1.0, None, ALU.mult))
                        result("dve", step, dve.tensor_tensor(sc8[:, :, 0:4], sc8[:, :, 12:16], sc8[:, :, 8:12], ALU.max))
                    elif what == "gmax":
                        result("dve", step, dve.tensor_scalar(gg[:, :, :], sc8[:, :, 12:16], 0.0, None, ALU.max))
                    elif what == "g":
                        after(dve, "act", ("geb",))
                        link(add(gg[:, :, :], gg[:, :, :], sc8[:, :, 4:8]))
                        link(dve.tensor_scalar(sc8[:, :, 8:12], sc8[:, :, 8:12], 1.0, None, ALU.add))
                        dve.reciprocal(beta[:, :, :], sc8[:, :, 8:12])
                        result("dve", step, stt(gg[:, :, :], gg[:, :, :], -1.0, dtb[:, 1:2, :].to_broadcast([P, 3, 4]),
                                                ALU.mult, ALU.mult))
                    elif what == "conv":
                        m, = i
                        if m == 0:
                            after(dve, "pool", "hist")
                        after(dve, "act", ("ext", m))
                        if m >= 2:
                            after(dve, "act", ("cv", m - 2))
                        o = convacc[:, m % 2, :]
                        link(dve.tensor_scalar(o[:, 0:CW], ext[:, m, 0:CW], colsA[:, m, 24:25], None, ALU.mult))
                        for j in range(1, 4):
                            ins = stt(o[:, 0:CW], ext[:, m, j:j + CW], colsA[:, m, 24 + j:25 + j], o[:, 0:CW],
                                      ALU.mult, ALU.add)
                            if j < 3:
                                link(ins)
                        result("dve", step, ins)
                    elif what == "bx":
                        m, = i
                        k = tile_of["in", 24 + m]
                        after(dve, "act", ("gt", 20 + m))
                        full(dve, k)
                        mul(bx[:, m, HIST:EP], B(k)[:, 0:NP_], cg[:, m, 0:NP_])
                        result("dve", step, mul(bxs[:, m, :, HIST:], samples(B(k)[:, NP_:T]), samples(cg[:, m, NP_:T])))
                    elif what == "catb":
                        m, = i
                        after(dve, "dve", ("bx", 3) if m == 0 else ("catb", m - 1))
                        o = bconv[:, m % 2, :]
                        link(dve.tensor_scalar(o[:, 0:CW], bx[:, m, 1:1 + CW], colsB[:, m, 16:17], None, ALU.mult))
                        for j in range(1, 3):
                            link(stt(o[:, 0:CW], bx[:, m, 1 + j:1 + j + CW], colsB[:, m, 16 + j:17 + j], o[:, 0:CW],
                                     ALU.mult, ALU.add))
                        mul(catT[:, 4 + m, 0:NP_], o[:, 0:NP_], bg[:, m, 0:NP_])
                        result("dve", step, mul(samples(catT[:, 4 + m, NP_:T]), sequences(o), samples(bg[:, m, NP_:T])))
                    elif what in ("l2r", "onr"):
                        col, src = (l2col, "l2s") if what == "l2r" else (oncol, "ons")
                        after(dve, "act", (src,))
                        dve.reciprocal(col[:, 0:2, :], col[:, 0:2, :])
                        result("dve", step, dve.reciprocal(col[0:NS, 2, :], col[0:NS, 2, :]))
                    elif what == "qn":
                        m, = i
                        k = tile_of["l2bc", m]
                        full(dve, k)
                        ps = B(k)[:, 0:T]
                        result("dve", step, stt(cT[:, m, :], cT[:, m, :], float(P) ** -0.5, ps, ALU.mult, ALU.mult)
                               if m < 4 else mul(cT[:, m, :], cT[:, m, :], ps))
                    elif what == "gcol":
                        k = tile_of["gcol",]
                        full(dve, k)
                        dve.tensor_copy(gcols[:, 0:2, :], B(k)[:, 0:16].rearrange("p (t n) -> p t n", t=2))
                        result("dve", step, dve.tensor_copy(gcols[0:NS, 2, :], B(k)[0:NS, 16:24]))
                    elif what == "gd":
                        k = tile_of["grow", t]
                        after(dve, "dve", ("gcol",))
                        full(dve, k)
                        after(dve, "act", ("eG", t))
                        for h in range(H):
                            ins = dve.tensor_scalar(gam[0:n, t, h, 0:n], B(k)[0:n, n * h:n * h + n],
                                                    gcols[0:n, t, h:h + 1], 0.0, ALU.subtract, ALU.min)
                        result("dve", step, ins)
                    elif what == "gam":
                        after(dve, "act", ("ge",))
                        for t, (a, n) in enumerate(TT):
                            m_ = K("upto") if t < 2 else K("upto_s", NS)
                            ins = mul(gam[0:n, t, :, 0:n], gam[0:n, t, :, 0:n], m_.unsqueeze(1).to_broadcast([n, H, n]))
                        result("dve", step, ins)
                    elif what == "kb":
                        k = tile_of["brow", t]
                        full(dve, k)
                        after(dve, "dve", ("qn", 7))
                        result("dve", step, mul(kb[:, :, a:a + n], cT[:, 4:8, a:a + n],
                                                B(k)[:, 0:H * n].rearrange("p (h i) -> p h i", h=H)))
                    elif what == "vb":
                        k = tile_of["vt", t]
                        full(dve, k)
                        result("dve", step, mul(vb[0:n, t, :, :], heads(B(k)[0:n, :]), b3(beta[0:n, t, :], P)))
                    elif what == "nbe":
                        after(dve, "act", ("egc",))
                        result("dve", step, stt(nbe[:, :, :], egc[:, :, 0:4], -1.0, beta[:, :, :], ALU.mult, ALU.mult))
                    elif what == "kd":
                        k = tile_of["kt", t]
                        full(dve, k)
                        result("dve", step, mul(kd[0:n, t, :, :], heads(B(k)[0:n, :]), b3(egc[0:n, t, 4:8], P)))
                    elif what == "at":
                        k = tile_of["at", t]
                        after(dve, "dve", ("gam",))
                        full(dve, k)
                        result("dve", step, mul(AT[0:n, t, :, 0:n], system(k, n), gam[0:n, t, :, 0:n]))
                    elif what == "xt1":
                        after(dve, "dve", ("at", t))
                        link(mul(XT[0:n, t, :, 0:n], AT[0:n, t, :, 0:n], level(1, n)))
                        result("dve", step, dve.tensor_tensor(
                            XT[0:n, t, :, 0:n], K("ident", n)[:, 0:n].unsqueeze(1).to_broadcast([n, H, n]),
                            XT[0:n, t, :, 0:n], ALU.subtract))
                    elif what == "qkg":
                        k = tile_of["qk", t]
                        full(dve, k)
                        result("dve", step, mul(qkg[0:n, t, :, 0:n], system(k, n), gam[0:n, t, :, 0:n]))
                    elif what == "qd":
                        result("dve", step, mul(qd, cT[:, 0:4, :], eG))
                    elif what == "lt":
                        result("dve", step, mul(LT[0:n, t, :, 0:n], AT[0:n, t, :, 0:n], level(i[0], n)))
                    elif what == "xt":
                        k = tile_of["XPt", i[0], t]
                        full(dve, k)
                        full(dve, k + 1)
                        result("dve", step, dve.tensor_tensor(XT[0:n, t, :, 0:n], XT[0:n, t, :, 0:n],
                                                              system(k, n), ALU.subtract))
                    elif what == "xi":
                        k = tile_of["XP", i[0], t]
                        if i[0] == 2:
                            after(dve, "act", ("x0", t))
                        result("dve", step, dve.tensor_tensor(X[0:n, t, :, 0:n], X[0:n, t, :, 0:n],
                                                              system(k, n), ALU.subtract))
                        after(dve, "dve", step)
                    elif what == "ktm":
                        link(dve.memset(kTm, 0.0))
                        for h in range(H):
                            own = arena[:, AT_AT + NB * NS * h:AT_AT + NB * NS * h + NB * (NS + LS)]
                            ins = dve.tensor_copy(own.rearrange("p (b w) -> p b w", b=NB)[:, :, 0:LS],
                                                  samples(cT[:, 4 + h, NP_:T]))
                        result("dve", step, ins)
                    elif what == "r":
                        k = tile_of["kS", t]
                        full(dve, k)
                        after(dve, "dve", ("vb", t))
                        for h in range(H):
                            ins = stt(RR[0:n, t, h, :], B(k)[0:n, P * h:P * h + P], nbe[0:n, t, h:h + 1],
                                      vb[0:n, t, h, :], ALU.mult, ALU.add)
                        result("dve", step, ins)
                    elif what == "o":
                        k = tile_of["o", t]
                        full(dve, k)
                        result("dve", step, dve.tensor_copy(oT[:, :, a:a + n],
                                                            B(k)[:, 0:H * n].rearrange("p (h i) -> p h i", h=H)))
                    elif what == "s" and t == 0:
                        k = tile_of["s", 0]
                        full(dve, k)
                        result("dve", step, dve.tensor_copy(S0, heads(B(k)[:, :])))
                    elif what == "s":
                        k = tile_of["s", 1]
                        full(dve, k)
                        after(dve, "dve", ("s", 0))
                        for h in range(H):
                            ins = stt(S0[:, h, :], S0[:, h, :], eG[:, h, 255:256], B(k)[:, P * h:P * h + P],
                                      ALU.mult, ALU.add)
                        result("dve", step, ins)
                    elif what == "ue":
                        h, = i
                        after(dve, "act", ("u", 2))
                        full(dve, tile_of["o", 2])
                        if h:
                            full(dve, tile_of["ds", h - 1, 1])
                        mul(ue, uu[0:NS, 2, h, :].unsqueeze(1).to_broadcast([NS, NB, P]), b3(K("batch_rows", NS), P))
                        dec = eG[:, h, NP_ + LS - 1:T:LS]
                        result("dve", step, mul(states[:, :, h, :], states[:, :, h, :], b3(dec, P)))
                    elif what == "ds":
                        h, j = i
                        k = tile_of["ds", h, j]
                        after(dve, "dve", ("ue", h))
                        full(dve, k)
                        st = states[:, 4 * j:4 * j + 4, h, :]
                        result("dve", step, add(st, st, B(k)[:, :].rearrange("p (b v) -> p b v", b=4)))
                    elif what == "on":
                        h, = i
                        k = tile_of["onbc", h]
                        full(dve, k)
                        result("dve", step, mul(oT[:, h, :], oT[:, h, :], B(k)[:, 0:T]))
                    elif what == "cat":
                        after(dve, "dve", ("on", H - 1))
                        result("dve", step, stt(catT[:, 0:4, :], oT, colsO[:, 0:1], zT, ALU.mult, ALU.mult))

            def mixer1():
                for i in range(6):
                    k = tile_of["vtok"] + i
                    n = TT[i // 2][1]
                    full(dve, k)
                    result("dve", ("vt", i), dve.tensor_copy(vtok[0:n, i // 2, 512 * (i % 2):512 * (i % 2) + 512], B(k)[0:n, :]))
                dve.wait_ge(ld_amask, 16)
                for what, *i in steps_of("mixer1", "dve"):
                    step = (what, *i)
                    n = i[0]
                    u = n % 2
                    if what == "mod":
                        mod_step(*i)
                    if what == "amax":
                        k = tile_of["S", n]
                        full(dve, k)
                        link(add(scr[:, u, :], B(k)[:, 0:384], KA("neg_prompt")))
                        dve.tensor_reduce(stat[:, u, 0:1], scr[:, u, 0:128], AX.X, ALU.max)
                        link(dve.tensor_reduce(stat[:, u, 1:2], scr[:, u, 128:384], AX.X, ALU.max))
                        result("dve", step, dve.tensor_scalar(stat[:, u, 2:4], stat[:, u, 0:2], -0.125, None, ALU.mult))
                    elif what == "apr":
                        after(dve, "act", ("aexp", n))
                        for r, (x, y) in enumerate(((0, 128), (128, 384))):
                            ins = stt(prb[:, u, x:y], prb[:, u, x:y], 1.0, KA("cnt_prompt")[:, x:y], ALU.mult, ALU.mult,
                                      accum_out=stat[:, u, 4 + r:5 + r])
                        link(ins)
                        link(dve.reciprocal(stat[:, u, 4:6], stat[:, u, 4:6]))
                        dve.tensor_scalar(prb[:, u, 0:128], prb[:, u, 0:128], stat[:, u, 4:5], None, ALU.mult)
                        result("dve", step, dve.tensor_scalar(prb[:, u, 128:384], prb[:, u, 128:384],
                                                              stat[:, u, 5:6], None, ALU.mult))
                    elif what == "kt":
                        k = tile_of["K", n, i[1]]
                        full(dve, k)
                        if n:
                            full(dve, tile_of["Ss", n - 1])
                        result("dve", step, dve.tensor_copy(KT[:, 2 * i[1]:2 * i[1] + 2, :],
                                                            B(k)[:, :].rearrange("p (c j) -> p c j", c=2)))
                    elif what == "smax":
                        k = tile_of["Ss", n]
                        full(dve, k)
                        add(scrS[:, u, 0:256], B(k)[:, 0:256], KA("neg_cache"))
                        link(add(scrS[:, u, 256:320], B(k)[:, 256:320], KA("neg_new")[:, 56 - LS * n:120 - LS * n]))
                        link(dve.tensor_reduce(statS[:, u, 0:1], scrS[:, u, 0:T], AX.X, ALU.max))
                        result("dve", step, dve.tensor_scalar(statS[:, u, 2:3], statS[:, u, 0:1], -0.125, None, ALU.mult))
                    elif what == "spr":
                        after(dve, "act", ("sexp", n))
                        stt(prbS[:, u, 0:256], prbS[:, u, 0:256], 1.0, KA("cnt_cache"), ALU.mult, ALU.mult,
                            accum_out=statS[:, u, 4:5])
                        link(stt(prbS[:, u, 256:320], prbS[:, u, 256:320], 1.0,
                                 KA("cnt_new")[:, 56 - LS * n:120 - LS * n], ALU.mult, ALU.mult,
                                 accum_out=statS[:, u, 5:6]))
                        link(add(statS[:, u, 6:7], statS[:, u, 4:5], statS[:, u, 5:6]))
                        link(dve.reciprocal(statS[:, u, 6:7], statS[:, u, 6:7]))
                        result("dve", step, dve.tensor_scalar(prbS[:, u, 0:T], prbS[:, u, 0:T], statS[:, u, 6:7],
                                                              None, ALU.mult))
                    elif what == "sout":
                        k = tile_of["Os", n]
                        full(dve, k)
                        a = NP_ + LS * n
                        for e in range(2):
                            r = slice(64 * e, 64 * e + 64)
                            ins = dve.tensor_copy(attnT[r, :, a:a + LS],
                                                  B(k)[r, 0:128].rearrange("p (c q) -> p c q", c=C)[:, :, LS * e:LS * e + LS])
                        result("dve", step, ins)

            def router(l):
                k = tile_of[f"rt{l}"]
                lg = small[:, :, 0:36]
                full(dve, k)
                dve.tensor_copy(small[:, 0:2, 0:36], B(k)[:, 0:72].rearrange("p (t n) -> p t n", t=2))
                result("dve", f"rt{l}", dve.tensor_copy(small[0:NS, 2, 0:36], B(k)[0:NS, 72:108]))
                after(dve, "dve", f"rt{l}")
                if l == 1:
                    dve.wait_ge(ld_router1, 64)
                link(add(lg, lg, br[l][:, :].unsqueeze(1).to_broadcast([P, 3, 36])))
                lg4 = small[:, :, 0:4]

                def v3(a, n):
                    return rt[:, a:a + 3 * n].rearrange("p (t n) -> p t n", t=3)

                iota = K("iota8")

                def first_of(out, vals, top, tmp, topv, n):
                    link(dve.tensor_reduce(top, vals, AX.X, ALU.max))
                    link(dve.tensor_tensor(tmp, vals, b3(top, n), ALU.is_equal))
                    link(mul(tmp, tmp, iota[:, 0:n].unsqueeze(1).to_broadcast([P, 3, n])))
                    link(dve.tensor_reduce(topv, tmp, AX.X, ALU.max))
                    return dve.tensor_tensor(out, tmp, b3(topv, n), ALU.is_equal)

                gmax, tmp4, topv = rt[:, 0:3], v3(3, 4), rt[:, 15:18]
                oh_ins = first_of(onehot[:, :, :], lg4, gmax, tmp4, topv, 4)
                link(oh_ins)
                result("dve", f"rm{l}", dve.tensor_tensor(v3(48, 4), lg4, b3(gmax, 4), ALU.subtract))
                prod = rt[:, 100:196].rearrange("p (t g e) -> p t g e", t=3, g=NG)
                for t in range(3):
                    ins = mul(prod[:, t], small[:, t, 4:36].rearrange("p (g e) -> p g e", g=NG), b3(onehot[:, t, :], NE))
                result("dve", f"oh{l}", ins)
                after(dve, "dve", f"oh{l}")
                el, tmp8, oh1, oh2 = v3(200, 8), v3(224, 8), v3(248, 8), v3(272, 8)
                link(dve.tensor_reduce(el, prod.rearrange("p t g e -> p t e g"), AX.X, ALU.add))
                m1, m2 = rt[:, 296:299], rt[:, 309:312]
                link(first_of(oh1, el, m1, tmp8, topv, 8))
                link(stt(el, oh1, NEG, el, ALU.mult, ALU.add))
                link(first_of(oh2, el, m2, tmp8, topv, 8))
                result("dve", f"rt2{l}", dve.tensor_tensor(rt[:, 300:303], m2, m1, ALU.subtract))
                after(dve, "act", f"re2{l}")
                psum_, r_, w1, w2 = rt[:, 18:21], rt[:, 303:306], rt[:, 24:27], rt[:, 27:30]
                link(dve.tensor_reduce(psum_, v3(60, 4), AX.X, ALU.add))
                link(dve.tensor_scalar(w1, r_, 1.0, None, ALU.add))
                link(mul(w1, w1, psum_))
                link(dve.reciprocal(w1, w1))
                link(mul(w2, w1, r_))
                link(mul(oh1, oh1, b3(w1, 8)))
                link(mul(oh2, oh2, b3(w2, 8)))
                link(add(oh1, oh1, oh2))
                for t in range(3):
                    mul(gates[:, t, :].rearrange("p (g e) -> p g e", g=NG),
                        oh1[:, t, :].unsqueeze(1).to_broadcast([P, NG, NE]), b3(onehot[:, t, :], NE))
                k = tile_of[f"rk{l}"]
                link(dve.memset(rank[:, :, :], -2000.0))
                full(dve, k)
                dve.tensor_scalar(rank[:, 0:2, :], B(k)[:, 0:8].rearrange("p (t n) -> p t n", t=2), 1000.0, None, ALU.add)
                link(dve.tensor_scalar(rank[0:NS, 2, :], B(k)[0:NS, 8:12], 1000.0, None, ALU.add))
                link(mul(rank[:, :, :], rank[:, :, :], onehot[:, :, :]))
                dve.tensor_scalar(rank[:, :, :], rank[:, :, :], -1001.0, None, ALU.add)
                link(dve.tensor_reduce(rt[0:1, 30:31], B(k)[0:1, 16:20], AX.X, ALU.max))
                result("dve", f"flag{l}", dve.tensor_scalar(flag[:, :], rt[0:1, 30:31], SLOTS + 0.5, None, ALU.is_gt))

            def expert_pass(l, S, i, first, link):
                if not first:
                    link(dve.tensor_scalar(rank[:, :, :], rank[:, :, :], -float(SLOTS), None, ALU.add))
                for t in range(3):
                    ins = dve.tensor_tensor(perm[:, t, :, :], K("iota").unsqueeze(1).to_broadcast([P, NG, SLOTS]),
                                            b3(rank[:, t, :], SLOTS), ALU.is_equal)
                ins.then_inc(S["perm"], 1)
                link(dve.memset(AM["ys"], 0.0))
                dve.wait_ge(S["gsl"], i + 1)
                ins = dve.tensor_copy(gslot[:, :], bank[7][:, 0:NG * NE])
                if i == 0:
                    ins.then_inc(S["hid"], 2)
                    dve.wait_ge(S["hid"], 2)
                    dve.memset(stat[:, 0, 6:7], 0.0).then_inc(S["yadd"], 1)
                else:
                    link(ins)
                for g in range(NG):
                    with dve.Fori(0, 2) as j:
                        for u in range(4):
                            k0 = 32 * i + 8 * g + u
                            dve.wait_ge(S["silu"], 4 * j + (k0 + 1))
                            dve.wait_ge(S["gu"], 8 * j + 2 * (k0 + 1))
                            gate = gslot[:, bass.ds(4 * j + (8 * g + u), 1)]
                            stt(hid[:, u % 2, :], sg[:, u % 2, :], gate, bank[5 + u % 2][:, 0:256], ALU.mult, ALU.mult)\
                                .then_inc(S["hid"], 1)
                        dve.wait_ge(S["down"], 4 * j + (32 * i + 8 * g + 4))
                        dve.wait_ge(S["yadd"], j + (8 * i + 2 * g + 1))
                        add(ys[:, g, 0:512], ys[:, g, 0:512], bank[3][:, :])
                        add(ys[:, g, 512:1024], ys[:, g, 512:1024], bank[4][:, :]).then_inc(S["yadd"], 1)
                for m in range(C):
                    dve.wait_ge(S["sc"], 8 * i + m + 1)
                    ps = bank[5 + m % 2]
                    tmp, ins = residual(l, m, ps, 5)
                    ins.then_inc(S["scfree"], 1)
                    dve.wait_ge(S["scfree"], 8 * i + m + 1)
                    ins = add(xT[:, m, NP_:T], xT[:, m, NP_:T], tmp)
                link(ins)

            def experts(l):
                expert_pass(l, moe, l, True, link)
                S = more[l]
                v = dve.value_load(flag[:, :], min_val=0, max_val=1)
                with dve.If(v >= 1):
                    more_steps = [0]

                    def link2(ins):
                        more_steps[0] += 1
                        ins.then_inc(S["step"], 1)
                        dve.wait_ge(S["step"], more_steps[0])

                    for i in range(2):
                        expert_pass(l, S, i, False, link2)
                result("dve", f"x{l}2", dve.tensor_copy(stat[:, 0, 0:1], xT[:, C - 1, T - 1:T]))

            dve.memset(small[:, :, :], 0.0)
            for what, *i in steps_of("head", "dve"):
                step = (what, *i)
                if what == "mod":
                    mod_step(*i)
                    continue
                k = tile_of[step]
                full(dve, k)
                if what == "cols":
                    dst, n = ((cols, C), (colsA, 12), (colsB, 4))[i[0]]
                    w = dst.shape[2]
                    result("dve", step, dve.tensor_copy(dst[:, :, :], B(k)[:, 0:w * n].rearrange("p (c n) -> p c n", c=n)))
                else:
                    result("dve", step, dve.tensor_copy(xT[:, i[0], :], B(k)[:, 0:T]))
            for l in range(2):
                if l == 0:
                    after(dve, "dve", ("mod", 0, HEAD_UNITS - 1))
                norm(f"{l}1", tile_of[f"norm{l}1"])
                (mixer0 if l == 0 else mixer1)()
                for m in range(C):
                    k = tile_of[f"out{l}"] + m
                    full(dve, k)
                    tmp, ins = residual(l, m, B(k), 2)
                    link(ins)
                    result("dve", (f"xo{l}", m), add(xT[:, m, NP_:T], xT[:, m, NP_:T], tmp))
                after(dve, "dve", (f"xo{l}", C - 1))
                after(dve, "pool", f"mixer{l}")
                norm(f"{l}2", tile_of[f"norm{l}2"])
                router(l)
                experts(l)
                after(dve, "dve", f"x{l}2")
            norm("f", tile_of["normf"])

        assert made == {"dve": len(DVE_ORDER), "act": len(ACT_ORDER), "pool": len(POOL_ORDER)}, made


_INS = ["x_prompt", "x_sample", "state_a_ssm", "state_a_conv", "state_b_conv", "cache_c_k", "cache_c_v",
        "c_prompt", "c_sample", "w_ada", "b_ada", "norm1", "norm2", "norm_f", "w_in_even", "conv_a_w", "a_log",
        "dt_bias", "o_gain_a", "conv_b_w", "w_out_even", "w_qkv_odd", "w_out_odd", "w_router_group",
        "b_router_group", "w_router_expert", "b_router_expert", "w_exp_gate", "w_exp_up", "w_exp_down"]
_OUTS = {"y_p": (1, 256, 1024), "y_s": (8, 8, 1024), "ssm_p": (1, 1, 4, 128, 128), "ssm_s": (1, 8, 4, 128, 128),
         "aconv_p": (1, 1, 3, 1536), "aconv_s": (1, 8, 3, 1536), "bconv_p": (1, 1, 2, 512), "bconv_s": (1, 8, 2, 512),
         "ck_p": (1, 1, 256, 16, 64), "ck_s": (1, 8, 8, 16, 64), "cv_p": (1, 1, 256, 16, 64), "cv_s": (1, 8, 8, 16, 64)}


def kernel(**inputs):
    import numpy as _np
    import concourse.bacc as _bacc
    from concourse import mybir as _mybir
    from concourse.bass_utils import run_bass_kernel_spmd as _run

    nc = _bacc.Bacc("TRN2", target_bir_lowering=False, num_devices=1)
    given = {name: _np.ascontiguousarray(inputs[name]) for name in _INS}
    given["masks"] = packed(constants())
    given["amasks"] = packed(attention_constants())
    arrays = {f"in_{name}_dram": a for name, a in given.items()}
    ins = {name: nc.dram_tensor(f"in_{name}_dram", a.shape, _mybir.dt.from_np(a.dtype), kind="ExternalInput").ap()
           for name, a in given.items()}
    outs = {name: nc.dram_tensor(f"out_{name}_dram", shape, _mybir.dt.float32, kind="ExternalOutput").ap()
            for name, shape in _OUTS.items()}
    trunk_program(nc, ins, outs)
    r = _run(nc, [arrays], core_ids=[0])
    return tuple(r.results[0][f"out_{name}_dram"] for name in _OUTS)
```

```python
from contextlib import ExitStack

import numpy as np

import concourse.bass as bass
from concourse import mybir

F32 = mybir.dt.float32
F32R = mybir.dt.float32r
I32 = mybir.dt.int32
ALU = mybir.AluOpType
ACT = mybir.ActivationFunctionType
AX = mybir.AxisListType

P = 128
D = 1024
C = D // P
NP_, NS, NB = 256, 64, 8
LS = NS // NB
T = NP_ + NS
TT = [(0, 128), (128, 128), (256, 64)]
NCOND = 1 + NB
H = 4
HIST = 3
EP, ES = HIST + NP_, HIST + LS
EW = EP + NB * ES
CW = EW - HIST
EPS = 1e-6
NG, NE, DE = 4, 8, 256
SLOTS = 128
R = 6
U = 2048
NEG = -1e30
NBANK = 8
STREAM = [(0, 0), (0, 1), (1, 0), (1, 1), (0, 2), (2, 0), (2, 1), (1, 2), (3, 0), (3, 1), (2, 2), (3, 2)]
HALVES = 2 * len(STREAM)
NH = 3
PASS_HALVES = HALVES * NG * NE // 4
AT_HALF = {(u, w): 2 * p for p, (u, w) in enumerate(STREAM)}


def constants():
    i = np.arange(P)
    j = i[:, None]
    i = i[None, :]
    out = {"ident": j == i, "ones": np.ones((P, P)), "upto": j <= i, "after": j > i}
    for s in (1, 2, 4, 8, 16, 32, 64):
        out[f"lev{s}"] = (j // (2 * s) == i // (2 * s)) & (j // s % 2 == 0) & (i // s % 2 == 1)
    same = (j // LS == i // LS)[:, :NS]
    out["upto_s"] = same & (j <= i)[:, :NS]
    out["after_s"] = same & (j > i)[:, :NS]
    out["batch_rows"] = j // LS == np.arange(NB)[None, :]
    out["iota"] = np.broadcast_to(i, (P, P))
    out["iota8"] = np.broadcast_to(np.arange(8)[None, ::-1] + 1, (P, 8))
    out["eps"] = np.full((P, 1), EPS)
    out["one"] = np.ones((P, 1))
    return {k: np.asarray(v, np.float32) for k, v in out.items()}


def attention_constants():
    def count(d):
        return ((d >= 0) & (d <= 128)) * 1.0 + ((d >= 0) & (d <= 512) & (d % 4 == 0)) + ((d >= 0) & (d <= 2048) & (d % 16 == 0))
    p = np.arange(P)[:, None]
    k = np.arange(256)[None]
    col = np.arange(120)[None] - 56
    prompt = np.concatenate([count(p - k[:, :128]), count(p + 128 - k)], 1)
    cache = count(256 + p % LS - k)
    new = np.where((col >= 0) & (col < LS), count(p % LS - col), 0.0)
    out = {}
    for n, c in (("prompt", prompt), ("cache", cache), ("new", new)):
        out["cnt_" + n] = c
        out["neg_" + n] = np.where(c > 0, 0.0, NEG)
    return {k: np.asarray(v, np.float32) for k, v in out.items()}


def packed(tables):
    return np.ascontiguousarray(np.concatenate(list(tables.values()), 1))


def trunk_program(nc, I, O):
    at, n = {}, 0
    for k, v in constants().items():
        at[k] = (n, n + v.shape[1])
        n += v.shape[1]
    NCONST = n
    aat, n = {}, 0
    for k, v in attention_constants().items():
        aat[k] = (n, n + v.shape[1])
        n += v.shape[1]
    NACONST = n

    with ExitStack() as ctx:
        def sb(name, shape, dt=F32):
            return ctx.enter_context(nc.sbuf_tensor(name, shape, dt))

        def sem(name):
            return ctx.enter_context(nc.semaphore(name))

        ring = sb("ring", [P, R, U])
        const = sb("const", [P, NCONST])
        xT = sb("xT", [P, C, T])
        hT = sb("hT", [P, C, T])
        scratch = sb("scratch", [P, C, T])
        rstd = sb("rstd", [P, T])
        mod = sb("mod", [P, 2, 6, C, NCOND])
        gainA = sb("gainA", [P, C, NCOND])
        cols = sb("cols", [P, C, 26])
        condT = sb("condT", [P, C, NCOND])
        small = sb("small", [P, 3, 40])
        flag = sb("flag", [1, 1], I32)
        gates = sb("gates", [P, 3, NG * NE])
        tiny = sb("tiny", [P, 512])
        ARENA = 28080
        with nc.sbuf_tensor("arena", [P, ARENA], F32) as arena:
            pass
        BEFORE_PARTS = 11648
        sb("below_parts", [P, BEFORE_PARTS])
        hgh = sb("hgh", [P, C, NG * SLOTS], F32R)
        hgl = sb("hgl", [P, C, NG * SLOTS], F32R)
        hidTh = sb("hidTh", [P, 2, 2, SLOTS], F32R)
        hidTl = sb("hidTl", [P, 2, 2, SLOTS], F32R)
        wh = sb("wh", [P, NH, U // 2], F32R)
        wl = sb("wl", [P, NH, U // 2], F32R)
        sb("above_parts", [P, ARENA - BEFORE_PARTS - 2 * C * NG * SLOTS - 2 * 2 * 2 * SLOTS - NH * U])

        def K(name, rows=P):
            a, b = at[name]
            return const[0:rows, a:b]

        modrows = [x[0:NCOND, :].rearrange("p (u n) -> p u n", u=2) for x in
                   (hT[:, :, :].rearrange("p c t -> p (c t)")[:, 2048:2560], tiny[:, :])]

        def modrow(l, u):
            return modrows[l == 1 and u >= HEAD_UNITS][:, u % 2, :]

        def carve(spec, base=0, limit=ARENA):
            out, n = {}, base
            for name, size in spec:
                out[name] = arena[:, n:n + size]
                n += size
            assert n <= limit, n
            return out

        A0 = carve([("ext", 12 * EW), ("cT", 12 * T), ("z", 4 * T), ("bx", 4 * EW), ("bg", 4 * T),
                    ("cg", 4 * T), ("cat", 8 * T), ("gam", 12 * P), ("AT", 12 * P), ("X", 12 * P),
                    ("qkg", 12 * P), ("XT", 12 * P), ("LT", 12 * P), ("PB", 12 * P), ("vb", 12 * P)])
        AT_AT = 12 * EW + 12 * T + 4 * T + 4 * EW + 4 * T + 4 * T + 8 * T + 12 * P
        ext = A0["ext"].rearrange("p (m e) -> p m e", e=EW)
        states = A0["ext"][:, 0:NB * H * P].rearrange("p (b h v) -> p b h v", b=NB, h=H)
        cT = A0["cT"].rearrange("p (m t) -> p m t", t=T)
        zT = A0["z"].rearrange("p (m t) -> p m t", t=T)
        bx = A0["bx"].rearrange("p (m e) -> p m e", e=EW)
        bg = A0["bg"].rearrange("p (m t) -> p m t", t=T)
        cg = A0["cg"].rearrange("p (m t) -> p m t", t=T)
        catT = A0["cat"].rearrange("p (m t) -> p m t", t=T)

        def sysview(name):
            return A0[name].rearrange("p (t h i) -> p t h i", t=3, h=H)
        gam, AT, X, qkg, XT, LT, PB, vb = [sysview(x) for x in ("gam", "AT", "X", "qkg", "XT", "LT", "PB", "vb")]
        kd = scratch[:, :, :].rearrange("p c t -> p (c t)")[:, 0:12 * P].rearrange("p (t h i) -> p t h i", t=3, h=H)
        eG = A0["cat"][:, 0:H * T].rearrange("p (m t) -> p m t", t=T)
        kb = A0["LT"][:, 0:H * T].rearrange("p (m t) -> p m t", t=T)
        qd = cT[:, 0:H, :]
        uu, RR = LT, PB
        oT = cT[:, 0:H, :]
        kTm = arena[:, AT_AT:AT_AT + H * NB * NS].rearrange("p (h b i) -> p h b i", h=H, b=NB)
        ue = arena[0:NS, AT_AT + 2048:AT_AT + 3072].rearrange("p (b v) -> p b v", b=NB)
        convacc = arena[:, ARENA - 1024:ARENA - 1024 + 2 * EW].rearrange("p (u e) -> p u e", u=2)
        S0 = tiny[:, :].rearrange("p (h v) -> p h v", h=H)
        rowsA0 = arena[0:28, 20000:20000 + 1536]
        rowsB0 = arena[0:19, 21600:21600 + 512]
        rowsM0 = arena[0:26, 22200:22200 + D]
        xload = arena[:, 23300:23300 + 3 * D].rearrange("p (t d) -> p t d", t=3)
        colsA = sb("colsA", [P, 12, 28])
        colsB = sb("colsB", [P, 4, 19])
        colsO = sb("colsO", [P, 1])
        wab = sb("wab", [P, C, 8])
        dtb = sb("dtb", [P, 2, 4])
        wr = [sb("wr", [P, C, 36]), arena[:, 27200:27200 + C * 36].rearrange("p (c n) -> p c n", c=C)]
        br = [sb("br", [P, 36]), arena[:, 27500:27536]]
        gab = sb("gab", [P, 3, 8])
        gg = sb("gg", [P, 3, 4])
        sc8 = sb("sc8", [P, 3, 16])
        beta = sb("beta", [P, 3, 4])
        nbe = sb("nbe", [P, 3, 4])
        gcols = sb("gcols", [P, 3, 8])
        egc = sb("egc", [P, 3, 8])
        bconv = scratch[:, :, :].rearrange("p c t -> p (c t)")[:, 12 * P:12 * P + 2 * EW].rearrange("p (u e) -> p u e", u=2)
        osq = A0["bx"][:, 0:H * T].rearrange("p (m t) -> p m t", t=T)
        l2col = sb("l2col", [P, 3, 8])
        oncol = sb("oncol", [P, 3, H])
        onehot = sb("onehot", [P, 3, NG])
        stout = hT[:, :, :].rearrange("p c t -> p (c t)")[0:27, 0:2048]
        stg = tiny[:, 0:12 * 27]
        stgb = tiny[:, 324:324 + 4 * 18]

        QB = C * (P + 16)
        A1 = carve([("qkv", 24 * T), ("Kc", 2 * D), ("vtok", 3 * D), ("pTS", 2 * 384), ("scS", 2 * T),
                    ("msk", NACONST), ("gap", 16), ("Vc", 2 * 2 * D), ("KT", C * 256),
                    ("qbd", 2 * QB), ("sc", 2 * 384), ("pr", 2 * 384), ("pT", 2 * 384), ("prS", 2 * T)])
        hTh, hTl = [x[:, :, :].rearrange("p c s -> p (c s)")[:, 0:C * T].rearrange("p (c t) -> p c t", t=T)
                    for x in (hgh, hgl)]
        qkvT = A1["qkv"].rearrange("p (m t) -> p m t", t=T)
        vtok = A1["vtok"].rearrange("p (t d) -> p t d", t=3)
        ktok = scratch[:, :, :].rearrange("p c t -> p (c t)")[:, 0:2 * D].rearrange("p (u d) -> p u d", u=2)
        Kc = A1["Kc"].rearrange("p (a d) -> p a d", a=2)
        Vc = A1["Vc"].rearrange("p (u a d) -> p u a d", u=2, a=2)
        KT = A1["KT"].rearrange("p (c j) -> p c j", c=C)
        qbd = A1["qbd"].rearrange("p (u q) -> p u q", u=2)
        scr = A1["sc"].rearrange("p (u j) -> p u j", u=2)
        prb = A1["pr"].rearrange("p (u j) -> p u j", u=2)
        pT = A1["pT"].rearrange("p (u j) -> p u j", u=2)
        scrS, prbS, pTS = [A1[n].rearrange("p (u j) -> p u j", u=2) for n in ("scS", "prS", "pTS")]
        attnT = hT
        stat = sb("stat", [P, 2, 8])
        statS = sb("statS", [P, 2, 8])

        def KA(name):
            a, b = aat[name]
            return A1["msk"][:, a:b]

        AM = carve([("htok", 3 * D), ("perm", 3 * NG * SLOTS), ("permT", NG * T),
                    ("ys", NG * D), ("sg", 2 * DE), ("hid", 2 * DE), ("rt", 600)], limit=BEFORE_PARTS)
        htok = AM["htok"].rearrange("p (t d) -> p t d", t=3)
        perm = AM["perm"].rearrange("p (t g s) -> p t g s", t=3, g=NG)
        permT = AM["permT"].rearrange("p (g t) -> p g t", g=NG)
        ys = AM["ys"].rearrange("p (g d) -> p g d", g=NG)
        sg = AM["sg"].rearrange("p (u f) -> p u f", u=2)
        hid = AM["hid"].rearrange("p (u f) -> p u f", u=2)
        rt = AM["rt"]
        sumbuf = scratch[:, :, :].rearrange("p c t -> p (c t)")[:, 0:D]
        ytok = AM["htok"].rearrange("p (t d) -> p t d", t=3)
        rank = sb("rank", [P, 3, NG])
        gslot = sb("gslot", [P, NG * NE])

        bank = [ctx.enter_context(nc.psum_tensor(f"bank{i}", [P, 512], F32)) for i in range(NBANK)]

        tile_of, ntile = {}, 0

        def tiles(name, n):
            nonlocal ntile
            tile_of[name] = ntile
            ntile += n

        schedule = {"head": [], "mixer0": [], "mixer1": []}
        readers = {}
        LEVELS = [(s, [0, 1, 2] if s <= 4 else [0, 1]) for s in (2, 4, 8, 16, 32, 64)]

        def fills(part, step, *read_by):
            nonlocal ntile
            schedule[part].append(("pe", step))
            tile_of[step] = ntile
            readers[ntile] = list(read_by)
            ntile += 1

        def makes(part, who, *steps):
            schedule[part] += [(who, step) for step in steps]

        def steps_of(part, who):
            return [step for w, step in schedule[part] if w == who]

        def ada_rows(part, l, u):
            fills(part, ("row", l, u), ("act", ("row", l, u)))
            makes(part, "act", ("row", l, u))

        def ada_turn(part, l, u):
            fills(part, ("turn", l, u), ("dve", ("mod", l, u)))
            makes(part, "dve", ("mod", l, u))

        SPLIT_UNITS = [7, 12]
        def plan_head():
            fills("head", ("cols", 0), ("dve", ("cols", 0)))
            makes("head", "dve", ("cols", 0))
            makes("head", "act", ("cond",))
            for u in range(HEAD_UNITS):
                ada_rows("head", 0, u)
                if u >= 1:
                    ada_turn("head", 0, u - 1)
                if u == 2:
                    for i in (1, 2):
                        fills("head", ("cols", i), ("dve", ("cols", i)))
                        makes("head", "dve", ("cols", i))
                    for c in range(C):
                        fills("head", ("x", c), ("dve", ("x", c)))
                        makes("head", "dve", ("x", c))
                if u == 3:
                    fills("head", ("stats",), ("act", "std01"))
                    makes("head", "act", ("stats",))
                    makes("head", "dve", ("stats",))
            ada_turn("head", 0, HEAD_UNITS - 1)

        def plan_mixer0():
            M = "mixer0"

            def next_half(n):
                if n < 2 * SPLIT_UNITS[0]:
                    makes(M, "act", ("hi", 0, n))
                    makes(M, "dve", ("lo", 0, n))

            def project_in(m):
                fills(M, ("in", m), ("act", ("ext", m)) if m < 12 else ("act", ("z", m)) if m < 16
                      else ("act", ("gt", m)) if m < 24 else ("dve", ("bx", m - 24)))
                if m < 12:
                    makes(M, "act", ("ext", m))
                    makes(M, "dve", ("conv", m))
                elif m < 24:
                    makes(M, "act", ("z", m) if m < 16 else ("gt", m))
                else:
                    makes(M, "dve", ("bx", m - 24))
                if 2 <= m < 14:
                    makes(M, "act", ("cv", m - 2))
                if 2 <= m < 10:
                    makes(M, "act", ("sq", m - 2))
                next_half(m + 3)

            rest_units = [(0, u) for u in range(HEAD_UNITS, 24)] + [(1, u) for u in range(HEAD_UNITS)]
            done = {"in": 22, "unit": 0}

            def fill(n=1):
                for _ in range(n):
                    if done["in"] < 28:
                        project_in(done["in"])
                        done["in"] += 1
                        continue
                    i = done["unit"]
                    if i > len(rest_units):
                        return
                    if i:
                        ada_turn(M, *rest_units[i - 1])
                    if i < len(rest_units):
                        ada_rows(M, *rest_units[i])
                    if i < 4:
                        makes(M, "dve", ("catb", i))
                    if 4 <= i < 8:
                        fills(M, ("st", i - 4), ("act", ("so", i - 4)))
                        makes(M, "act", ("so", i - 4))
                    done["unit"] += 1

            for n in range(NH):
                next_half(n)
            for m in range(22):
                project_in(m)
                if m == 3:
                    fills(M, ("ab",), ("dve", ("gab",)))
                    makes(M, "dve", ("gab",), ("gabs",), ("gmax",))
                    makes(M, "act", ("gea",), ("geb",))
                if m == 5:
                    makes(M, "dve", ("g",))
                if m == 14:
                    fills(M, ("gcol",), ("dve", ("gcol",)))
                    makes(M, "dve", ("gcol",))
                    makes(M, "act", ("egc",))
                    for t in range(3):
                        fills(M, ("grow", t), ("act", ("eG", t)), ("dve", ("gd", t)))
                        makes(M, "act", ("eG", t))
                        makes(M, "dve", ("gd", t))
                    makes(M, "act", ("ge",))
                    makes(M, "dve", ("gam",))
                if m == 15:
                    fills(M, ("l2ss",), ("act", ("l2s",)))
                    makes(M, "act", ("l2s",))
                    makes(M, "dve", ("l2r",))
                if m in (16, 17):
                    for j in range(4 * (m - 16), 4 * (m - 16) + 4):
                        fills(M, ("l2bc", j), ("dve", ("qn", j)))
                        makes(M, "dve", ("qn", j))
                for at_m, tile, res in ((18, "brow", "kb"), (18, "vt", "vb"), (19, "kt", "kd"), (20, "at", "at"),
                                        (21, "qk", "qkg")):
                    if m == at_m:
                        if tile == "kt":
                            makes(M, "dve", ("nbe",))
                        for t in range(3):
                            fills(M, (tile, t), ("dve", (res, t)))
                            makes(M, "dve", (res, t))
                if m == 20:
                    makes(M, "dve", *[("xt1", t) for t in range(3)])
                if m == 21:
                    makes(M, "dve", ("qd",))
                    for t in range(3):
                        fills(M, ("xt0", t), ("act", ("x0", t)))
                        makes(M, "act", ("x0", t))
            for s, ts in LEVELS:
                makes(M, "dve", *[("lt", s, t) for t in ts])
                for t in ts:
                    fills(M, ("P", s, t), ("act", ("pb", s, t)))
                    makes(M, "act", ("pb", s, t))
                fill()
                for t in ts:
                    fills(M, ("XPt", s, t), ("dve", ("xt", s, t)))
                    fills(M, ("XP", s, t), ("dve", ("xi", s, t)))
                    makes(M, "dve", ("xt", s, t), ("xi", s, t))
                fill()
            makes(M, "dve", ("ktm",))

            def solve(t):
                fills(M, ("u", t), ("act", ("u", t)))
                makes(M, "act", ("u", t))

            def from_state(t):
                fills(M, ("kS", t), ("dve", ("r", t)))
                makes(M, "dve", ("r", t))

            def outputs(t):
                fills(M, ("o", t), ("dve", ("o", t)))
                makes(M, "dve", ("o", t))

            def prompt_state(t):
                fills(M, ("s", t), ("dve", ("s", t)))
                makes(M, "dve", ("s", t))

            def sample_states(h):
                makes(M, "dve", ("ue", h))
                for j in range(2):
                    fills(M, ("ds", h, j), ("dve", ("ds", h, j)))
                    makes(M, "dve", ("ds", h, j))

            solve(0)
            from_state(2)
            fill(3)
            outputs(0)
            prompt_state(0)
            solve(2)
            fill(3)
            from_state(1)
            outputs(2)
            fill(3)
            solve(1)
            sample_states(0)
            fill(3)
            outputs(1)
            prompt_state(1)
            makes(M, "act", ("osq",))
            sample_states(1)
            fill(3)
            fills(M, ("onss",), ("act", ("ons",)))
            makes(M, "act", ("ons",))
            makes(M, "dve", ("onr",))
            sample_states(2)
            fill(3)
            for h_ in range(H):
                fills(M, ("onbc", h_), ("dve", ("on", h_)))
                makes(M, "dve", ("on", h_))
            sample_states(3)
            fill(len(rest_units))
            makes(M, "dve", ("cat",))

        def plan_mixer1():
            M = "mixer1"
            for st in range(18):
                b = st // 2
                if st < 16:
                    fills(M, ("S", st), ("dve", ("amax", st)))
                    makes(M, "dve", ("amax", st))
                    makes(M, "act", ("aexp", st))
                if b < NB and st % 2 == 0:
                    for i in range(4):
                        fills(M, ("K", b, i), ("act" if i < 2 else "dve", ("kt", b, i)))
                if b < NB and st % 2 == 1:
                    fills(M, ("Ss", b), ("dve", ("smax", b)))
                if 1 <= st <= 16:
                    makes(M, "dve", ("apr", st - 1))
                    fills(M, ("T", st - 1), ("act", ("apT", st - 1)))
                    makes(M, "act", ("apT", st - 1))
                if b >= 1 and st % 2 == 0:
                    makes(M, "dve", ("spr", b - 1))
                    fills(M, ("Ts", b - 1), ("act", ("spT", b - 1)))
                    makes(M, "act", ("spT", b - 1))
                if b < NB and st % 2 == 0:
                    for i in range(4):
                        makes(M, "act" if i < 2 else "dve", ("kt", b, i))
                if b < NB and st % 2 == 1:
                    makes(M, "dve", ("smax", b))
                    makes(M, "act", ("sexp", b))
                if st >= 2:
                    h_ = st - 2
                    if h_ % 2 == 0:
                        fills(M, ("O", h_), ("act", ("aout", h_ // 2)))
                    else:
                        schedule[M].append(("pe", ("O", h_)))
                        tile_of["O", h_] = tile_of["O", h_ - 1]
                        makes(M, "act", ("aout", h_ // 2))
                if st < 17:
                    if HEAD_UNITS + st < 24:
                        ada_rows(M, 1, HEAD_UNITS + st)
                    if st:
                        ada_turn(M, 1, HEAD_UNITS + st - 1)
                if b >= 1 and st % 2 == 1:
                    fills(M, ("Os", b - 1), ("dve", ("sout", b - 1)))
                    makes(M, "dve", ("sout", b - 1))

        HEAD_UNITS = 8
        plan_head()
        tile_of["norm01"] = tile_of["stats",]
        for l in range(2):
            if l:
                tiles(f"norm{l}1", 1)
            if l == 0:
                plan_mixer0()
            else:
                tiles("qkv", 24)
                tiles("ktok", 6)
                tiles("vtok", 6)
                plan_mixer1()
            tiles(f"out{l}", C)
            tiles(f"norm{l}2", 1)
            tiles(f"rt{l}", 1)
            tiles(f"ht{l}", 6)
            tiles(f"rk{l}", 1)
        tiles("normf", 1)
        tiles("y", 6)

        bank_full = [sem(f"bank_full{i}") for i in range(NBANK)]

        def B(k):
            return bank[k % NBANK]

        def filled(ins, k):
            ins.then_inc(bank_full[k % NBANK], 1)

        def full(eng, k):
            eng.wait_ge(bank_full[k % NBANK], k // NBANK + 1)

        unit_of, nunit = {}, 0

        def units(name, n):
            nonlocal nunit
            unit_of[name] = nunit
            nunit += n

        units("ada0", HEAD_UNITS)
        units("in", 14)
        units("ada_rest", 24)
        units("out0", 4)
        units("moe0", 96)
        units("qkv", 12)
        units("ada_late", 24 - HEAD_UNITS)
        units("out1", 4)
        units("moe1", 96)
        
        unit_loaded = [sem(f"unit_loaded{i}") for i in range(R)]

        def ada_unit(l, u):
            n = 24 * l + u
            if n < HEAD_UNITS:
                return unit_of["ada0"] + n
            return unit_of["ada_rest"] + n - HEAD_UNITS if n < HEAD_UNITS + 24 else unit_of["ada_late"] + n - HEAD_UNITS - 24

        def need_unit(pe, n):
            pe.wait_ge(unit_loaded[n % R], 16 * (n // R + 1))

        def slot(n, width=256):
            return ring[:, n % R, :].rearrange("p (c n) -> p c n", n=width)

        ld_const, ld_rowsM, ld_rows = sem("ld_const"), sem("ld_rowsM"), sem("ld_rows")
        ld_x, ld_small, ld_router1 = sem("ld_x"), sem("ld_small"), sem("ld_router1")
        ld_states, ld_amask = sem("ld_states"), sem("ld_amask")
        ld_kc, ld_vc = sem("ld_kc"), [sem("ld_vc0"), sem("ld_vc1")]
        sent = sem("sent")
        ktok_sent = sem("ktok_sent")
        NROWSM, NROWS, NSMALL = 6, 4, 8
        half_used = sem("half_used")
        vstep, astep = sem("vstep"), sem("astep")
        dve_results, act_results, pool_results = sem("dve_results"), sem("act_results"), sem("pool_results")

        DVE_ORDER = []
        for step in steps_of("head", "dve"):
            DVE_ORDER += ["xa01", "xn01"] if step == ("stats",) else [step]
        for l in range(2):
            DVE_ORDER += (["xa11", "xn11"] if l else ["gain01"]) + [f"hs{l}1"] + [("hl", l, c) for c in range(C)]
            if l == 0:
                DVE_ORDER += steps_of("mixer0", "dve")
            else:
                DVE_ORDER += [("lo", 1, n) for n in range(24)] + [("vt", i) for i in range(6)]
                DVE_ORDER += steps_of("mixer1", "dve")
            DVE_ORDER += [(f"xo{l}", m) for m in range(C)] + [f"xa{l}2", f"xn{l}2", f"hs{l}2"]
            DVE_ORDER += [f"rt{l}", f"rm{l}", f"oh{l}", f"rt2{l}", f"flag{l}", f"x{l}2"]
        DVE_ORDER += ["xaf", "xnf"]
        ACT_ORDER = []
        for step in steps_of("head", "act"):
            ACT_ORDER += [("sq01", c) for c in range(C)] + ["std01"] if step == ("stats",) else [step]
        for l in range(2):
            ACT_ORDER += ([("sq11", c) for c in range(C)] + ["std11"] if l else []) + [f"hp{l}1"] + [("hh", l, c) for c in range(C)]
            if l == 0:
                ACT_ORDER += steps_of("mixer0", "act")
            else:
                ACT_ORDER += [("hi", 1, n) for n in range(NH)]
                for m in range(24):
                    ACT_ORDER += [("qkv", m)] + ([("hi", 1, m + NH)] if m + NH < 24 else [])
                ACT_ORDER += [("ktok", i) for i in range(6)]
                ACT_ORDER += steps_of("mixer1", "act")
            ACT_ORDER += [(f"sq{l}2", c) for c in range(C)] + [f"std{l}2", f"hp{l}2"] + [(f"ht{l}", i) for i in range(6)] + [f"re{l}", f"re2{l}"]
        ACT_ORDER += [("sqf", c) for c in range(C)] + ["stdf", "hpf"] + [("yt", i) for i in range(6)]
        POOL_ORDER = ["hist", "stg", "mixer0", "qbd0"] + [("qbd", b) for b in range(NB)] + ["mixer1"]
        ORDER = {"dve": (dve_results, {n: i for i, n in enumerate(DVE_ORDER)}),
                 "act": (act_results, {n: i for i, n in enumerate(ACT_ORDER)}),
                 "pool": (pool_results, {n: i for i, n in enumerate(POOL_ORDER)})}
        made = {"dve": 0, "act": 0, "pool": 0}

        def after(eng, who, name):
            s, order = ORDER[who]
            eng.wait_ge(s, order[name] + 1)

        def result(who, name, ins):
            s, order = ORDER[who]
            assert order[name] == made[who], (who, name, order[name], made[who])
            made[who] += 1
            ins.then_inc(s, 1)

        def reads(name, *per_tile):
            for m, rs in enumerate(per_tile):
                readers[tile_of[name] + m] = rs if isinstance(rs, list) else [rs]

        for l in range(2):
            for s in "12"[1 - l:]:
                reads(f"norm{l}{s}", ("act", f"std{l}{s}"))
            reads(f"out{l}", *[("dve", (f"xo{l}", m)) for m in range(C)])
            reads(f"rt{l}", ("dve", f"rt{l}"))
            reads(f"ht{l}", *[("act", (f"ht{l}", i)) for i in range(6)])
            reads(f"rk{l}", ("dve", f"flag{l}"))
        reads("qkv", *[("act", ("qkv", m)) for m in range(24)])
        reads("ktok", *[("act", ("ktok", i)) for i in range(6)])
        reads("vtok", *[("dve", ("vt", i)) for i in range(6)])
        reads("normf", ("act", "stdf"))
        reads("y", *[("act", ("yt", i)) for i in range(6)])

        def claim(pe, k):
            if k >= NBANK:
                for who, name in readers[k - NBANK]:
                    after(pe, who, name)

        PASS = ("perm", "aux", "auxfree", "hghi", "hglo", "gsl", "hi", "lo", "used", "silu", "hid", "tr", "hidhi",
                "hidlo", "ysz", "taken", "yadd", "sc", "scfree")
        moe = {k: sem(f"moe_{k}") for k in PASS}
        more = [{k: sem(f"more{l}_{k}") for k in PASS + ("wl0", "wl1", "wl2", "step")} for l in range(2)]

        unit_tile = {}
        for l in range(2):
            for u in range(24):
                unit_tile[ada_unit(l, u)] = tile_of["row", l, u]
            for u in range(4):
                unit_tile[unit_of[f"out{l}"] + u] = tile_of[f"out{l}"] + 2 * u + 1
        for u in range(14):
            unit_tile[unit_of["in"] + u] = tile_of["in", 2 * u + 1]
        for u in range(12):
            unit_tile[unit_of["qkv"] + u] = tile_of["qkv"] + 2 * u + 1

        def wait_slot(sp, n):
            n -= R
            if n < 0:
                return
            for l, name in enumerate(("in", "qkv")):
                if 0 <= n - unit_of[name] < SPLIT_UNITS[l]:
                    after(sp, "dve", ("lo", l, 2 * (n - unit_of[name]) + 1))
                    return
            if n in unit_tile:
                full(sp, unit_tile[n])
                return
            l = 0 if n < unit_of["qkv"] else 1
            sp.wait_ge(moe["lo"], PASS_HALVES * l + 2 * (n - unit_of[f"moe{l}"]) + 2)

        gate_v = I["w_exp_gate"].rearrange("l g e (c p) f -> (l g e) p c f", p=P)
        up_v = I["w_exp_up"].rearrange("l g e (c p) f -> (l g e) p c f", p=P)
        down_v = I["w_exp_down"].rearrange("l g e (f p) d -> (l g e) p f d", p=P)
        expert_views = [(gate_v, 256), (up_v, 256), (down_v, D)]

        def wide(w, a):
            return w.rearrange("(c p) n -> p c n", p=P)[:, :, a:a + 256]

        def expert_unit(S, l, i, p):
            if S is moe:
                n = unit_of[f"moe{l}"] + p
                return ring[:, n % R, :], unit_loaded[n % R], 16 * (n // R + 1), 16 * (len(STREAM) // R)
            return ring[:, p % 3, :], S[f"wl{p % 3}"], 16 * (4 * 8 * i + p // 3 + 1), 16 * 4

        def buffer_free(eng, l, n):
            name = ("in", "qkv")[l]
            if n >= NH:
                if n % 2 == 0:
                    full(eng, tile_of[name, n - 3] if l == 0 else tile_of[name] + n - 3)
                else:
                    eng.wait_ge(half_used, SPLIT_UNITS[0] * l + n // 2)

        def load_router(eng, l, s):
            for dst, src in ((wr[l][:, :, 0:4], I["w_router_group"][l].rearrange("(c p) n -> p c n", p=P)),
                             (wr[l][:, :, 4:36], I["w_router_expert"][l].rearrange("(c p) n -> p c n", p=P)),
                             (br[l][:, 0:4], I["b_router_group"][l:l + 1].to_broadcast([P, 4])),
                             (br[l][:, 4:36], I["b_router_expert"][l:l + 1].to_broadcast([P, 32]))):
                eng.dma_start(dst, src).then_inc(s, 16)

        block = ctx.enter_context(nc.Block())

        @block.sync
        def _(sp):
            def load(n, src, width=256):
                wait_slot(sp, n)
                sp.dma_start(slot(n, width), src).then_inc(unit_loaded[n % R], 16)

            def load_experts(l):
                base = unit_of[f"moe{l}"]
                for p, (u, w) in enumerate(STREAM):
                    view, width = expert_views[w]
                    load(base + p, view[NG * NE * l + u], width)
                with sp.Fori(1, NG * NE // 4) as q:
                    for p, (u, w) in enumerate(STREAM):
                        view, width = expert_views[w]
                        sp.wait_ge(moe["lo"], HALVES * q + (PASS_HALVES * l + 2 * (p - R) + 2))
                        src = view[bass.ds(4 * q + (NG * NE * l + u), 1)].rearrange("a p c f -> p (a c) f")
                        sp.dma_start(slot(base + p, width), src).then_inc(unit_loaded[(base + p) % R], 16)
                after(sp, "dve", f"flag{l}")
                S = more[l]
                v = sp.value_load(flag[:, :], min_val=0, max_val=1)
                with sp.If(v >= 1):
                    sp.wait_ge(moe["lo"], PASS_HALVES * (l + 1))
                    for i in range(2):
                        if i == 0:
                            for p, (u, w) in enumerate(STREAM):
                                view, width = expert_views[w]
                                if p >= 3:
                                    sp.wait_ge(S["lo"], 2 * (p - 3) + 2)
                                sp.dma_start(slot(p % 3, width), view[NG * NE * l + u]).then_inc(S[f"wl{p % 3}"], 16)
                        with sp.Fori(1 - i, NG * NE // 4) as q:
                            for p, (u, w) in enumerate(STREAM):
                                view, width = expert_views[w]
                                sp.wait_ge(S["lo"], HALVES * q + (PASS_HALVES * i + 2 * (p - 3) + 2))
                                src = view[bass.ds(4 * q + (NG * NE * l + u), 1)].rearrange("a p c f -> p (a c) f")
                                sp.dma_start(slot(p % 3, width), src).then_inc(S[f"wl{p % 3}"], 16)
                    sp.wait_ge(S["lo"], 2 * PASS_HALVES)

            for dst, src in ((rowsM0[0:2], I["norm1"]), (rowsM0[2:4], I["norm2"]),
                             (rowsM0[4:5], I["norm_f"].rearrange("(a d) -> a d", a=1)),
                             (rowsM0[5:17], I["b_ada"].rearrange("l (j d) -> (l j) d", d=D)),
                             (rowsM0[17:18], I["c_prompt"]), (rowsM0[18:26], I["c_sample"])):
                sp.dma_start(dst, src).then_inc(ld_rowsM, 16)
            for l in range(2):
                if l == 0:
                    for u in range(HEAD_UNITS):
                        load(ada_unit(0, u), wide(I["w_ada"][0], 256 * u))
                    for u in range(14):
                        load(unit_of["in"] + u, wide(I["w_in_even"][0], 256 * u if u < 8 else 256 * u + 8))
                    for n in range(HEAD_UNITS, HEAD_UNITS + 24):
                        load(ada_unit(0, n), wide(I["w_ada"][n // 24], 256 * (n % 24)))
                    for u in range(4):
                        load(unit_of["out0"] + u, wide(I["w_out_even"][0], 256 * u))
                else:
                    for u in range(12):
                        load(unit_of["qkv"] + u, wide(I["w_qkv_odd"][0], 256 * u))
                    for u in range(HEAD_UNITS, 24):
                        load(ada_unit(1, u), wide(I["w_ada"][1], 256 * u))
                    for u in range(4):
                        load(unit_of["out1"] + u, wide(I["w_out_odd"][0], 256 * u))
                load_experts(l)

        @block.gpsimd
        def _(pool):
            def expert_pass(S, i):
                pool.wait_ge(S["perm"], i + 1)
                pool.memset(AM["ys"], 0.0).then_inc(S["ysz"], 1)
                pool.wait_ge(S["ysz"], i + 1)
                if i == 0:
                    pool.memset(statS[:, 0, 7:8], 0.0).then_inc(S["yadd"], 2)
                for g in range(NG):
                    with pool.Fori(0, 2) as j:
                        pool.wait_ge(S["taken"], j + (9 * i + 2 * g + 2))
                        pool.tensor_tensor(ys[:, g, :], ys[:, g, :], sumbuf, ALU.add).then_inc(S["yadd"], 1)
                        pool.wait_ge(S["yadd"], j + (8 * i + 2 * g + 3))

            def expert_sums(l):
                expert_pass(moe, l)
                after(pool, "dve", f"flag{l}")
                v = pool.value_load(flag[:, :], min_val=0, max_val=1)
                with pool.If(v >= 1):
                    for i in range(2):
                        expert_pass(more[l], i)

            pool.memset(ext[:, :, 0:HIST], 0.0)
            pool.memset(bx[:, :, 0:HIST], 0.0)
            after(pool, "dve", ("cols", 2))
            exts = ext[:, :, EP:EW].rearrange("p m (b e) -> p m b e", b=NB)
            bxs = bx[:, :, EP:EW].rearrange("p m (b e) -> p m b e", b=NB)
            pool.memset(bxs[:, :, :, 0:1], 0.0)
            for m in range(12):
                pool.tensor_copy(exts[:, m, :, 0:HIST], colsA[:, m, 0:24].rearrange("p (b j) -> p b j", b=NB))
            for m in range(4):
                ins = pool.tensor_copy(bxs[:, m, :, 1:HIST], colsB[:, m, 0:16].rearrange("p (b j) -> p b j", b=NB))
            result("pool", "hist", ins)
            after(pool, "act", ("ext", 11))
            after(pool, "dve", ("bx", 3))
            s27 = stg.rearrange("p (m r) -> p m r", m=12)
            s18 = stgb.rearrange("p (m r) -> p m r", m=4)
            pool.tensor_copy(s27[:, :, 0:3], ext[:, :, EP - 3:EP])
            for m in range(12):
                pool.tensor_copy(s27[:, m, 3:27].rearrange("p (b j) -> p b j", b=NB), exts[:, m, :, ES - 3:ES])
            pool.tensor_copy(s18[:, :, 0:2], bx[:, :, EP - 2:EP])
            for m in range(4):
                ins = pool.tensor_copy(s18[:, m, 2:18].rearrange("p (b j) -> p b j", b=NB), bxs[:, m, :, ES - 2:ES])
            result("pool", "stg", ins)
            after(pool, "pool", "stg")
            after(pool, "dve", ("conv", 11))
            for h in range(H):
                pool.dma_start(states[:, :, h, :], I["state_a_ssm"][0, :, h].rearrange("b k v -> k b v"))\
                    .then_inc(ld_states, 16)
            after(pool, "act", ("so", 3))
            for src, dst in ((stout[0:3, 0:1536], O["aconv_p"][0, 0]),
                             (stout[3:27, 0:1536], O["aconv_s"][0].rearrange("b j n -> (b j) n")),
                             (stout[0:2, 1536:2048], O["bconv_p"][0, 0]),
                             (stout[2:18, 1536:2048], O["bconv_s"][0].rearrange("b j n -> (b j) n"))):
                pool.dma_start(dst, src).then_inc(sent, 16)
            after(pool, "dve", ("s", 1))
            pool.dma_start(O["ssm_p"][0, 0].rearrange("h k v -> k h v"), S0).then_inc(sent, 16)
            after(pool, "dve", ("ds", H - 1, 1))
            for h in range(H):
                pool.dma_start(O["ssm_s"][0, :, h].rearrange("b k v -> k b v"), states[:, :, h, :]).then_inc(sent, 16)
            pool.wait_ge(sent, 16 * 9)
            result("pool", "mixer0", pool.memset(stat[:, 0, 7:8], 0.0))
            expert_sums(0)
            after(pool, "dve", "x02")
            pool.dma_start(A1["msk"], I["amasks"]).then_inc(ld_amask, 16)
            load_router(pool, 1, ld_router1)

            def load_cache(b):
                kv = [I[n][0, b].rearrange("(a p) h d -> p a (h d)", p=P) for n in ("cache_c_k", "cache_c_v")]
                if b >= 1:
                    after(pool, "act", ("kt", b - 1, 1))
                    after(pool, "dve", ("kt", b - 1, 3))
                pool.dma_start(Kc, kv[0]).then_inc(ld_kc, 16)
                if b == 0:
                    after(pool, "act", ("qkv", 23))
                if b >= 2:
                    after(pool, "dve", ("sout", b - 2))
                pool.dma_start(Vc[:, b % 2], kv[1]).then_inc(ld_vc[b % 2], 16)

            load_cache(0)
            result("pool", "qbd0", pool.memset(A1["qbd"], 0.0))
            after(pool, "pool", "qbd0")
            for i in range(6):
                t = i // 2
                a, n = TT[t]
                if i % 2 == 1:
                    after(pool, "act", ("ktok", i))
                    if t < 2:
                        dst = O["ck_p"][0, 0, a:a + n].rearrange("t h d -> t (h d)")
                    else:
                        dst = O["ck_s"][0].rearrange("b t h d -> (b t) (h d)")
                    pool.dma_start(dst, ktok[0:n, t % 2, :]).then_inc(ktok_sent if t == 0 else sent, 16)
            after(pool, "dve", ("vt", 5))
            for t, (a, n) in enumerate(TT):
                if t < 2:
                    dst = O["cv_p"][0, 0, a:a + n].rearrange("t h d -> t (h d)")
                else:
                    dst = O["cv_s"][0].rearrange("b t h d -> (b t) (h d)")
                pool.dma_start(dst, vtok[0:n, t, :]).then_inc(sent, 16)
            for b in range(NB):
                if b >= 2:
                    after(pool, "dve", ("smax", b - 2))
                for e in range(2):
                    r = slice(64 * e, 64 * e + 64)
                    cells = qbd[r, b % 2, :].rearrange("p (c w) -> p c w", w=P + 16)[:, :, 8 * e:8 * e + LS]
                    ins = pool.tensor_copy(cells, qkvT[r, 0:C, NP_ + LS * b:NP_ + LS * b + LS])
                result("pool", ("qbd", b), ins)
                after(pool, "pool", ("qbd", b))
                if b + 1 < NB:
                    load_cache(b + 1)
            pool.wait_ge(sent, 16 * 14)
            result("pool", "mixer1", pool.memset(stat[:, 1, 7:8], 0.0))
            expert_sums(1)
            for t, (a, n) in enumerate(TT):
                after(pool, "act", ("yt", 2 * t + 1))
                dst = O["y_p"][0, a:a + n] if t < 2 else O["y_s"].rearrange("b t d -> (b t) d")
                pool.dma_start(dst, ytok[0:n, t, :]).then_inc(sent, 16)
            pool.wait_ge(sent, 16 * 17)
            pool.wait_ge(ktok_sent, 16)

        @block.tensor
        def _(pe):
            def I_(n):
                return K("ident")[0:n, 0:n]

            def transposes(k, parts):
                claim(pe, k)
                for (a, b), src in parts:
                    ins = pe.transpose(B(k)[0:src.shape[1], a:b], src, I_(src.shape[0]))
                filled(ins, k)

            def three(out, a, b, start, stop):
                pe.matmul(out, a[0], b[0], start=start, stop=False)
                pe.matmul(out, a[0], b[1], start=False, stop=False)
                return pe.matmul(out, a[1], b[0], start=False, stop=stop)

            def project_split(l, m, k):
                claim(pe, k)
                for c in range(C):
                    if m == 0:
                        after(pe, "dve", ("hl", l, c))
                    n = m // 2 * 2 + c // (C // 2)
                    if c % (C // 2) == 0:
                        after(pe, "dve", ("lo", l, n))
                    at = 256 * (c % (C // 2)) + P * (m % 2)
                    ins = three(B(k)[:, 0:T], [x[:, n % NH, at:at + P] for x in (wh, wl)],
                                [x[:, c, :] for x in (hTh, hTl)], c == 0, c == C - 1)
                    if m % 2 == 1 and c == C // 2 - 1:
                        ins.then_inc(half_used, 1)
                filled(ins, k)

            def project(name, n, rhs):
                for m in range(n):
                    project_chunk(name, m, tile_of[name] + m, rhs)

            def project_chunk(name, m, k, rhs):
                u = unit_of[name] + m // 2
                if m % 2 == 0:
                    need_unit(pe, u)
                claim(pe, k)
                for c in range(C):
                    w = slot(u)[:, c, P * (m % 2):P * (m % 2) + P]
                    ins = pe.matmul(B(k)[:, 0:T], w, rhs(c), start=(c == 0), stop=(c == C - 1))
                filled(ins, k)

            def norm_sum(tag, c):
                k = tile_of[f"norm{tag}"]
                if c == 0:
                    claim(pe, k)
                after(pe, "act", (f"sq{tag}", c))
                ins = pe.matmul(B(k)[:, 0:T], K("ones"), scratch[:, c, :], start=(c == 0), stop=(c == C - 1))
                if c == C - 1:
                    filled(ins, k)

            def project_out(l, rhs):
                for m in range(C):
                    project_chunk(f"out{l}", m, tile_of[f"out{l}"] + m, rhs)
                    if m >= 2:
                        norm_sum(f"{l}2", m - 2)
                norm_sum(f"{l}2", C - 2)
                norm_sum(f"{l}2", C - 1)

            def norm(tag):
                if tag in ("11", "f"):
                    for c in range(C):
                        norm_sum(tag, c)
                after(pe, "act", f"hp{tag}")
                if tag != "f":
                    after(pe, "dve", f"hs{tag}")

            def ada_step(what, l, u):
                k = tile_of[what, l, u]
                if what == "turn":
                    after(pe, "act", ("row", l, u))
                    transposes(k, [((NCOND * i, NCOND * i + NCOND), modrow(l, u)[:, P * i:P * i + P]) for i in range(2)])
                    return
                claim(pe, k)
                need_unit(pe, ada_unit(l, u))
                for c in range(C):
                    ins = pe.matmul(B(k)[0:NCOND, 0:256], condT[:, c, :], slot(ada_unit(l, u))[:, c, :],
                                    start=(c == 0), stop=(c == C - 1))
                filled(ins, k)

            def head():
                for what, *i in steps_of("head", "pe"):
                    k = tile_of[(what, *i)]
                    if what == "cols":
                        rows, n, m = ((rowsM0, 26, C), (rowsA0, 28, 12), (rowsB0, 19, 4))[i[0]]
                        if i[0] == 0:
                            pe.wait_ge(ld_const, 16)
                            pe.wait_ge(ld_rowsM, 16 * NROWSM)
                        else:
                            pe.wait_ge(ld_rows, 16 * NROWS)
                        transposes(k, [((n * c, n * c + n), rows[:, P * c:P * c + P]) for c in range(m)])
                    elif what == "stats":
                        for c in range(C):
                            norm_sum("01", c)
                    elif what == "x":
                        c, = i
                        pe.wait_ge(ld_x, 48)
                        transposes(k, [((a, a + n), xload[0:n, t, P * c:P * c + P]) for t, (a, n) in enumerate(TT)])
                    else:
                        if (what, *i) == ("row", 0, 0):
                            after(pe, "act", ("cond",))
                        ada_step(what, *i)

            def mixer0():
                def four(k, n, lhs, rhs):
                    claim(pe, k)
                    for h in range(H):
                        ins = pe.matmul(B(k)[0:n, n * h:n * h + n], lhs(h), rhs(h), start=True, stop=True)
                    filled(ins, k)

                def spread(k, col, up, n):
                    claim(pe, k)
                    for h in range(H):
                        ins = pe.matmul(B(k)[:, n * h:n * h + n], col[0:n, h:h + 1].to_broadcast([n, P]), up,
                                        start=True, stop=True)
                    filled(ins, k)

                def spread_tokens(k, col):
                    claim(pe, k)
                    for t, (a, n) in enumerate(TT):
                        ins = pe.matmul(B(k)[:, a:a + n], col(t, n).to_broadcast([n, P]), I_(n), start=True, stop=True)
                    filled(ins, k)

                def token_sums(k, sq, m):
                    claim(pe, k)
                    for t, (a, n) in enumerate(TT):
                        for j in range(m):
                            ins = pe.matmul(B(k)[0:n, m * t + j:m * t + j + 1], sq[:, j, a:a + n], K("ones")[:, 0:1],
                                            start=True, stop=True)
                    filled(ins, k)

                for what, *i in steps_of("mixer0", "pe"):
                    k = tile_of[(what, *i)]
                    t = i[-1] if i else 0
                    a, n = TT[t] if t < 3 else TT[0]
                    up = K("upto") if n == P else K("upto_s", NS)
                    if what in ("row", "turn"):
                        ada_step(what, *i)
                    elif what == "ab":
                        pe.wait_ge(ld_small, 16 * NSMALL)
                        claim(pe, k)
                        for t, (a, n) in enumerate(TT):
                            for c in range(C):
                                ins = pe.matmul(B(k)[0:n, 8 * t:8 * t + 8], hT[:, c, a:a + n], wab[:, c, :],
                                                start=(c == 0), stop=(c == C - 1))
                        filled(ins, k)
                    elif what == "in":
                        if i[0] < 2 * SPLIT_UNITS[0]:
                            project_split(0, i[0], k)
                        else:
                            project_chunk("in", i[0], k, lambda c: hT[:, c, :])
                    elif what == "gcol":
                        after(pe, "dve", ("g",))
                        claim(pe, k)
                        for t, (a, n) in enumerate(TT):
                            up, af = (K("upto"), K("after")) if t < 2 else (K("upto_s", NS), K("after_s", NS))
                            pe.matmul(B(k)[0:n, 8 * t:8 * t + 4], up, gg[0:n, t, :], start=True, stop=True)
                            ins = pe.matmul(B(k)[0:n, 8 * t + 4:8 * t + 8], af, gg[0:n, t, :], start=True, stop=True)
                        filled(ins, k)
                    elif what == "grow":
                        spread(k, gg[:, t, :], up, n)
                    elif what == "l2ss":
                        after(pe, "act", ("sq", 7))
                        token_sums(k, scratch, 8)
                    elif what == "l2bc":
                        after(pe, "dve", ("l2r",))
                        spread_tokens(k, lambda t, n, m=i[0]: l2col[0:n, t, m:m + 1])
                    elif what == "brow":
                        spread(k, beta[:, t, :], I_(n), n)
                    elif what == "vt":
                        after(pe, "act", ("cv", 11))
                        transposes(k, [((P * h, P * h + P), cT[:, 8 + h, a:a + n]) for h in range(H)])
                    elif what == "kt":
                        after(pe, "dve", ("qn", 7))
                        transposes(k, [((P * h, P * h + P), cT[:, 4 + h, a:a + n]) for h in range(H)])
                    elif what in ("at", "qk"):
                        after(pe, "dve", ("kb", 2))
                        rhs = kb if what == "at" else cT
                        four(k, n, lambda h: cT[:, 4 + h, a:a + n], lambda h: rhs[:, h, a:a + n])
                    elif what == "xt0":
                        after(pe, "dve", ("xt1", t))
                        transposes(k, [((n * h, n * h + n), XT[0:n, t, h, 0:n]) for h in range(H)])
                    elif what == "P":
                        after(pe, "dve", ("lt", *i))
                        if i[0] == 2:
                            after(pe, "act", ("x0", t))
                        four(k, n, lambda h: LT[0:n, t, h, 0:n], lambda h: X[0:n, t, h, 0:n])
                    elif what == "XPt":
                        after(pe, "act", ("pb", *i))
                        four(k, n, lambda h: PB[0:n, t, h, 0:n], lambda h: XT[0:n, t, h, 0:n])
                    elif what == "XP":
                        four(k, n, lambda h: XT[0:n, t, h, 0:n], lambda h: PB[0:n, t, h, 0:n])
                    elif what == "u":
                        after(pe, "dve", ("r", t) if t else ("xi", 64, 1))
                        claim(pe, k)
                        for h in range(H):
                            ins = pe.matmul(B(k)[0:n, P * h:P * h + P], XT[0:n, t, h, 0:n],
                                            (RR if t else vb)[0:n, t, h, :], start=True, stop=True)
                        filled(ins, k)
                    elif what == "kS" and t == 1:
                        after(pe, "dve", ("s", 0))
                        claim(pe, k)
                        for h in range(H):
                            ins = pe.matmul(B(k)[0:n, P * h:P * h + P], cT[:, 4 + h, a:a + n], S0[:, h, :],
                                            start=True, stop=True)
                        filled(ins, k)
                    elif what == "kS":
                        after(pe, "dve", ("ktm",))
                        pe.wait_ge(ld_states, 64)
                        claim(pe, k)
                        for h in range(H):
                            for b in range(NB):
                                ins = pe.matmul(B(k)[0:n, P * h:P * h + P], kTm[:, h, b, :], states[:, b, h, :],
                                                start=(b == 0), stop=(b == NB - 1))
                        filled(ins, k)
                    elif what == "o":
                        after(pe, "act", ("u", t))
                        claim(pe, k)
                        for h in range(H):
                            o = B(k)[:, n * h:n * h + n]
                            ins = pe.matmul(o, uu[0:n, t, h, :], qkg[0:n, t, h, 0:n], start=True, stop=(t != 1))
                            if t == 1:
                                ins = pe.matmul(o, S0[:, h, :], qd[:, h, a:a + n], start=False, stop=True)
                            if t == 2:
                                for b in range(NB):
                                    ins = pe.matmul(o[:, LS * b:LS * b + LS], states[:, b, h, :],
                                                    qd[:, h, a + LS * b:a + LS * b + LS], start=False, stop=True,
                                                    skip_group_check=True)
                        filled(ins, k)
                    elif what == "s":
                        claim(pe, k)
                        for h in range(H):
                            ins = pe.matmul(B(k)[:, P * h:P * h + P], kd[0:n, t, h, :], uu[0:n, t, h, :],
                                            start=True, stop=True)
                        filled(ins, k)
                    elif what == "ds":
                        h, j = i
                        after(pe, "dve", ("ue", h))
                        claim(pe, k)
                        filled(pe.matmul(B(k)[:, 0:512], kd[0:NS, 2, h, :],
                                         ue[:, 4 * j:4 * j + 4, :].rearrange("p b v -> p (b v)"),
                                         start=True, stop=True), k)
                    elif what == "st":
                        after(pe, "pool", "stg")
                        j0 = i[0]
                        transposes(k, [((P * j, P * j + P), stg[:, 27 * (4 * j0 + j):27 * (4 * j0 + j) + 27] if j0 < 3
                                        else stgb[:, 18 * j:18 * j + 18]) for j in range(4)])
                    elif what == "onss":
                        after(pe, "act", ("osq",))
                        token_sums(k, osq, H)
                    elif what == "onbc":
                        after(pe, "dve", ("onr",))
                        spread_tokens(k, lambda t, n, h=i[0]: oncol[0:n, t, h:h + 1])
                after(pe, "dve", ("cat",))
                project_out(0, lambda c: catT[:, c, :])

            def mixer1():
                for m in range(24):
                    project_split(1, m, tile_of["qkv"] + m)
                after(pe, "act", ("qkv", 23))
                for name, m0 in (("ktok", 8), ("vtok", 16)):
                    for i in range(6):
                        a, n = TT[i // 2]
                        transposes(tile_of[name] + i, [((P * j, P * j + P), qkvT[:, m0 + 4 * (i % 2) + j, a:a + n])
                                                       for j in range(4)])
                for what, *i in steps_of("mixer1", "pe"):
                    k = tile_of[(what, *i)]
                    n = i[0]
                    u = n % 2
                    if what in ("row", "turn"):
                        ada_step(what, *i)
                    if what == "S":
                        c, r = n // 2, slice(64 * u, 64 * u + 64)
                        claim(pe, k)
                        pe.matmul(B(k)[:, 0:128], qkvT[r, c, 0:128], qkvT[r, 8 + c, 0:128], start=True, stop=True)
                        filled(pe.matmul(B(k)[:, 128:384], qkvT[r, c, 128:256], qkvT[r, 8 + c, 0:256],
                                         start=True, stop=True), k)
                    elif what == "T":
                        after(pe, "dve", ("apr", n))
                        transposes(k, [((P * j, P * j + P), prb[:, u, P * j:P * j + P]) for j in range(3)])
                    elif what == "O":
                        if n == 0:
                            after(pe, "dve", ("vt", 5))
                        if u == 0:
                            claim(pe, k)
                        after(pe, "act", ("apT", n))
                        r = slice(64 * u, 64 * u + 64)
                        v = slice(64 * n, 64 * n + 64)
                        pe.matmul(B(k)[r, 0:128], vtok[:, 0, v], pT[:, u, 0:128], start=True, stop=True)
                        pe.matmul(B(k)[r, 128:256], vtok[:, 0, v], pT[:, u, 128:256], start=True, stop=False)
                        ins = pe.matmul(B(k)[r, 128:256], vtok[:, 1, v], pT[:, u, 256:384], start=False, stop=True)
                        if u == 1:
                            filled(ins, k)
                    elif what == "K":
                        pe.wait_ge(ld_kc, 16 * (n + 1))
                        transposes(k, [((256 * j + P * a_, 256 * j + P * a_ + P),
                                        Kc[:, a_, P * (2 * i[1] + j):P * (2 * i[1] + j) + P])
                                       for j in range(2) for a_ in range(2)])
                    elif what == "Ss":
                        after(pe, "act", ("kt", n, 1))
                        after(pe, "dve", ("kt", n, 3))
                        after(pe, "pool", ("qbd", n))
                        claim(pe, k)
                        for c in range(C):
                            pe.matmul(B(k)[:, 0:256], qbd[:, u, P * c:P * c + P], KT[:, c, :],
                                      start=(c == 0), stop=(c == C - 1))
                        for c in range(C):
                            ins = pe.matmul(B(k)[:, 256:320], qbd[:, u, P * c:P * c + P], qkvT[:, 8 + c, NP_:T],
                                            start=(c == 0), stop=(c == C - 1))
                        filled(ins, k)
                    elif what == "Ts":
                        after(pe, "dve", ("spr", n))
                        claim(pe, k)
                        for j in range(2):
                            pe.transpose(B(k)[:, P * j:P * j + P], prbS[:, u, P * j:P * j + P], I_(P))
                        filled(pe.transpose(B(k)[0:NS, 256:384], prbS[:, u, 256:320], I_(P)), k)
                    elif what == "Os":
                        after(pe, "act", ("spT", n))
                        pe.wait_ge(ld_vc[u], 16 * (n // 2 + 1))
                        claim(pe, k)
                        for c in range(C):
                            o = B(k)[:, 16 * c:16 * c + 16]
                            q = slice(16 * c, 16 * c + 16)
                            for a_ in range(2):
                                pe.matmul(o, Vc[:, u, a_, P * c:P * c + P], pTS[:, u, P * a_:P * a_ + P][:, q],
                                          start=(a_ == 0), stop=False)
                            ins = pe.matmul(o, vtok[0:NS, 2, P * c:P * c + P], pTS[0:NS, u, 256:384][:, q],
                                            start=False, stop=True)
                        filled(ins, k)
                after(pe, "act", ("aout", 7))
                after(pe, "dve", ("sout", NB - 1))
                project_out(1, lambda c: attnT[:, c, :])

            def router(l):
                k = tile_of[f"rt{l}"]
                if l == 1:
                    pe.wait_ge(ld_router1, 64)
                claim(pe, k)
                for t, (a, n) in enumerate(TT):
                    for c in range(C):
                        ins = pe.matmul(B(k)[0:n, 36 * t:36 * t + 36], hT[:, c, a:a + n], wr[l][:, c, :],
                                        start=(c == 0), stop=(c == C - 1))
                filled(ins, k)
                for i in range(6):
                    a, n = TT[i // 2]
                    transposes(tile_of[f"ht{l}"] + i, [((P * j, P * j + P), hT[:, 4 * (i % 2) + j, a:a + n])
                                                       for j in range(4)])
                k = tile_of[f"rk{l}"]
                after(pe, "dve", f"oh{l}")
                claim(pe, k)
                for t, (a, n) in enumerate(TT):
                    for t2 in range(t + 1):
                        n2 = TT[t2][1]
                        m = K("ones", n2)[:, 0:n] if t2 < t else K("upto", n)[:, 0:n]
                        pe.matmul(B(k)[0:n, 4 * t:4 * t + 4], m, onehot[0:n2, t2, :], start=(t2 == 0), stop=(t2 == t))
                for t, (a, n) in enumerate(TT):
                    ins = pe.matmul(B(k)[:, 16:20], K("ones", n), onehot[0:n, t, :], start=(t == 0), stop=(t == 2))
                filled(ins, k)

            def expert_pass(S, i):
                pe.wait_ge(S["perm"], i + 1)
                for a in range(12):
                    bk = bank[5 + a % 2]
                    if a in (2, 3, 4, 5):
                        pe.wait_ge(S["auxfree"], 4 * i + a - 1)
                    elif a >= 6:
                        pe.wait_ge(S["hglo"], 8 * i + a - 5)
                    if a < 4:
                        for t, (x, m) in enumerate(TT):
                            ins = pe.transpose(bk[:, x:x + m], perm[0:m, t, a, :], I_(m))
                    else:
                        for t, (x, m) in enumerate(TT):
                            ins = pe.matmul(bk[:, :], htok[0:m, t, P * (a - 4):P * (a - 4) + P],
                                            perm[0:m, t, :, :].rearrange("p g s -> p (g s)"),
                                            start=(t == 0), stop=(t == 2))
                    ins.then_inc(S["aux"], 1)
                for g in range(NG):
                    for t, (x, m) in enumerate(TT):
                        ins = pe.matmul(bank[7][:, NE * g:NE * g + NE], perm[0:m, t, g, :],
                                        gates[0:m, t, NE * g:NE * g + NE], start=(t == 0), stop=(t == 2))
                        if g == 0 and t == 0 and i == 0:
                            ins.then_inc(S["used"], NH)
                ins.then_inc(S["gsl"], 1)
                pe.wait_ge(S["hglo"], 8 * i + 8)

                for g in range(NG):
                    with pe.Fori(0, 2) as j:
                        def half_ready(h):
                            pe.wait_ge(S["lo"], HALVES * j + (PASS_HALVES * i + HALVES * 2 * g + h + 1))
                            return wh[:, h % NH, :], wl[:, h % NH, :]

                        def gate_up(u, w):
                            if w == 0:
                                pe.wait_ge(S["hid"], 4 * j + (32 * i + 8 * g + u + 1))
                            for q in range(2):
                                parts = half_ready(AT_HALF[u, w] + q)
                                for c in range(C // 2):
                                    cc = C // 2 * q + c
                                    ins = three(bank[u % 2 + 5 * w][:, 0:256],
                                                [x[:, cc, P * g:P * g + P] for x in (hgh, hgl)],
                                                [x[:, 256 * c:256 * c + 256] for x in parts], cc == 0, cc == C - 1)
                                ins.then_inc(S["used"], 1)

                        def turn(u):
                            pe.wait_ge(S["hid"], 4 * j + (32 * i + 8 * g + u + 3))
                            for f in range(2):
                                ins = pe.transpose(bank[2][:, 256 * (u % 2) + P * f:256 * (u % 2) + P * f + P],
                                                   hid[:, u % 2, P * f:P * f + P], I_(P))
                            ins.then_inc(S["tr"], 1)

                        def down(u):
                            if u == 0:
                                pe.wait_ge(S["taken"], j + (9 * i + 2 * g + 1))
                            pe.wait_ge(S["hidlo"], 4 * j + (32 * i + 8 * g + u + 1))
                            for f in range(2):
                                parts = half_ready(AT_HALF[u, 2] + f)
                                for d in range(2):
                                    ins = three(bank[3 + d][:, :], [x[:, u % 2, f, :] for x in (hidTh, hidTl)],
                                                [x[:, 512 * d:512 * d + 512] for x in parts],
                                                u == 0 and f == 0, u == 3 and f == 1)
                                ins.then_inc(S["used"], 1)

                        for u in range(4):
                            gate_up(u, 0)
                            if u:
                                turn(u - 1)
                            gate_up(u, 1)
                            if u:
                                down(u - 1)
                        turn(3)
                        down(3)
                pe.wait_ge(S["yadd"], 8 * i + 10)
                for m in range(C):
                    n = 8 * i + m
                    if m >= 2 or i:
                        pe.wait_ge(S["scfree"], n - 1)
                    for g in range(NG):
                        ins = pe.matmul(bank[5 + m % 2][:, 0:T], ys[:, g, P * m:P * m + P], permT[:, g, :],
                                        start=(g == 0), stop=(g == NG - 1))
                    ins.then_inc(S["sc"], 1)

            def experts(l):
                k = tile_of[f"rk{l}"] + 1
                for b in range(NBANK):
                    claim(pe, k + b)
                expert_pass(moe, l)
                after(pe, "dve", f"flag{l}")
                v = pe.value_load(flag[:, :], min_val=0, max_val=1)
                with pe.If(v >= 1):
                    for i in range(2):
                        expert_pass(more[l], i)
                after(pe, "dve", f"x{l}2")

            head()
            for l in range(2):
                norm(f"{l}1")
                if l == 0:
                    mixer0()
                else:
                    mixer1()
                norm(f"{l}2")
                router(l)
                experts(l)
            norm("f")
            for i in range(6):
                a, n = TT[i // 2]
                transposes(tile_of["y"] + i, [((P * j, P * j + P), hT[:, 4 * (i % 2) + j, a:a + n]) for j in range(4)])
        def samples(ap):
            return ap.rearrange("p (b t) -> p b t", b=NB)

        def sequences(flat):
            return flat[:, EP:EW].rearrange("p (b e) -> p b e", b=NB)[:, :, 0:LS]

        @block.scalar
        def _(act):
            steps = [0]

            def link(ins):
                steps[0] += 1
                ins.then_inc(astep, 1)
                act.wait_ge(astep, steps[0])

            act.dma_start(const[:, :], I["masks"]).then_inc(ld_const, 16)
            for t, (a, n) in enumerate(TT):
                src = I["x_prompt"][0, a:a + n] if t < 2 else I["x_sample"].rearrange("b t d -> (b t) d")
                act.dma_start(xload[0:n, t, :], src).then_inc(ld_x, 16)
            for dst, src in ((rowsA0[0:24], I["state_a_conv"][0].rearrange("b j n -> (b j) n")),
                             (rowsA0[24:28], I["conv_a_w"][0]),
                             (rowsB0[0:16], I["state_b_conv"][0].rearrange("b j n -> (b j) n")),
                             (rowsB0[16:19], I["conv_b_w"][0])):
                act.dma_start(dst, src).then_inc(ld_rows, 16)
            with nc.allow_non_contiguous_dma(reason="a column of 128 gains"):
                act.dma_start(colsO[:, :], I["o_gain_a"].rearrange("a p -> p a")).then_inc(ld_small, 16)
            act.dma_start(wab[:, :, :], I["w_in_even"][0].rearrange("(c p) n -> p c n", p=P)[:, :, 2048:2056])\
               .then_inc(ld_small, 16)
            act.dma_start(dtb[:, 0, :], I["dt_bias"][0:1].to_broadcast([P, 4])).then_inc(ld_small, 16)
            act.dma_start(dtb[:, 1, :], I["a_log"][0:1].to_broadcast([P, 4])).then_inc(ld_small, 16)
            load_router(act, 0, ld_small)

            def copy(dst, src):
                return act.activation(dst, src, ACT.Copy)

            def norm_stats(tag):
                if tag == "12":
                    after(act, "pool", "mixer1")
                for c in range(C):
                    after(act, "dve", {"01": ("x", c), "02": ("xo0", c), "11": "x02", "12": ("xo1", c), "f": "x12"}[tag])
                    result("act", (f"sq{tag}", c), act.activation(scratch[:, c, :], xT[:, c, :], ACT.Square))
                k = tile_of[f"norm{tag}"]
                full(act, k)
                result("act", f"std{tag}", act.activation(rstd[:, :], B(k)[:, 0:T], ACT.Sqrt, scale=1.0 / D,
                                                          bias=K("eps")))

            def norm_apply(tag):
                if tag == "01":
                    after(act, "dve", "gain01")
                if tag == "02":
                    after(act, "pool", "mixer0")
                for c in range(C):
                    if c % 4 == 0:
                        after(act, "dve", f"xn{tag}" if c else f"xa{tag}")
                    if tag == "f":
                        ins = act.activation(hT[:, c, :], scratch[:, c, :], ACT.Copy, scale=cols[:, c, 4:5])
                    else:
                        j = 0 if tag[1] == "1" else 3
                        ins = act.activation(hT[:, c, 0:NP_], scratch[:, c, 0:NP_], ACT.Identity,
                                             scale=gainA[:, c, 0:1], bias=mod[:, int(tag[0]), j, c, 0:1])
                result("act", f"hp{tag}", ins)
                if tag[1:] == "1":
                    l = int(tag[0])
                    after(act, "act", f"hp{tag}")
                    after(act, "dve", f"hs{tag}")
                    for c in range(C):
                        result("act", ("hh", l, c), copy(hTh[:, c, :], hT[:, c, :]))

            def split_half(l, n):
                unit = unit_of[("in", "qkv")[l]] + n // 2
                if n % 2 == 0:
                    need_unit(act, unit)
                buffer_free(act, l, n)
                result("act", ("hi", l, n), copy(wh[:, n % NH, :],
                                                 ring[:, unit % R, U // 2 * (n % 2):U // 2 * (n % 2) + U // 2]))

            def ada_row(l, u):
                k = tile_of["row", l, u]
                full(act, k)
                if (l, u) != (0, 0) and (l, u) != (0, 1):
                    v = 24 * l + u - 2
                    full(act, tile_of["turn", v // 24, v % 24])
                result("act", ("row", l, u), copy(modrow(l, u), B(k)[0:NCOND, 0:256]))

            def mixer0():
                exts = ext[:, :, EP:EW].rearrange("p m (b e) -> p m b e", b=NB)
                after(act, "pool", "hist")

                def heads(ap, n):
                    return ap[0:n, 0:H * n].rearrange("p (h i) -> p h i", h=H)

                for what, *i in steps_of("mixer0", "act"):
                    step = (what, *i)
                    t = i[-1] if i else 0
                    a, n = TT[t] if t < 3 else TT[0]
                    if what == "row":
                        ada_row(*i)
                    elif what == "hi":
                        split_half(*i)
                    elif what == "gea":
                        after(act, "dve", ("gabs",))
                        link(act.activation(sc8[:, :, 4:8], sc8[:, :, 0:4], ACT.Exp, scale=-1.0))
                        link(act.activation(sc8[:, :, 4:8], sc8[:, :, 4:8], ACT.Ln, bias=K("one")))
                        result("act", step, act.activation(dtb[:, 1, :], dtb[:, 1, :], ACT.Exp))
                    elif what == "geb":
                        result("act", step, act.activation(sc8[:, :, 8:12], gab[:, :, 4:8], ACT.Exp, scale=-1.0))
                    elif what == "ext":
                        m, = i
                        k = tile_of["in", m]
                        full(act, k)
                        copy(ext[:, m, HIST:EP], B(k)[:, 0:NP_])
                        result("act", step, copy(exts[:, m, :, HIST:], samples(B(k)[:, NP_:T])))
                    elif what == "z":
                        k = tile_of["in", i[0]]
                        full(act, k)
                        result("act", step, act.activation(zT[:, i[0] - 12, :], B(k)[:, 0:T], ACT.Silu))
                    elif what == "gt":
                        m, = i
                        k = tile_of["in", m]
                        full(act, k)
                        result("act", step, copy(bg[:, m - 16, :] if m < 20 else cg[:, m - 20, :], B(k)[:, 0:T]))
                    elif what == "cv":
                        v, = i
                        after(act, "dve", ("conv", v))
                        acc = convacc[:, v % 2, :]
                        act.activation(cT[:, v, 0:NP_], acc[:, 0:NP_], ACT.Silu)
                        result("act", step, act.activation(samples(cT[:, v, NP_:T]), sequences(acc), ACT.Silu))
                    elif what == "sq":
                        after(act, "act", ("cv", i[0]))
                        result("act", step, act.activation(scratch[:, i[0], :], cT[:, i[0], :], ACT.Square))
                    elif what == "egc":
                        after(act, "dve", ("gcol",))
                        result("act", step, act.activation(egc[:, :, :], gcols[:, :, :], ACT.Exp))
                    elif what == "eG":
                        k = tile_of["grow", t]
                        full(act, k)
                        result("act", step, act.activation(eG[:, :, a:a + n], B(k)[:, 0:H * n]
                                                           .rearrange("p (h i) -> p h i", h=H), ACT.Exp))
                    elif what == "ge":
                        after(act, "dve", ("gd", 2))
                        act.activation(gam[:, 0:2, :, :], gam[:, 0:2, :, :], ACT.Exp)
                        result("act", step, act.activation(gam[0:NS, 2, :, 0:NS], gam[0:NS, 2, :, 0:NS], ACT.Exp))
                    elif what in ("l2s", "ons"):
                        k, col, m, scale = ((tile_of["l2ss",], l2col, 8, 1.0) if what == "l2s" else
                                            (tile_of["onss",], oncol, H, 1.0 / P))
                        full(act, k)
                        act.activation(col[:, 0:2, :], B(k)[:, 0:2 * m].rearrange("p (t m) -> p t m", t=2), ACT.Sqrt,
                                       bias=K("eps"), scale=scale)
                        result("act", step, act.activation(col[0:NS, 2, :], B(k)[0:NS, 2 * m:3 * m], ACT.Sqrt,
                                                           bias=K("eps", NS), scale=scale))
                    elif what == "x0":
                        k = tile_of["xt0", t]
                        full(act, k)
                        result("act", step, copy(X[0:n, t, :, 0:n], heads(B(k), n)))
                    elif what == "pb":
                        k = tile_of["P", i[0], t]
                        full(act, k)
                        result("act", step, copy(PB[0:n, t, :, 0:n], heads(B(k), n)))
                    elif what == "u":
                        k = tile_of["u", t]
                        full(act, k)
                        result("act", step, copy(uu[0:n, t, :, :], B(k)[0:n, :].rearrange("p (h v) -> p h v", h=H)))
                    elif what == "so":
                        k = tile_of["st", i[0]]
                        full(act, k)
                        n = 27 if i[0] < 3 else 18
                        result("act", step, copy(stout[0:n, 512 * i[0]:512 * i[0] + 512], B(k)[0:n, :]))
                    elif what == "osq":
                        after(act, "dve", ("o", 2))
                        after(act, "dve", ("o", 1))
                        after(act, "dve", ("catb", 3))
                        result("act", step, act.activation(osq, oT, ACT.Square))

            def mixer1():
                for n in range(NH):
                    split_half(1, n)
                for m in range(24):
                    k = tile_of["qkv"] + m
                    full(act, k)
                    result("act", ("qkv", m), copy(qkvT[:, m, :], B(k)[:, 0:T]))
                    if m + NH < 24:
                        split_half(1, m + NH)
                for i in range(6):
                    k = tile_of["ktok"] + i
                    n = TT[i // 2][1]
                    full(act, k)
                    if i == 4:
                        act.wait_ge(ktok_sent, 16)
                    result("act", ("ktok", i), copy(ktok[0:n, i // 2 % 2, 512 * (i % 2):512 * (i % 2) + 512], B(k)[0:n, :]))
                for what, *i in steps_of("mixer1", "act"):
                    step = (what, *i)
                    n = i[0]
                    u = n % 2
                    if what == "row":
                        ada_row(*i)
                    if what == "aexp":
                        after(act, "dve", ("amax", n))
                        act.activation(prb[:, u, 0:128], scr[:, u, 0:128], ACT.Exp, bias=stat[:, u, 2:3], scale=0.125)
                        result("act", step, act.activation(prb[:, u, 128:384], scr[:, u, 128:384], ACT.Exp,
                                                           bias=stat[:, u, 3:4], scale=0.125))
                    elif what == "apT":
                        k = tile_of["T", n]
                        full(act, k)
                        result("act", step, copy(pT[:, u, :], B(k)[:, 0:384]))
                    elif what == "aout":
                        k = tile_of["O", 2 * n]
                        full(act, k)
                        result("act", step, copy(attnT[:, n, 0:NP_], B(k)[:, 0:NP_]))
                    elif what == "kt":
                        k = tile_of["K", n, i[1]]
                        full(act, k)
                        if n:
                            full(act, tile_of["Ss", n - 1])
                        result("act", step, copy(KT[:, 2 * i[1]:2 * i[1] + 2, :],
                                                 B(k)[:, :].rearrange("p (c j) -> p c j", c=2)))
                    elif what == "sexp":
                        after(act, "dve", ("smax", n))
                        result("act", step, act.activation(prbS[:, u, 0:T], scrS[:, u, 0:T], ACT.Exp,
                                                           bias=statS[:, u, 2:3], scale=0.125))
                    elif what == "spT":
                        k = tile_of["Ts", n]
                        full(act, k)
                        copy(pTS[:, u, 0:256], B(k)[:, 0:256])
                        result("act", step, copy(pTS[0:NS, u, 256:384], B(k)[0:NS, 256:384]))

            def expert_pass(S, l, i):
                for a in range(12):
                    act.wait_ge(S["aux"], 12 * i + a + 1)
                    src = bank[5 + a % 2]
                    if a < 4:
                        copy(permT[:, a, :], src[:, 0:T]).then_inc(S["auxfree"], 1)
                    else:
                        copy(hgh[:, a - 4, :], src[:, :]).then_inc(S["hghi"], 1)

                def take(used, added):
                    act.wait_ge(S["used"], used)
                    act.wait_ge(S["yadd"], added)
                    copy(sumbuf[:, 0:512], bank[3][:, :])
                    copy(sumbuf[:, 512:1024], bank[4][:, :]).then_inc(S["taken"], 1)

                for g in range(NG):
                    with act.Fori(0, 2) as j:
                        k0 = 32 * i + 8 * g
                        h0 = PASS_HALVES * i + HALVES * 2 * g

                        def split(h):
                            unit, loaded, first, step = expert_unit(S, l, i, h // 2)
                            if h % 2 == 0:
                                act.wait_ge(loaded, step * j + (first + step * 2 * g))
                            act.wait_ge(S["used"], HALVES * j + (h0 + h + 1))
                            copy(wh[:, h % NH, :], unit[:, U // 2 * (h % 2):U // 2 * (h % 2) + U // 2])\
                                .then_inc(S["hi"], 1)

                        def silu(u):
                            act.wait_ge(S["used"], HALVES * j + (NH + h0 + AT_HALF[u, 0] + 2))
                            act.activation(sg[:, u % 2, :], bank[u % 2][:, 0:256], ACT.Silu).then_inc(S["silu"], 1)

                        def turn(u):
                            act.wait_ge(S["tr"], 4 * j + (k0 + u + 1))
                            copy(hidTh[:, u % 2, :, :].rearrange("p f s -> p (f s)"),
                                 bank[2][:, 256 * (u % 2):256 * (u % 2) + 256]).then_inc(S["hidhi"], 1)

                        for h in range(HALVES):
                            if h == NH:
                                take(HALVES * j + (NH + h0), j + (8 * i + 2 * g + 1))
                            for u in range(4):
                                if h == AT_HALF[u, 0] + 2 + NH:
                                    silu(u)
                                if h == AT_HALF[u, 0] + 2 + NH and u:
                                    turn(u - 1)
                            split(h)
                        turn(3)
                take(NH + PASS_HALVES * (i + 1), 8 * i + 9)

            def experts(l):
                for i in range(6):
                    k = tile_of[f"ht{l}"] + i
                    n = TT[i // 2][1]
                    full(act, k)
                    result("act", (f"ht{l}", i), copy(htok[0:n, i // 2, 512 * (i % 2):512 * (i % 2) + 512], B(k)[0:n, :]))
                after(act, "dve", f"rm{l}")
                result("act", f"re{l}", act.activation(rt[:, 60:72], rt[:, 48:60], ACT.Exp))
                after(act, "dve", f"rt2{l}")
                result("act", f"re2{l}", act.activation(rt[:, 303:306], rt[:, 300:303], ACT.Exp))
                expert_pass(moe, l, l)
                after(act, "dve", f"flag{l}")
                v = act.value_load(flag[:, :], min_val=0, max_val=1)
                with act.If(v >= 1):
                    for i in range(2):
                        expert_pass(more[l], l, i)

            for what, *i in steps_of("head", "act"):
                if what == "cond":
                    after(act, "dve", ("cols", 0))
                    result("act", ("cond",), act.activation(condT[:, :, :], cols[:, :, 17:26], ACT.Silu))
                elif what == "stats":
                    norm_stats("01")
                else:
                    ada_row(*i)
            for l in range(2):
                if l:
                    norm_stats("11")
                norm_apply(f"{l}1")
                (mixer0 if l == 0 else mixer1)()
                norm_stats(f"{l}2")
                norm_apply(f"{l}2")
                experts(l)
            norm_stats("f")
            norm_apply("f")
            for i in range(6):
                k = tile_of["y"] + i
                n = TT[i // 2][1]
                full(act, k)
                result("act", ("yt", i), copy(ytok[0:n, i // 2, 512 * (i % 2):512 * (i % 2) + 512], B(k)[0:n, :]))

        @block.vector
        def _(dve):
            steps = [0]

            def link(ins):
                steps[0] += 1
                ins.then_inc(vstep, 1)
                dve.wait_ge(vstep, steps[0])

            def mul(out, a, b):
                return dve.tensor_tensor(out, a, b, ALU.mult)

            def add(out, a, b):
                return dve.tensor_tensor(out, a, b, ALU.add)

            def stt(out, a, s, b, op0, op1, **kw):
                return dve.scalar_tensor_tensor(out, a, s, b, op0, op1, **kw)

            def b3(ap, n):
                return ap.unsqueeze(len(ap.shape)).to_broadcast(list(ap.shape) + [n])

            def mid(ap, n):
                s = list(ap.shape)
                return ap.unsqueeze(2).to_broadcast([s[0], s[1], n, s[2]])

            def norm_stats(tag):
                after(dve, "act", f"std{tag}")
                link(dve.reciprocal(rstd[:, :], rstd[:, :]))
                for res, c in (("xa", 0), ("xn", C // 2)):
                    half = slice(c, c + C // 2)
                    result("dve", f"{res}{tag}", mul(scratch[:, half, :], xT[:, half, :],
                                                     rstd[:, :].unsqueeze(1).to_broadcast([P, C // 2, T])))

            def norm_gain(tag):
                l = int(tag[0])
                j, g = (0, l) if tag[1] == "1" else (3, 2 + l)
                return stt(gainA[:, :, :], mod[:, l, j + 1, :, :], 1.0, cols[:, :, g:g + 1].to_broadcast([P, C, NCOND]),
                           ALU.add, ALU.mult)

            def norm_apply(tag):
                l = int(tag[0])
                j = 0 if tag[1] == "1" else 3
                after(dve, "dve", f"xn{tag}")
                for c in range(C):
                    ins = mul(samples(hT[:, c, NP_:T]), samples(scratch[:, c, NP_:T]), b3(gainA[:, c, 1:NCOND], LS))
                link(ins)
                for c in range(C):
                    ins = add(samples(hT[:, c, NP_:T]), samples(hT[:, c, NP_:T]), b3(mod[:, l, j, c, 1:NCOND], LS))
                result("dve", f"hs{tag}", ins)
                if tag[1] == "1":
                    for c in range(C):
                        after(dve, "act", ("hh", l, c))
                        result("dve", ("hl", l, c), dve.tensor_tensor(hTl[:, c, :], hT[:, c, :],
                                                                      hTh[:, c, :].bitcast(F32), ALU.subtract))

            def residual(l, m, ps, gate):
                stt(xT[:, m, 0:NP_], ps[:, 0:NP_], mod[:, l, gate, m, 0:1], xT[:, m, 0:NP_], ALU.mult, ALU.add)
                tmp = rstd[:, NS * (m % 4):NS * (m % 4) + NS]
                return tmp, mul(samples(tmp), samples(ps[:, NP_:T]), b3(mod[:, l, gate, m, 1:NCOND], LS))

            def split_half(l, n):
                unit = unit_of[("in", "qkv")[l]] + n // 2
                after(dve, "act", ("hi", l, n))
                result("dve", ("lo", l, n), dve.tensor_tensor(
                    wl[:, n % NH, :], ring[:, unit % R, U // 2 * (n % 2):U // 2 * (n % 2) + U // 2],
                    wh[:, n % NH, :].bitcast(F32), ALU.subtract))

            def mod_step(l, u):
                k = tile_of["turn", l, u]
                full(dve, k)
                j, c0 = u // 4, 2 * (u % 4)
                bias = cols[:, c0:c0 + 2, 5 + 6 * l + j:6 + 6 * l + j].to_broadcast([P, 2, NCOND])
                result("dve", ("mod", l, u), add(mod[:, l, j, c0:c0 + 2, :],
                                                 B(k)[:, 0:2 * NCOND].rearrange("p (c n) -> p c n", c=2), bias))

            def mixer0():
                bxs = bx[:, :, EP:EW].rearrange("p m (b e) -> p m b e", b=NB)

                def system(k, n):
                    return B(k)[0:n, 0:H * n].rearrange("p (h i) -> p h i", h=H)

                def level(s, n):
                    return K(f"lev{s}", n)[:, 0:n].unsqueeze(1).to_broadcast([n, H, n])

                def heads(ap):
                    return ap.rearrange("p (h v) -> p h v", h=H)

                for what, *i in steps_of("mixer0", "dve"):
                    step = (what, *i)
                    t = i[-1] if i else 0
                    a, n = TT[t] if t < 3 else TT[0]
                    if what == "mod":
                        mod_step(*i)
                    elif what == "lo":
                        split_half(*i)
                    elif what == "gab":
                        k = tile_of["ab",]
                        dve.memset(gcols[:, :, :], 0.0)
                        link(dve.memset(gab[:, :, :], 0.0))
                        dve.wait_ge(ld_small, 16 * NSMALL)
                        full(dve, k)
                        dve.tensor_copy(gab[:, 0:2, :], B(k)[:, 0:16].rearrange("p (t n) -> p t n", t=2))
                        result("dve", step, dve.tensor_copy(gab[0:NS, 2, :], B(k)[0:NS, 16:24]))
                    elif what == "gabs":
                        after(dve, "dve", ("gab",))
                        link(add(sc8[:, :, 12:16], gab[:, :, 0:4], dtb[:, 0:1, :].to_broadcast([P, 3, 4])))
                        link(dve.tensor_scalar(sc8[:, :, 8:12], sc8[:, :, 12:16], -1.0, None, ALU.mult))
                        result("dve", step, dve.tensor_tensor(sc8[:, :, 0:4], sc8[:, :, 12:16], sc8[:, :, 8:12], ALU.max))
                    elif what == "gmax":
                        result("dve", step, dve.tensor_scalar(gg[:, :, :], sc8[:, :, 12:16], 0.0, None, ALU.max))
                    elif what == "g":
                        after(dve, "act", ("geb",))
                        link(add(gg[:, :, :], gg[:, :, :], sc8[:, :, 4:8]))
                        link(dve.tensor_scalar(sc8[:, :, 8:12], sc8[:, :, 8:12], 1.0, None, ALU.add))
                        dve.reciprocal(beta[:, :, :], sc8[:, :, 8:12])
                        result("dve", step, stt(gg[:, :, :], gg[:, :, :], -1.0, dtb[:, 1:2, :].to_broadcast([P, 3, 4]),
                                                ALU.mult, ALU.mult))
                    elif what == "conv":
                        m, = i
                        if m == 0:
                            after(dve, "pool", "hist")
                        after(dve, "act", ("ext", m))
                        if m >= 2:
                            after(dve, "act", ("cv", m - 2))
                        o = convacc[:, m % 2, :]
                        link(dve.tensor_scalar(o[:, 0:CW], ext[:, m, 0:CW], colsA[:, m, 24:25], None, ALU.mult))
                        for j in range(1, 4):
                            ins = stt(o[:, 0:CW], ext[:, m, j:j + CW], colsA[:, m, 24 + j:25 + j], o[:, 0:CW],
                                      ALU.mult, ALU.add)
                            if j < 3:
                                link(ins)
                        result("dve", step, ins)
                    elif what == "bx":
                        m, = i
                        k = tile_of["in", 24 + m]
                        after(dve, "act", ("gt", 20 + m))
                        full(dve, k)
                        mul(bx[:, m, HIST:EP], B(k)[:, 0:NP_], cg[:, m, 0:NP_])
                        result("dve", step, mul(bxs[:, m, :, HIST:], samples(B(k)[:, NP_:T]), samples(cg[:, m, NP_:T])))
                    elif what == "catb":
                        m, = i
                        after(dve, "dve", ("bx", 3) if m == 0 else ("catb", m - 1))
                        o = bconv[:, m % 2, :]
                        link(dve.tensor_scalar(o[:, 0:CW], bx[:, m, 1:1 + CW], colsB[:, m, 16:17], None, ALU.mult))
                        for j in range(1, 3):
                            link(stt(o[:, 0:CW], bx[:, m, 1 + j:1 + j + CW], colsB[:, m, 16 + j:17 + j], o[:, 0:CW],
                                     ALU.mult, ALU.add))
                        mul(catT[:, 4 + m, 0:NP_], o[:, 0:NP_], bg[:, m, 0:NP_])
                        result("dve", step, mul(samples(catT[:, 4 + m, NP_:T]), sequences(o), samples(bg[:, m, NP_:T])))
                    elif what in ("l2r", "onr"):
                        col, src = (l2col, "l2s") if what == "l2r" else (oncol, "ons")
                        after(dve, "act", (src,))
                        dve.reciprocal(col[:, 0:2, :], col[:, 0:2, :])
                        result("dve", step, dve.reciprocal(col[0:NS, 2, :], col[0:NS, 2, :]))
                    elif what == "qn":
                        m, = i
                        k = tile_of["l2bc", m]
                        full(dve, k)
                        ps = B(k)[:, 0:T]
                        result("dve", step, stt(cT[:, m, :], cT[:, m, :], float(P) ** -0.5, ps, ALU.mult, ALU.mult)
                               if m < 4 else mul(cT[:, m, :], cT[:, m, :], ps))
                    elif what == "gcol":
                        k = tile_of["gcol",]
                        full(dve, k)
                        dve.tensor_copy(gcols[:, 0:2, :], B(k)[:, 0:16].rearrange("p (t n) -> p t n", t=2))
                        result("dve", step, dve.tensor_copy(gcols[0:NS, 2, :], B(k)[0:NS, 16:24]))
                    elif what == "gd":
                        k = tile_of["grow", t]
                        after(dve, "dve", ("gcol",))
                        full(dve, k)
                        after(dve, "act", ("eG", t))
                        for h in range(H):
                            ins = dve.tensor_scalar(gam[0:n, t, h, 0:n], B(k)[0:n, n * h:n * h + n],
                                                    gcols[0:n, t, h:h + 1], 0.0, ALU.subtract, ALU.min)
                        result("dve", step, ins)
                    elif what == "gam":
                        after(dve, "act", ("ge",))
                        for t, (a, n) in enumerate(TT):
                            m_ = K("upto") if t < 2 else K("upto_s", NS)
                            ins = mul(gam[0:n, t, :, 0:n], gam[0:n, t, :, 0:n], m_.unsqueeze(1).to_broadcast([n, H, n]))
                        result("dve", step, ins)
                    elif what == "kb":
                        k = tile_of["brow", t]
                        full(dve, k)
                        after(dve, "dve", ("qn", 7))
                        result("dve", step, mul(kb[:, :, a:a + n], cT[:, 4:8, a:a + n],
                                                B(k)[:, 0:H * n].rearrange("p (h i) -> p h i", h=H)))
                    elif what == "vb":
                        k = tile_of["vt", t]
                        full(dve, k)
                        result("dve", step, mul(vb[0:n, t, :, :], heads(B(k)[0:n, :]), b3(beta[0:n, t, :], P)))
                    elif what == "nbe":
                        after(dve, "act", ("egc",))
                        result("dve", step, stt(nbe[:, :, :], egc[:, :, 0:4], -1.0, beta[:, :, :], ALU.mult, ALU.mult))
                    elif what == "kd":
                        k = tile_of["kt", t]
                        full(dve, k)
                        result("dve", step, mul(kd[0:n, t, :, :], heads(B(k)[0:n, :]), b3(egc[0:n, t, 4:8], P)))
                    elif what == "at":
                        k = tile_of["at", t]
                        after(dve, "dve", ("gam",))
                        full(dve, k)
                        result("dve", step, mul(AT[0:n, t, :, 0:n], system(k, n), gam[0:n, t, :, 0:n]))
                    elif what == "xt1":
                        after(dve, "dve", ("at", t))
                        link(mul(XT[0:n, t, :, 0:n], AT[0:n, t, :, 0:n], level(1, n)))
                        result("dve", step, dve.tensor_tensor(
                            XT[0:n, t, :, 0:n], K("ident", n)[:, 0:n].unsqueeze(1).to_broadcast([n, H, n]),
                            XT[0:n, t, :, 0:n], ALU.subtract))
                    elif what == "qkg":
                        k = tile_of["qk", t]
                        full(dve, k)
                        result("dve", step, mul(qkg[0:n, t, :, 0:n], system(k, n), gam[0:n, t, :, 0:n]))
                    elif what == "qd":
                        result("dve", step, mul(qd, cT[:, 0:4, :], eG))
                    elif what == "lt":
                        result("dve", step, mul(LT[0:n, t, :, 0:n], AT[0:n, t, :, 0:n], level(i[0], n)))
                    elif what == "xt":
                        k = tile_of["XPt", i[0], t]
                        full(dve, k)
                        full(dve, k + 1)
                        result("dve", step, dve.tensor_tensor(XT[0:n, t, :, 0:n], XT[0:n, t, :, 0:n],
                                                              system(k, n), ALU.subtract))
                    elif what == "xi":
                        k = tile_of["XP", i[0], t]
                        if i[0] == 2:
                            after(dve, "act", ("x0", t))
                        result("dve", step, dve.tensor_tensor(X[0:n, t, :, 0:n], X[0:n, t, :, 0:n],
                                                              system(k, n), ALU.subtract))
                        after(dve, "dve", step)
                    elif what == "ktm":
                        link(dve.memset(kTm, 0.0))
                        for h in range(H):
                            own = arena[:, AT_AT + NB * NS * h:AT_AT + NB * NS * h + NB * (NS + LS)]
                            ins = dve.tensor_copy(own.rearrange("p (b w) -> p b w", b=NB)[:, :, 0:LS],
                                                  samples(cT[:, 4 + h, NP_:T]))
                        result("dve", step, ins)
                    elif what == "r":
                        k = tile_of["kS", t]
                        full(dve, k)
                        after(dve, "dve", ("vb", t))
                        for h in range(H):
                            ins = stt(RR[0:n, t, h, :], B(k)[0:n, P * h:P * h + P], nbe[0:n, t, h:h + 1],
                                      vb[0:n, t, h, :], ALU.mult, ALU.add)
                        result("dve", step, ins)
                    elif what == "o":
                        k = tile_of["o", t]
                        full(dve, k)
                        result("dve", step, dve.tensor_copy(oT[:, :, a:a + n],
                                                            B(k)[:, 0:H * n].rearrange("p (h i) -> p h i", h=H)))
                    elif what == "s" and t == 0:
                        k = tile_of["s", 0]
                        full(dve, k)
                        result("dve", step, dve.tensor_copy(S0, heads(B(k)[:, :])))
                    elif what == "s":
                        k = tile_of["s", 1]
                        full(dve, k)
                        after(dve, "dve", ("s", 0))
                        for h in range(H):
                            ins = stt(S0[:, h, :], S0[:, h, :], eG[:, h, 255:256], B(k)[:, P * h:P * h + P],
                                      ALU.mult, ALU.add)
                        result("dve", step, ins)
                    elif what == "ue":
                        h, = i
                        after(dve, "act", ("u", 2))
                        full(dve, tile_of["o", 2])
                        if h:
                            full(dve, tile_of["ds", h - 1, 1])
                        mul(ue, uu[0:NS, 2, h, :].unsqueeze(1).to_broadcast([NS, NB, P]), b3(K("batch_rows", NS), P))
                        dec = eG[:, h, NP_ + LS - 1:T:LS]
                        result("dve", step, mul(states[:, :, h, :], states[:, :, h, :], b3(dec, P)))
                    elif what == "ds":
                        h, j = i
                        k = tile_of["ds", h, j]
                        after(dve, "dve", ("ue", h))
                        full(dve, k)
                        st = states[:, 4 * j:4 * j + 4, h, :]
                        result("dve", step, add(st, st, B(k)[:, :].rearrange("p (b v) -> p b v", b=4)))
                    elif what == "on":
                        h, = i
                        k = tile_of["onbc", h]
                        full(dve, k)
                        result("dve", step, mul(oT[:, h, :], oT[:, h, :], B(k)[:, 0:T]))
                    elif what == "cat":
                        after(dve, "dve", ("on", H - 1))
                        result("dve", step, stt(catT[:, 0:4, :], oT, colsO[:, 0:1], zT, ALU.mult, ALU.mult))

            def mixer1():
                for n in range(24):
                    split_half(1, n)
                for i in range(6):
                    k = tile_of["vtok"] + i
                    n = TT[i // 2][1]
                    full(dve, k)
                    result("dve", ("vt", i), dve.tensor_copy(vtok[0:n, i // 2, 512 * (i % 2):512 * (i % 2) + 512], B(k)[0:n, :]))
                dve.wait_ge(ld_amask, 16)
                for what, *i in steps_of("mixer1", "dve"):
                    step = (what, *i)
                    n = i[0]
                    u = n % 2
                    if what == "mod":
                        mod_step(*i)
                    if what == "amax":
                        k = tile_of["S", n]
                        full(dve, k)
                        link(add(scr[:, u, :], B(k)[:, 0:384], KA("neg_prompt")))
                        dve.tensor_reduce(stat[:, u, 0:1], scr[:, u, 0:128], AX.X, ALU.max)
                        link(dve.tensor_reduce(stat[:, u, 1:2], scr[:, u, 128:384], AX.X, ALU.max))
                        result("dve", step, dve.tensor_scalar(stat[:, u, 2:4], stat[:, u, 0:2], -0.125, None, ALU.mult))
                    elif what == "apr":
                        after(dve, "act", ("aexp", n))
                        for r, (x, y) in enumerate(((0, 128), (128, 384))):
                            ins = stt(prb[:, u, x:y], prb[:, u, x:y], 1.0, KA("cnt_prompt")[:, x:y], ALU.mult, ALU.mult,
                                      accum_out=stat[:, u, 4 + r:5 + r])
                        link(ins)
                        link(dve.reciprocal(stat[:, u, 4:6], stat[:, u, 4:6]))
                        dve.tensor_scalar(prb[:, u, 0:128], prb[:, u, 0:128], stat[:, u, 4:5], None, ALU.mult)
                        result("dve", step, dve.tensor_scalar(prb[:, u, 128:384], prb[:, u, 128:384],
                                                              stat[:, u, 5:6], None, ALU.mult))
                    elif what == "kt":
                        k = tile_of["K", n, i[1]]
                        full(dve, k)
                        if n:
                            full(dve, tile_of["Ss", n - 1])
                        result("dve", step, dve.tensor_copy(KT[:, 2 * i[1]:2 * i[1] + 2, :],
                                                            B(k)[:, :].rearrange("p (c j) -> p c j", c=2)))
                    elif what == "smax":
                        k = tile_of["Ss", n]
                        full(dve, k)
                        add(scrS[:, u, 0:256], B(k)[:, 0:256], KA("neg_cache"))
                        link(add(scrS[:, u, 256:320], B(k)[:, 256:320], KA("neg_new")[:, 56 - LS * n:120 - LS * n]))
                        link(dve.tensor_reduce(statS[:, u, 0:1], scrS[:, u, 0:T], AX.X, ALU.max))
                        result("dve", step, dve.tensor_scalar(statS[:, u, 2:3], statS[:, u, 0:1], -0.125, None, ALU.mult))
                    elif what == "spr":
                        after(dve, "act", ("sexp", n))
                        stt(prbS[:, u, 0:256], prbS[:, u, 0:256], 1.0, KA("cnt_cache"), ALU.mult, ALU.mult,
                            accum_out=statS[:, u, 4:5])
                        link(stt(prbS[:, u, 256:320], prbS[:, u, 256:320], 1.0,
                                 KA("cnt_new")[:, 56 - LS * n:120 - LS * n], ALU.mult, ALU.mult,
                                 accum_out=statS[:, u, 5:6]))
                        link(add(statS[:, u, 6:7], statS[:, u, 4:5], statS[:, u, 5:6]))
                        link(dve.reciprocal(statS[:, u, 6:7], statS[:, u, 6:7]))
                        result("dve", step, dve.tensor_scalar(prbS[:, u, 0:T], prbS[:, u, 0:T], statS[:, u, 6:7],
                                                              None, ALU.mult))
                    elif what == "sout":
                        k = tile_of["Os", n]
                        full(dve, k)
                        a = NP_ + LS * n
                        for e in range(2):
                            r = slice(64 * e, 64 * e + 64)
                            ins = dve.tensor_copy(attnT[r, :, a:a + LS],
                                                  B(k)[r, 0:128].rearrange("p (c q) -> p c q", c=C)[:, :, LS * e:LS * e + LS])
                        result("dve", step, ins)

            def router(l):
                k = tile_of[f"rt{l}"]
                lg = small[:, :, 0:36]
                full(dve, k)
                dve.tensor_copy(small[:, 0:2, 0:36], B(k)[:, 0:72].rearrange("p (t n) -> p t n", t=2))
                result("dve", f"rt{l}", dve.tensor_copy(small[0:NS, 2, 0:36], B(k)[0:NS, 72:108]))
                after(dve, "dve", f"rt{l}")
                if l == 1:
                    dve.wait_ge(ld_router1, 64)
                link(add(lg, lg, br[l][:, :].unsqueeze(1).to_broadcast([P, 3, 36])))
                lg4 = small[:, :, 0:4]

                def v3(a, n):
                    return rt[:, a:a + 3 * n].rearrange("p (t n) -> p t n", t=3)

                iota = K("iota8")

                def first_of(out, vals, top, tmp, topv, n):
                    link(dve.tensor_reduce(top, vals, AX.X, ALU.max))
                    link(dve.tensor_tensor(tmp, vals, b3(top, n), ALU.is_equal))
                    link(mul(tmp, tmp, iota[:, 0:n].unsqueeze(1).to_broadcast([P, 3, n])))
                    link(dve.tensor_reduce(topv, tmp, AX.X, ALU.max))
                    return dve.tensor_tensor(out, tmp, b3(topv, n), ALU.is_equal)

                gmax, tmp4, topv = rt[:, 0:3], v3(3, 4), rt[:, 15:18]
                oh_ins = first_of(onehot[:, :, :], lg4, gmax, tmp4, topv, 4)
                link(oh_ins)
                result("dve", f"rm{l}", dve.tensor_tensor(v3(48, 4), lg4, b3(gmax, 4), ALU.subtract))
                prod = rt[:, 100:196].rearrange("p (t g e) -> p t g e", t=3, g=NG)
                for t in range(3):
                    ins = mul(prod[:, t], small[:, t, 4:36].rearrange("p (g e) -> p g e", g=NG), b3(onehot[:, t, :], NE))
                result("dve", f"oh{l}", ins)
                after(dve, "dve", f"oh{l}")
                el, tmp8, oh1, oh2 = v3(200, 8), v3(224, 8), v3(248, 8), v3(272, 8)
                link(dve.tensor_reduce(el, prod.rearrange("p t g e -> p t e g"), AX.X, ALU.add))
                m1, m2 = rt[:, 296:299], rt[:, 309:312]
                link(first_of(oh1, el, m1, tmp8, topv, 8))
                link(stt(el, oh1, NEG, el, ALU.mult, ALU.add))
                link(first_of(oh2, el, m2, tmp8, topv, 8))
                result("dve", f"rt2{l}", dve.tensor_tensor(rt[:, 300:303], m2, m1, ALU.subtract))
                after(dve, "act", f"re2{l}")
                psum_, r_, w1, w2 = rt[:, 18:21], rt[:, 303:306], rt[:, 24:27], rt[:, 27:30]
                link(dve.tensor_reduce(psum_, v3(60, 4), AX.X, ALU.add))
                link(dve.tensor_scalar(w1, r_, 1.0, None, ALU.add))
                link(mul(w1, w1, psum_))
                link(dve.reciprocal(w1, w1))
                link(mul(w2, w1, r_))
                link(mul(oh1, oh1, b3(w1, 8)))
                link(mul(oh2, oh2, b3(w2, 8)))
                link(add(oh1, oh1, oh2))
                for t in range(3):
                    mul(gates[:, t, :].rearrange("p (g e) -> p g e", g=NG),
                        oh1[:, t, :].unsqueeze(1).to_broadcast([P, NG, NE]), b3(onehot[:, t, :], NE))
                k = tile_of[f"rk{l}"]
                link(dve.memset(rank[:, :, :], -2000.0))
                full(dve, k)
                dve.tensor_scalar(rank[:, 0:2, :], B(k)[:, 0:8].rearrange("p (t n) -> p t n", t=2), 1000.0, None, ALU.add)
                link(dve.tensor_scalar(rank[0:NS, 2, :], B(k)[0:NS, 8:12], 1000.0, None, ALU.add))
                link(mul(rank[:, :, :], rank[:, :, :], onehot[:, :, :]))
                dve.tensor_scalar(rank[:, :, :], rank[:, :, :], -1001.0, None, ALU.add)
                link(dve.tensor_reduce(rt[0:1, 30:31], B(k)[0:1, 16:20], AX.X, ALU.max))
                result("dve", f"flag{l}", dve.tensor_scalar(flag[:, :], rt[0:1, 30:31], SLOTS + 0.5, None, ALU.is_gt))

            def expert_pass(l, S, i, first, link):
                if not first:
                    link(dve.tensor_scalar(rank[:, :, :], rank[:, :, :], -float(SLOTS), None, ALU.add))
                for t in range(3):
                    ins = dve.tensor_tensor(perm[:, t, :, :], K("iota").unsqueeze(1).to_broadcast([P, NG, SLOTS]),
                                            b3(rank[:, t, :], SLOTS), ALU.is_equal)
                ins.then_inc(S["perm"], 1)
                for c in range(C):
                    dve.wait_ge(S["hghi"], 8 * i + c + 1)
                    dve.tensor_tensor(hgl[:, c, :], bank[5 + c % 2][:, :], hgh[:, c, :].bitcast(F32), ALU.subtract)\
                        .then_inc(S["hglo"], 1)
                dve.wait_ge(S["gsl"], i + 1)
                ins = dve.tensor_copy(gslot[:, :], bank[7][:, 0:NG * NE])
                if i == 0:
                    ins.then_inc(S["hid"], 2)
                    dve.wait_ge(S["hid"], 2)
                else:
                    link(ins)
                for g in range(NG):
                    with dve.Fori(0, 2) as j:
                        k0 = 32 * i + 8 * g
                        h0 = PASS_HALVES * i + HALVES * 2 * g

                        def split(h):
                            unit = expert_unit(S, l, i, h // 2)[0]
                            dve.wait_ge(S["hi"], HALVES * j + (h0 + h + 1))
                            dve.tensor_tensor(wl[:, h % NH, :], unit[:, U // 2 * (h % 2):U // 2 * (h % 2) + U // 2],
                                              wh[:, h % NH, :].bitcast(F32), ALU.subtract).then_inc(S["lo"], 1)

                        def gated(u):
                            dve.wait_ge(S["silu"], 4 * j + (k0 + u + 1))
                            dve.wait_ge(S["used"], HALVES * j + (NH + h0 + AT_HALF[u, 1] + 2))
                            gate = gslot[:, bass.ds(4 * j + (8 * g + u), 1)]
                            stt(hid[:, u % 2, :], sg[:, u % 2, :], gate, bank[5 + u % 2][:, 0:256], ALU.mult, ALU.mult)\
                                .then_inc(S["hid"], 1)

                        def turn(u):
                            dve.wait_ge(S["hidhi"], 4 * j + (k0 + u + 1))
                            dve.tensor_tensor(hidTl[:, u % 2, :, :].rearrange("p f s -> p (f s)"),
                                              bank[2][:, 256 * (u % 2):256 * (u % 2) + 256],
                                              hidTh[:, u % 2, :, :].rearrange("p f s -> p (f s)").bitcast(F32),
                                              ALU.subtract).then_inc(S["hidlo"], 1)

                        for h in range(HALVES):
                            for u in range(4):
                                if h == AT_HALF[u, 0] + 2 + NH and u:
                                    turn(u - 1)
                                if h == AT_HALF[u, 1] + 2 + NH:
                                    gated(u)
                            split(h)
                        turn(3)
                for m in range(C):
                    dve.wait_ge(S["sc"], 8 * i + m + 1)
                    ps = bank[5 + m % 2]
                    tmp, ins = residual(l, m, ps, 5)
                    ins.then_inc(S["scfree"], 1)
                    dve.wait_ge(S["scfree"], 8 * i + m + 1)
                    ins = add(xT[:, m, NP_:T], xT[:, m, NP_:T], tmp)
                link(ins)

            def experts(l):
                expert_pass(l, moe, l, True, link)
                S = more[l]
                v = dve.value_load(flag[:, :], min_val=0, max_val=1)
                with dve.If(v >= 1):
                    more_steps = [0]

                    def link2(ins):
                        more_steps[0] += 1
                        ins.then_inc(S["step"], 1)
                        dve.wait_ge(S["step"], more_steps[0])

                    for i in range(2):
                        expert_pass(l, S, i, False, link2)
                result("dve", f"x{l}2", dve.tensor_copy(stat[:, 0, 0:1], xT[:, C - 1, T - 1:T]))

            dve.memset(small[:, :, :], 0.0)
            for what, *i in steps_of("head", "dve"):
                step = (what, *i)
                if what == "mod":
                    mod_step(*i)
                    continue
                if what == "stats":
                    norm_stats("01")
                    continue
                k = tile_of[step]
                full(dve, k)
                if what == "cols":
                    dst, n = ((cols, C), (colsA, 12), (colsB, 4))[i[0]]
                    w = dst.shape[2]
                    result("dve", step, dve.tensor_copy(dst[:, :, :], B(k)[:, 0:w * n].rearrange("p (c n) -> p c n", c=n)))
                else:
                    result("dve", step, dve.tensor_copy(xT[:, i[0], :], B(k)[:, 0:T]))
            for l in range(2):
                if l == 0:
                    after(dve, "dve", ("mod", 0, HEAD_UNITS - 1))
                    result("dve", "gain01", norm_gain("01"))
                    after(dve, "dve", "gain01")
                else:
                    norm_gain("11")
                    norm_stats("11")
                norm_apply(f"{l}1")
                (mixer0 if l == 0 else mixer1)()
                for m in range(C):
                    k = tile_of[f"out{l}"] + m
                    full(dve, k)
                    tmp, ins = residual(l, m, B(k), 2)
                    link(ins)
                    result("dve", (f"xo{l}", m), add(xT[:, m, NP_:T], xT[:, m, NP_:T], tmp))
                after(dve, "dve", (f"xo{l}", C - 1))
                after(dve, "pool", f"mixer{l}")
                norm_gain(f"{l}2")
                norm_stats(f"{l}2")
                norm_apply(f"{l}2")
                router(l)
                experts(l)
                after(dve, "dve", f"x{l}2")
            norm_stats("f")

        assert made == {"dve": len(DVE_ORDER), "act": len(ACT_ORDER), "pool": len(POOL_ORDER)}, made


_INS = ["x_prompt", "x_sample", "state_a_ssm", "state_a_conv", "state_b_conv", "cache_c_k", "cache_c_v",
        "c_prompt", "c_sample", "w_ada", "b_ada", "norm1", "norm2", "norm_f", "w_in_even", "conv_a_w", "a_log",
        "dt_bias", "o_gain_a", "conv_b_w", "w_out_even", "w_qkv_odd", "w_out_odd", "w_router_group",
        "b_router_group", "w_router_expert", "b_router_expert", "w_exp_gate", "w_exp_up", "w_exp_down"]
_OUTS = {"y_p": (1, 256, 1024), "y_s": (8, 8, 1024), "ssm_p": (1, 1, 4, 128, 128), "ssm_s": (1, 8, 4, 128, 128),
         "aconv_p": (1, 1, 3, 1536), "aconv_s": (1, 8, 3, 1536), "bconv_p": (1, 1, 2, 512), "bconv_s": (1, 8, 2, 512),
         "ck_p": (1, 1, 256, 16, 64), "ck_s": (1, 8, 8, 16, 64), "cv_p": (1, 1, 256, 16, 64), "cv_s": (1, 8, 8, 16, 64)}


def kernel(**inputs):
    import numpy as _np
    import concourse.bacc as _bacc
    from concourse import mybir as _mybir
    from concourse.bass_utils import run_bass_kernel_spmd as _run

    nc = _bacc.Bacc("TRN2", target_bir_lowering=False, num_devices=1)
    given = {name: _np.ascontiguousarray(inputs[name]) for name in _INS}
    given["masks"] = packed(constants())
    given["amasks"] = packed(attention_constants())
    arrays = {f"in_{name}_dram": a for name, a in given.items()}
    ins = {name: nc.dram_tensor(f"in_{name}_dram", a.shape, _mybir.dt.from_np(a.dtype), kind="ExternalInput").ap()
           for name, a in given.items()}
    outs = {name: nc.dram_tensor(f"out_{name}_dram", shape, _mybir.dt.float32, kind="ExternalOutput").ap()
            for name, shape in _OUTS.items()}
    trunk_program(nc, ins, outs)
    r = _run(nc, [arrays], core_ids=[0])
    return tuple(r.results[0][f"out_{name}_dram"] for name in _OUTS)
```
